# Optimizing a Trainium2 kernel written in Bass

```python
import jax, jax.numpy as jnp
from jax import lax
import numpy as np

D_MODEL = 1024
BATCH = 1
SEQ = 256
DEPTH = 2

N_HEADS = 8
N_KV_HEADS = 2
HEAD_DIM = 64
ATTN_WIDTH = N_HEADS * HEAD_DIM
KV_WIDTH = N_KV_HEADS * HEAD_DIM
WINDOW = 128
BLOCK = 128
ROPE_DIM = HEAD_DIM // 4
ROPE_THETA = 500000.0
CONV_WIDTH = D_MODEL - ATTN_WIDTH
CONV_K = 3
MIX_WIDTH = ATTN_WIDTH + CONV_WIDTH
IN_WIDTH = ATTN_WIDTH + 2 * KV_WIDTH + 3 * CONV_WIDTH
SPLITS = (ATTN_WIDTH, ATTN_WIDTH + KV_WIDTH, ATTN_WIDTH + 2 * KV_WIDTH,
          ATTN_WIDTH + 2 * KV_WIDTH + CONV_WIDTH, ATTN_WIDTH + 2 * KV_WIDTH + 2 * CONV_WIDTH)
N_EXPERT_GROUPS = 4
EXPERTS_PER_GROUP = 8
N_EXPERTS = N_EXPERT_GROUPS * EXPERTS_PER_GROUP
TOP_K = 2
D_EXPERT = 512
MOE_BLOCK = 256
EPS = 1e-6
NEG_INF = -1e30


def rmsnorm(x, g):
    xf = x.astype(jnp.float32)
    y = xf * lax.rsqrt(jnp.mean(xf * xf, axis=-1, keepdims=True) + EPS)
    return (y * g.astype(jnp.float32)).astype(x.dtype)

def rope_tables(seq):
    pos = jnp.arange(seq, dtype=jnp.float32)
    inv_freq = ROPE_THETA ** (-jnp.arange(0, ROPE_DIM, 2, dtype=jnp.float32) / ROPE_DIM)
    ang = pos[:, None] * inv_freq[None, :]
    return jnp.cos(ang)[:, None, :], jnp.sin(ang)[:, None, :]

def partial_rope(x, cos, sin):
    half = ROPE_DIM // 2
    xf = x.astype(jnp.float32)
    x1, x2, rest = xf[..., :half], xf[..., half:ROPE_DIM], xf[..., ROPE_DIM:]
    out = jnp.concatenate([x1 * cos - x2 * sin, x2 * cos + x1 * sin, rest], axis=-1)
    return out.astype(x.dtype)

def windowed_gqa_with_sink(q, k, v, sink):
    b, s = q.shape[0], q.shape[1]
    nb = s // BLOCK
    grp = N_HEADS // N_KV_HEADS
    qb = q.reshape(b, nb, BLOCK, N_KV_HEADS, grp, HEAD_DIM)

    def band(t):
        tp = jnp.pad(t, ((0, 0), (BLOCK, BLOCK), (0, 0), (0, 0)))
        tp = tp.reshape(b, nb + 2, BLOCK, N_KV_HEADS, HEAD_DIM)
        return jnp.concatenate([tp[:, :-2], tp[:, 1:-1], tp[:, 2:]], axis=2)

    kb, vb = band(k), band(v)
    scores = jnp.einsum('bnqhgd,bnkhd->bnhgqk', qb, kb,
                        preferred_element_type=jnp.float32) * (HEAD_DIM ** -0.5)
    qi = jnp.arange(BLOCK)[:, None]
    kj = jnp.arange(3 * BLOCK)[None, :]
    k_pos = (jnp.arange(nb)[:, None, None] - 1) * BLOCK + kj
    mask = (jnp.abs(kj - BLOCK - qi) <= WINDOW) & (k_pos >= 0) & (k_pos < s)
    scores = jnp.where(mask[None, :, None, None], scores, NEG_INF)
    sink_col = jnp.broadcast_to(
        sink.astype(jnp.float32).reshape(N_KV_HEADS, grp)[None, None, :, :, None, None],
        scores.shape[:-1] + (1,))
    probs = jax.nn.softmax(jnp.concatenate([scores, sink_col], axis=-1), axis=-1)[..., :-1]
    out = jnp.einsum('bnhgqk,bnkhd->bnqhgd', probs.astype(v.dtype), vb)
    return out.reshape(b, s, ATTN_WIDTH)

def centred_short_conv(u, w):
    up = jnp.pad(u, ((0, 0), (1, 1), (0, 0)))
    return up[:, :-2] * w[0] + up[:, 1:-1] * w[1] + up[:, 2:] * w[2]

def hybrid_mixer(h, w_in, sink, conv_w, g_attn, g_conv, w_out, cos, sin):
    b, s, _ = h.shape
    proj = h @ w_in
    q, k, v, gate_b, gate_c, u = jnp.split(proj, SPLITS, axis=-1)
    q = partial_rope(q.reshape(b, s, N_HEADS, HEAD_DIM), cos, sin)
    k = partial_rope(k.reshape(b, s, N_KV_HEADS, HEAD_DIM), cos, sin)
    v = v.reshape(b, s, N_KV_HEADS, HEAD_DIM)
    y_attn = windowed_gqa_with_sink(q, k, v, sink)
    y_conv = gate_b * centred_short_conv(gate_c * u, conv_w)
    y = jnp.concatenate([rmsnorm(y_attn, g_attn), rmsnorm(y_conv, g_conv)], axis=-1)
    return y @ w_out

def hierarchical_moe(h, w_rg, b_rg, w_re, b_re, w_gate, w_up, w_down):
    b, s, d = h.shape
    t = b * s
    xf = h.reshape(t, d)
    group_logits = (xf @ w_rg).astype(jnp.float32) + b_rg.astype(jnp.float32)
    group_prob = jax.nn.softmax(group_logits, axis=-1)
    grp = jnp.argmax(group_logits, axis=-1)
    p_grp = jnp.take_along_axis(group_prob, grp[:, None], axis=-1)
    expert_logits = ((xf @ w_re).astype(jnp.float32) + b_re.astype(jnp.float32)
                     ).reshape(t, N_EXPERT_GROUPS, EXPERTS_PER_GROUP)
    in_group = jnp.take_along_axis(expert_logits, grp[:, None, None], axis=1)[:, 0]
    top_logit, top_local = lax.top_k(in_group, TOP_K)
    gates = p_grp * jax.nn.softmax(top_logit, axis=-1)
    experts = grp[:, None] * EXPERTS_PER_GROUP + top_local

    a = t * TOP_K
    flat_e = experts.reshape(a)
    flat_tok = jnp.arange(a, dtype=jnp.int32) // TOP_K
    flat_g = gates.reshape(a)
    order = jnp.argsort(flat_e)
    e_sorted, tok_sorted, g_sorted = flat_e[order], flat_tok[order], flat_g[order]
    counts = jnp.bincount(flat_e, length=N_EXPERTS)
    starts = jnp.cumsum(counts) - counts
    padded = (counts + MOE_BLOCK - 1) // MOE_BLOCK * MOE_BLOCK
    padded_end = jnp.cumsum(padded)
    dest = (padded_end - padded)[e_sorted] + jnp.arange(a) - starts[e_sorted]
    n_blocks = -(-a // MOE_BLOCK) + N_EXPERTS
    cap = n_blocks * MOE_BLOCK
    slot_tok = jnp.zeros((cap,), jnp.int32).at[dest].set(tok_sorted)
    block_expert = jnp.minimum(
        jnp.searchsorted(padded_end, jnp.arange(n_blocks) * MOE_BLOCK, side='right'),
        N_EXPERTS - 1)
    x_slots = xf[slot_tok].reshape(n_blocks, MOE_BLOCK, d)

    def expert_block(args):
        xb, e = args
        return (jax.nn.silu(xb @ w_gate[e]) * (xb @ w_up[e])) @ w_down[e]

    y_slots = lax.map(expert_block, (x_slots, block_expert)).reshape(cap, d)
    y_assign = y_slots[dest] * g_sorted[:, None].astype(h.dtype)
    y = jax.ops.segment_sum(y_assign, tok_sorted, num_segments=t)
    return y.reshape(b, s, d)

def first_inputs(seed: int = 0) -> dict:
    key = jax.random.key(seed)
    ks = jax.random.split(key, 17)
    f32 = jnp.float32
    nrm = lambda k, shape, scale: jax.random.normal(k, shape, f32) * scale
    res_scale = (2.0 * DEPTH) ** -0.5
    return {
        "x": nrm(ks[0], (BATCH, SEQ, D_MODEL), 1.0),
        "norm_mix": 1.0 + nrm(ks[1], (DEPTH, D_MODEL), 0.02),
        "w_in": nrm(ks[2], (DEPTH, D_MODEL, IN_WIDTH), D_MODEL ** -0.5),
        "attn_sink": nrm(ks[3], (DEPTH, N_HEADS), 0.5),
        "conv_w": nrm(ks[4], (DEPTH, CONV_K, CONV_WIDTH), CONV_K ** -0.5),
        "norm_attn_out": 1.0 + nrm(ks[5], (DEPTH, ATTN_WIDTH), 0.02),
        "norm_conv_out": 1.0 + nrm(ks[6], (DEPTH, CONV_WIDTH), 0.02),
        "w_out": nrm(ks[7], (DEPTH, MIX_WIDTH, D_MODEL), MIX_WIDTH ** -0.5 * res_scale),
        "norm_ffn": 1.0 + nrm(ks[8], (DEPTH, D_MODEL), 0.02),
        "w_router_group": nrm(ks[9], (DEPTH, D_MODEL, N_EXPERT_GROUPS), D_MODEL ** -0.5),
        "b_router_group": nrm(ks[10], (DEPTH, N_EXPERT_GROUPS), 0.01),
        "w_router_expert": nrm(ks[11], (DEPTH, D_MODEL, N_EXPERTS), D_MODEL ** -0.5),
        "b_router_expert": nrm(ks[12], (DEPTH, N_EXPERTS), 0.01),
        "w_expert_gate": nrm(ks[13], (DEPTH, N_EXPERTS, D_MODEL, D_EXPERT), D_MODEL ** -0.5),
        "w_expert_up": nrm(ks[14], (DEPTH, N_EXPERTS, D_MODEL, D_EXPERT), D_MODEL ** -0.5),
        "w_expert_down": nrm(ks[15], (DEPTH, N_EXPERTS, D_EXPERT, D_MODEL), D_EXPERT ** -0.5 * res_scale),
        "norm_final": 1.0 + nrm(ks[16], (D_MODEL,), 0.02),
    }

def first_block(x, norm_mix, w_in, attn_sink, conv_w, norm_attn_out, norm_conv_out, w_out,
              norm_ffn, w_router_group, b_router_group, w_router_expert, b_router_expert,
              w_expert_gate, w_expert_up, w_expert_down, norm_final):
    cos, sin = rope_tables(x.shape[1])
    for l in range(DEPTH):
        x = x + hybrid_mixer(rmsnorm(x, norm_mix[l]), w_in[l], attn_sink[l], conv_w[l],
                             norm_attn_out[l], norm_conv_out[l], w_out[l], cos, sin)
        x = x + hierarchical_moe(rmsnorm(x, norm_ffn[l]), w_router_group[l], b_router_group[l],
                                 w_router_expert[l], b_router_expert[l], w_expert_gate[l],
                                 w_expert_up[l], w_expert_down[l])
    return rmsnorm(x, norm_final)


N_MIXERS = 2
D_FF = 2816
POOL_WINDOWS = (2, 4, 8, 16)
N_POOL_GROUPS = 4
POOL_GROUP = D_MODEL // N_POOL_GROUPS
N_HEADS_2 = 16
HEAD_DIM_2 = D_MODEL // N_HEADS_2
N_KV_GROUPS = 4
HEADS_PER_GROUP = N_HEADS_2 // N_KV_GROUPS
ROPE_DIM_2 = HEAD_DIM_2 // 4
CMP_BLOCK = 32
CMP_STRIDE = 16
CMP_HIDDEN = 256
SEL_BLOCK = 64
N_SELECT = 8
SEL_Q_BLOCK = 32
WINDOW_2 = 256
WIN_Q_BLOCK = 128
Q_WIDTH = N_HEADS_2 * HEAD_DIM_2
KV_WIDTH_2 = N_KV_GROUPS * HEAD_DIM_2
GATE_WIDTH = 3 * N_HEADS_2
IN_WIDTH_2 = Q_WIDTH + 6 * KV_WIDTH_2 + GATE_WIDTH
SPLIT_POINTS = tuple(Q_WIDTH + i * KV_WIDTH_2 for i in range(7))
N_POOL_LAYERS = (DEPTH + N_MIXERS - 1) // N_MIXERS
N_NSA_LAYERS = DEPTH // N_MIXERS
NEG_INF_2 = -1e30


def rms_norm(x, g):
    xf = x.astype(jnp.float32)
    y = xf * lax.rsqrt(jnp.mean(xf * xf, axis=-1, keepdims=True) + EPS)
    return (y * g.astype(jnp.float32)).astype(x.dtype)

def swiglu(x, w_gate, w_up, w_down):
    return (jax.nn.silu(x @ w_gate) * (x @ w_up)) @ w_down

def rope_tables_2(seq):
    inv = 1.0 / (ROPE_THETA ** (jnp.arange(0, ROPE_DIM_2, 2, dtype=jnp.float32) / ROPE_DIM_2))
    ang = jnp.arange(seq, dtype=jnp.float32)[:, None] * inv[None, :]
    return jnp.cos(ang), jnp.sin(ang)

def partial_rope_2(t, cos, sin):
    half = ROPE_DIM_2 // 2
    c = cos[None, :, None, :].astype(t.dtype)
    s = sin[None, :, None, :].astype(t.dtype)
    x1, x2, rest = t[..., :half], t[..., half:ROPE_DIM_2], t[..., ROPE_DIM_2:]
    return jnp.concatenate([x1 * c - x2 * s, x1 * s + x2 * c, rest], axis=-1)

def pool_mixer(h, w_grp, b_grp, scale):
    B, S, D = h.shape
    hf = h.astype(jnp.float32)
    cum = jnp.concatenate([jnp.zeros((B, 1, D), jnp.float32), jnp.cumsum(hf, axis=1)], axis=1)
    end = jnp.arange(1, S + 1)
    outs = []
    for g, w in enumerate(POOL_WINDOWS):
        sl = slice(g * POOL_GROUP, (g + 1) * POOL_GROUP)
        lo = jnp.maximum(end - w, 0)
        cnt = (end - lo).astype(jnp.float32)[None, :, None]
        mean = (cum[:, 1:, sl] - cum[:, lo, sl]) / cnt
        outs.append(mean - hf[:, :, sl])
    d = jnp.stack(outs, axis=2).astype(h.dtype)
    y = jnp.einsum('bsgc,gce->bsge', d, w_grp) + b_grp
    return y.reshape(B, S, D) * scale

def compress_blocks(blk, pos_emb, w1, w2):
    B, Nc = blk.shape[:2]
    z = (blk + pos_emb[None, None, :, None, :]).transpose(0, 1, 3, 2, 4)
    z = z.reshape(B, Nc, N_KV_GROUPS, CMP_BLOCK * HEAD_DIM_2)
    return jax.nn.silu(z @ w1) @ w2

def nsa_mixer(h, w_in, pos_k, pos_v, wk1, wk2, wv1, wv2, w_o, cos, sin):
    B, S, _ = h.shape
    G, R, dh = N_KV_GROUPS, HEADS_PER_GROUP, HEAD_DIM_2
    scale = HEAD_DIM_2 ** -0.5
    proj = h @ w_in
    q, k_c, v_c, k_s, v_s, k_w, v_w, gate = jnp.split(proj, SPLIT_POINTS, axis=-1)
    q = q.reshape(B, S, N_HEADS_2, dh)
    q_nope = q.reshape(B, S, G, R, dh)
    q_rot = partial_rope_2(q, cos, sin).reshape(B, S, G, R, dh)
    k_c, v_c, k_s, v_s, k_w, v_w = [t.reshape(B, S, G, dh) for t in (k_c, v_c, k_s, v_s, k_w, v_w)]
    k_s = partial_rope_2(k_s, cos, sin)
    k_w = partial_rope_2(k_w, cos, sin)
    pos = jnp.arange(S)

    n_cmp = (S - CMP_BLOCK) // CMP_STRIDE + 1
    blk_tok = jnp.arange(n_cmp)[:, None] * CMP_STRIDE + jnp.arange(CMP_BLOCK)[None, :]
    k_cmp = compress_blocks(k_c[:, blk_tok], pos_k, wk1, wk2)
    v_cmp = compress_blocks(v_c[:, blk_tok], pos_v, wv1, wv2)
    blk_end = jnp.arange(n_cmp) * CMP_STRIDE + CMP_BLOCK - 1
    cmp_mask = blk_end[None, :] <= pos[:, None]
    s_c = jnp.einsum('bsgrd,bngd->bgrsn', q_nope, k_cmp).astype(jnp.float32) * scale
    p_c = jax.nn.softmax(jnp.where(cmp_mask, s_c, NEG_INF_2), axis=-1)
    p_c = p_c * jnp.any(cmp_mask, axis=-1)[:, None].astype(jnp.float32)
    o_cmp = jnp.einsum('bgrsn,bngd->bsgrd', p_c.astype(v_cmp.dtype), v_cmp)

    n_sel_blk = S // SEL_BLOCK
    n_pick = min(N_SELECT, n_sel_blk)
    ci = jnp.arange(n_cmp) * CMP_STRIDE
    sj = jnp.arange(n_sel_blk) * SEL_BLOCK
    overlap = ((ci[:, None] < sj[None, :] + SEL_BLOCK) &
               (ci[:, None] + CMP_BLOCK > sj[None, :])).astype(jnp.float32)
    imp = jnp.einsum('bgrsn,nj->bgsj', p_c, overlap)
    q_blk = pos // SEL_BLOCK
    j = jnp.arange(n_sel_blk)[None, :]
    future = j > q_blk[:, None]
    forced = (j == 0) | (j == q_blk[:, None]) | (j == q_blk[:, None] - 1)
    imp = jnp.where(forced, jnp.inf, jnp.where(future, -jnp.inf, imp))
    _, sel_idx = lax.top_k(imp, n_pick)

    k_blocks = k_s.reshape(B, n_sel_blk, SEL_BLOCK, G, dh).transpose(0, 3, 1, 2, 4)
    v_blocks = v_s.reshape(B, n_sel_blk, SEL_BLOCK, G, dh).transpose(0, 3, 1, 2, 4)
    n_qs = S // SEL_Q_BLOCK
    b_ix = jnp.arange(B)[:, None, None]
    g_ix = jnp.arange(G)[None, :, None]

    def sel_block(args):
        qb, idx, start = args
        flat = idx.reshape(B, G, SEL_Q_BLOCK * n_pick)
        kb = k_blocks[b_ix, g_ix, flat].reshape(B, G, SEL_Q_BLOCK, n_pick * SEL_BLOCK, dh)
        vb = v_blocks[b_ix, g_ix, flat].reshape(B, G, SEL_Q_BLOCK, n_pick * SEL_BLOCK, dh)
        tok = (idx[..., None] * SEL_BLOCK + jnp.arange(SEL_BLOCK)).reshape(B, G, SEL_Q_BLOCK, n_pick * SEL_BLOCK)
        qpos = start + jnp.arange(SEL_Q_BLOCK)
        mask = (tok <= qpos[None, None, :, None])[:, :, None]
        s = jnp.einsum('bqgrd,bgqtd->bgrqt', qb, kb).astype(jnp.float32) * scale
        p = jax.nn.softmax(jnp.where(mask, s, NEG_INF_2), axis=-1).astype(vb.dtype)
        return jnp.einsum('bgrqt,bgqtd->bqgrd', p, vb)

    q_sel = jnp.moveaxis(q_rot.reshape(B, n_qs, SEL_Q_BLOCK, G, R, dh), 1, 0)
    idx_sel = jnp.moveaxis(sel_idx.reshape(B, G, n_qs, SEL_Q_BLOCK, n_pick), 2, 0)
    o_sel = lax.map(sel_block, (q_sel, idx_sel, jnp.arange(n_qs) * SEL_Q_BLOCK))
    o_sel = jnp.moveaxis(o_sel, 0, 1).reshape(B, S, G, R, dh)

    n_qw = S // WIN_Q_BLOCK
    k_pad = jnp.pad(k_w, ((0, 0), (WINDOW_2, 0), (0, 0), (0, 0)))
    v_pad = jnp.pad(v_w, ((0, 0), (WINDOW_2, 0), (0, 0), (0, 0)))
    band = WIN_Q_BLOCK + WINDOW_2

    def win_block(args):
        qb, start = args
        kb = lax.dynamic_slice_in_dim(k_pad, start, band, axis=1)
        vb = lax.dynamic_slice_in_dim(v_pad, start, band, axis=1)
        qpos = start + jnp.arange(WIN_Q_BLOCK)
        kpos = start - WINDOW_2 + jnp.arange(band)
        diff = qpos[:, None] - kpos[None, :]
        mask = (diff >= 0) & (diff < WINDOW_2) & (kpos[None, :] >= 0)
        s = jnp.einsum('bqgrd,btgd->bgrqt', qb, kb).astype(jnp.float32) * scale
        p = jax.nn.softmax(jnp.where(mask, s, NEG_INF_2), axis=-1).astype(vb.dtype)
        return jnp.einsum('bgrqt,btgd->bqgrd', p, vb)

    q_win = jnp.moveaxis(q_rot.reshape(B, n_qw, WIN_Q_BLOCK, G, R, dh), 1, 0)
    o_win = lax.map(win_block, (q_win, jnp.arange(n_qw) * WIN_Q_BLOCK))
    o_win = jnp.moveaxis(o_win, 0, 1).reshape(B, S, G, R, dh)

    gts = jax.nn.sigmoid(gate.reshape(B, S, 3, G, R, 1))
    o = gts[:, :, 0] * o_cmp + gts[:, :, 1] * o_sel + gts[:, :, 2] * o_win
    return o.reshape(B, S, Q_WIDTH) @ w_o

def second_inputs(seed: int = 0) -> dict:
    key = jax.random.key(seed)
    ks = jax.random.split(key, 20)
    nrm = lambda k, shape, fan_in: jax.random.normal(k, shape, jnp.float32) * (fan_in ** -0.5)
    return {
        "x": jax.random.normal(ks[0], (BATCH, SEQ, D_MODEL), jnp.float32),
        "norm_gains": 1.0 + 0.05 * jax.random.normal(ks[1], (DEPTH, 6, D_MODEL), jnp.float32),
        "ffn_w_gate": nrm(ks[2], (DEPTH, 2, D_MODEL, D_FF), D_MODEL),
        "ffn_w_up": nrm(ks[3], (DEPTH, 2, D_MODEL, D_FF), D_MODEL),
        "ffn_w_down": nrm(ks[4], (DEPTH, 2, D_FF, D_MODEL), D_FF),
        "pool_w": nrm(ks[5], (N_POOL_LAYERS, N_POOL_GROUPS, POOL_GROUP, POOL_GROUP), POOL_GROUP),
        "pool_b": 0.01 * jax.random.normal(ks[6], (N_POOL_LAYERS, N_POOL_GROUPS, POOL_GROUP), jnp.float32),
        "pool_scale": 0.5 + 0.1 * jax.random.normal(ks[7], (N_POOL_LAYERS, D_MODEL), jnp.float32),
        "nsa_w_in": nrm(ks[8], (N_NSA_LAYERS, D_MODEL, IN_WIDTH_2), D_MODEL),
        "nsa_cmp_pos_k": 0.1 * jax.random.normal(ks[9], (N_NSA_LAYERS, CMP_BLOCK, HEAD_DIM_2), jnp.float32),
        "nsa_cmp_pos_v": 0.1 * jax.random.normal(ks[10], (N_NSA_LAYERS, CMP_BLOCK, HEAD_DIM_2), jnp.float32),
        "nsa_cmp_wk1": nrm(ks[11], (N_NSA_LAYERS, CMP_BLOCK * HEAD_DIM_2, CMP_HIDDEN), CMP_BLOCK * HEAD_DIM_2),
        "nsa_cmp_wk2": nrm(ks[12], (N_NSA_LAYERS, CMP_HIDDEN, HEAD_DIM_2), CMP_HIDDEN),
        "nsa_cmp_wv1": nrm(ks[13], (N_NSA_LAYERS, CMP_BLOCK * HEAD_DIM_2, CMP_HIDDEN), CMP_BLOCK * HEAD_DIM_2),
        "nsa_cmp_wv2": nrm(ks[14], (N_NSA_LAYERS, CMP_HIDDEN, HEAD_DIM_2), CMP_HIDDEN),
        "nsa_w_o": nrm(ks[15], (N_NSA_LAYERS, Q_WIDTH, D_MODEL), Q_WIDTH),
    }

def second_block(x, norm_gains, ffn_w_gate, ffn_w_up, ffn_w_down, pool_w, pool_b, pool_scale,
              nsa_w_in, nsa_cmp_pos_k, nsa_cmp_pos_v, nsa_cmp_wk1, nsa_cmp_wk2,
              nsa_cmp_wv1, nsa_cmp_wv2, nsa_w_o):
    cos, sin = rope_tables_2(x.shape[1])
    for i in range(DEPTH):
        g = norm_gains[i]
        f = swiglu(rms_norm(x, g[0]), ffn_w_gate[i, 0], ffn_w_up[i, 0], ffn_w_down[i, 0])
        x = x + 0.5 * rms_norm(f, g[1])
        h = rms_norm(x, g[2])
        j = i // N_MIXERS
        if i % N_MIXERS == 0:
            m = pool_mixer(h, pool_w[j], pool_b[j], pool_scale[j])
        else:
            m = nsa_mixer(h, nsa_w_in[j], nsa_cmp_pos_k[j], nsa_cmp_pos_v[j], nsa_cmp_wk1[j],
                          nsa_cmp_wk2[j], nsa_cmp_wv1[j], nsa_cmp_wv2[j], nsa_w_o[j], cos, sin)
        x = x + rms_norm(m, g[3])
        f = swiglu(rms_norm(x, g[4]), ffn_w_gate[i, 1], ffn_w_up[i, 1], ffn_w_down[i, 1])
        x = x + 0.5 * rms_norm(f, g[5])
    return x


def setup_inputs(seed=0):
    out = dict(first_inputs(seed))
    for name, value in second_inputs(seed + 1).items():
        if name != "x":
            out[name + "_2"] = value
    return out


def reference(
    x, norm_mix, w_in, attn_sink, conv_w, norm_attn_out, norm_conv_out, w_out, norm_ffn,
    w_router_group, b_router_group, w_router_expert, b_router_expert, w_expert_gate,
    w_expert_up, w_expert_down, norm_final, norm_gains_2, ffn_w_gate_2, ffn_w_up_2,
    ffn_w_down_2, pool_w_2, pool_b_2, pool_scale_2, nsa_w_in_2, nsa_cmp_pos_k_2,
    nsa_cmp_pos_v_2, nsa_cmp_wk1_2, nsa_cmp_wk2_2, nsa_cmp_wv1_2, nsa_cmp_wv2_2, nsa_w_o_2,
):
    x = first_block(
        x, norm_mix, w_in, attn_sink, conv_w, norm_attn_out, norm_conv_out, w_out, norm_ffn,
        w_router_group, b_router_group, w_router_expert, b_router_expert, w_expert_gate,
        w_expert_up, w_expert_down, norm_final,
    )
    return second_block(
        x, norm_gains_2, ffn_w_gate_2, ffn_w_up_2, ffn_w_down_2, pool_w_2, pool_b_2,
        pool_scale_2, nsa_w_in_2, nsa_cmp_pos_k_2, nsa_cmp_pos_v_2, nsa_cmp_wk1_2,
        nsa_cmp_wk2_2, nsa_cmp_wv1_2, nsa_cmp_wv2_2, nsa_w_o_2,
    )


_drawn_inputs = setup_inputs


def setup_inputs(seed=0):
    import zlib

    import numpy as np

    out = dict(_drawn_inputs(seed))
    spreads = {}
    factors = {'attn_sink': 8.0,
     'norm_conv_out': 2.841,
     'b_router_group': 18.464,
     'b_router_expert': 14.942,
     'nsa_cmp_pos_k_2': 7.785,
     'norm_attn_out': 3.454,
     'norm_ffn': 3.694}
    for name, (base, spread) in spreads.items():
        noise = np.random.default_rng([zlib.crc32(name.encode()), seed]).standard_normal(out[name].shape)
        drawn = base * np.exp(spread * noise) if base else spread * noise
        out[name] = __import__('jax').numpy.asarray(drawn.astype(out[name].dtype))
    for name, factor in factors.items():
        out[name] = (out[name] * factor).astype(out[name].dtype)
    return out
```

```python
from contextlib import ExitStack

import numpy as np

import concourse.bass as bass
from concourse import mybir

F32 = mybir.dt.float32
I32 = mybir.dt.int32
ALU = mybir.AluOpType
ACT = mybir.ActivationFunctionType
AX_X = mybir.AxisListType.X

P = 128
SEQ, D = 256, 1024
TT = SEQ // P
KT = D // P
EPS = 1e-6
DH = 64
SCALE = DH ** -0.5
BIG = 1e30
NE, NG = 32, 4
DE = 512
CAP = 64
PAIRS = NE // 2
MORE = SEQ // CAP - 1
FAR = 1e4
FF = 2816
NCMP = 15
ROPE = 16
THETA = 500000.0
RING = 6
STAGES = ["mix0", "moe0", "mix1", "moe1", "final", "ffn00", "pool", "ffn01", "ffn10", "nsa", "ffn11"]

CONSTS = {}
_at = 0
for _n, _w in (("ident", P), ("upper", P), ("ones", P), ("iota", CAP), ("tie", NG + NE), ("rope_c", TT * ROPE),
               ("rope_s", TT * ROPE), ("band", TT * SEQ), ("causal", SEQ), ("cmp_mask", TT * NCMP), ("cmp_any", TT)):
    CONSTS[_n] = (_at, _at + _w)
    _at += _w
N_CONSTS = _at


def constants():
    c = np.zeros((P, N_CONSTS), np.float32)

    def put(name, a):
        lo, hi = CONSTS[name]
        c[:, lo:hi] = np.asarray(a, np.float32).reshape(P, -1)

    i = np.arange(P)
    tok = i[:, None] + P * np.arange(TT)[None, :]
    put("ident", np.eye(P))
    put("upper", i[:, None] < i[None, :])
    put("ones", np.ones((P, P)))
    put("iota", np.broadcast_to(np.arange(CAP), (P, CAP)))
    put("tie", np.broadcast_to(np.concatenate([np.arange(NG, 0, -1), np.arange(NE, 0, -1)]), (P, NG + NE)))
    inv = np.float32(THETA) ** (-np.arange(0, ROPE, 2, dtype=np.float32) / np.float32(ROPE))
    ang = tok.astype(np.float32)[:, :, None] * inv.astype(np.float32)
    cos, sin = np.cos(ang), np.sin(ang)
    put("rope_c", np.concatenate([cos, cos], -1))
    put("rope_s", np.concatenate([-sin, sin], -1))
    keys = np.arange(SEQ)
    put("band", np.where(np.abs(keys[None, None, :] - tok[:, :, None]) <= 128, 0.0, -BIG))
    put("causal", np.where(keys[None, :] <= P + i[:, None], 0.0, -BIG))
    ends = np.arange(NCMP) * 16 + 31
    ok = ends[None, None, :] <= tok[:, :, None]
    put("cmp_mask", np.where(ok, 0.0, -BIG))
    put("cmp_any", ok.any(-1))
    q = np.arange(SEQ)
    means = np.zeros((SEQ, 4, SEQ), np.float32)
    for n, w in enumerate((2, 4, 8, 16)):
        gap = q[None, :] - q[:, None]
        means[:, n, :] = ((gap >= 0) & (gap < w)) / np.minimum(q + 1, w)[None, :] - (gap == 0)
    return c, means.astype(np.float32)


class Fields:
    pass


class Unit:

    def __init__(self, t, g, half, gp, tile, br, nk, qT, kT, v, mask):
        self.t, self.g, self.half, self.gp, self.tile, self.br, self.nk = t, g, half, gp, tile, br, nk
        self.qT, self.kT, self.v, self.mask = qT, kT, v, mask


class Follow:

    def __init__(self, step=None):
        self.step, self.n, self.p, self.per = step, {}, None, {}

    def past(self, sem, k=1):
        self.n[sem.name] = (sem, self.n.get(sem.name, (sem, 0))[1] + k)

    def to(self, sem, k=1):
        self.past(sem, k)
        v = self.n[sem.name][1]
        if self.p is not None:
            v = self.p * self.per[sem.name] + (v - self.per[sem.name] * self.first)
        return v

    def after(self, sem, k):
        return self.n[sem.name][1] + k

    def enter(self, p, per, first=0):
        self.p, self.per, self.first = p, {s.name: k for s, k in per.items()}, first
        self.was = {k: v for k, v in self.n.items()}

    def leave(self, passes):
        got = {k: v[1] - self.was.get(k, (0, 0))[1] for k, v in self.n.items()}
        got = {k: v for k, v in got.items() if v}
        want = {k: v for k, v in self.per.items() if v}
        assert got == want, (got, want)
        for k, v in got.items():
            self.n[k] = (self.n[k][0], self.n[k][1] + v * (passes - 1))
        self.p = None


def build(nc, a, out, stages):
    ctx = ExitStack()
    with ctx:
        def sb(name, shape, dt=F32):
            return ctx.enter_context(nc.sbuf_tensor(name, shape, dt))

        def sem(name):
            return ctx.enter_context(nc.semaphore(name))

        PS = ctx.enter_context(nc.psum_tensor("PS", [P, 8, 512], F32))

        ring = sb("ring", [P, RING, 4096])
        x = sb("x", [P, TT, D])
        hp = sb("hp", [P, TT, D])
        hT = sb("hT", [P, KT, SEQ])
        gB = sb("gB", [P, 2, D])
        cst = sb("cst", [P, N_CONSTS])
        work = sb("work", [P, 16700])
        gT = sb("gT", [P, 9, KT])
        cw = sb("cw", [P, 2, 3, 4])
        gaT = sb("gaT", [P, 2, 4])
        gcT = sb("gcT", [P, 2, 4])
        wr = sb("wr", [P, 2, KT, NG + NE])
        rbias = sb("rbias", [P, 2, NG + NE])
        sink = sb("sink", [P, 2, 8])
        rows1 = sb("rows1", [33, D])
        pbias, zeros = rows1[0:1, :], rows1[32:33, 0:512]
        w2k = sb("w2k", [P, 2, 2 * DH])
        w2v = sb("w2v", [P, 2, DH])
        cpos = sb("cpos", [P, 2, 16])
        small = sb("small", [P, 64])
        epsb = sb("epsb", [P, 1])
        flag_f = sb("flag_f", [P, 1])
        flag = sb("flag", [P, 1], I32)

        def const(name, parts=P):
            lo, hi = CONSTS[name]
            return cst[0:parts, lo:hi]

        ident, upper, ones = const("ident"), const("upper"), const("ones")
        ss, root, rstd = small[:, 0:2], small[:, 2:4], small[:, 4:6]
        ssc, rootc, rstdc = small[:, 6:8], small[:, 8:10], small[:, 10:12]

        class Carve:
            def __init__(self, start=0):
                self.at = start

            def __call__(self, *shape):
                n = int(np.prod(shape))
                v = work[:, self.at:self.at + n]
                self.at += n
                assert self.at <= 16700, self.at
                if len(shape) == 2:
                    v = v.rearrange("p (a b) -> p a b", a=shape[0])
                if len(shape) == 3:
                    v = v.rearrange("p (a b c) -> p a b c", a=shape[0], b=shape[1])
                return v

        S = Fields()
        S.set_up = sem("set_up")
        S.const_loaded = sem("const_loaded")
        S.x_loaded = sem("x_loaded")
        S.param_loaded = sem("param_loaded")
        S.means_loaded = sem("means_loaded")
        S.x_stored = sem("x_stored")
        S.dve_step = sem("dve_step")
        S.act_step = sem("act_step")
        S.x_ready = sem("x_ready")
        S.root_ready = sem("root_ready")
        S.h_ready = sem("h_ready")
        S.hT_psum = sem("hT_psum")
        S.hT_even = sem("hT_even")
        S.hT_odd = sem("hT_odd")
        S.projected = sem("projected")
        S.act_took = sem("act_took")
        S.dve_took = sem("dve_took")
        S.turned_q = sem("turned_q")
        S.q_turned_act = sem("q_turned_act")
        S.q_turned_dve = sem("q_turned_dve")
        S.scored = sem("scored")
        S.masked = sem("masked")
        S.maxed = sem("maxed")
        S.exped = sem("exped")
        S.turned = sem("turned")
        S.turned_taken = sem("turned_taken")
        S.valued = sem("valued")
        S.o_taken = sem("o_taken")
        S.conv_gain = sem("conv_gain")
        S.conv_ss = sem("conv_ss")
        S.conv_root = sem("conv_root")
        S.ya_root = sem("ya_root")
        S.ya_psum = sem("ya_psum")
        S.yaT_ready = sem("yaT_ready")
        S.half_done = sem("half_done")
        S.acc_done = sem("acc_done")
        S.routed = sem("routed")
        S.gate_e = sem("gate_e")
        S.gate_exp = sem("gate_exp")
        S.marked = sem("marked")
        S.ranked = sem("ranked")
        S.flag_ready = sem("flag_ready")
        S.moe_added = sem("moe_added")
        S.ffn_gu = sem("ffn_gu")
        S.ffn_silu = sem("ffn_silu")
        S.ffn_h = sem("ffn_h")
        S.ffn_down = sem("ffn_down")
        S.scaled = sem("scaled")
        S.z_built = sem("z_built")
        S.z_pos = sem("z_pos")
        S.hidden = sem("hidden")
        S.hc_ready = sem("hc_ready")
        S.compressed = sem("compressed")
        S.kc_ready = sem("kc_ready")
        S.cscored = sem("cscored")
        S.csub = sem("csub")
        S.cexp = sem("cexp")
        S.p_ready = sem("p_ready")
        S.p_turned = sem("p_turned")
        S.pT_ready = sem("pT_ready")
        S.cvalued = sem("cvalued")
        S.o_first = sem("o_first")
        S.gB_loaded = [sem(f"gB_loaded{i}") for i in range(2)]
        S.loaded = [sem(f"ring_loaded{i}") for i in range(RING)]

        def expert_sems(tag, loaded=None):
            s = Fields()
            s.gate_used = sem(f"gate_used_{tag}")
            s.gu_done = sem(f"gu_done_{tag}")
            s.down_done = sem(f"down_done_{tag}")
            s.gathered = sem(f"gathered_{tag}")
            s.oh_turned = sem(f"oh_turned_{tag}")
            s.y_turned = sem(f"y_turned_{tag}")
            s.combined = sem(f"combined_{tag}")
            s.onehot = sem(f"onehot_{tag}")
            s.onehot_g = sem(f"onehot_g_{tag}")
            s.g_taken = sem(f"g_taken_{tag}")
            s.h_made = sem(f"h_made_{tag}")
            s.yT_odd = sem(f"yT_odd_{tag}")
            s.x_odd = sem(f"x_odd_{tag}")
            s.y_hi = sem(f"y_hi_{tag}")
            s.step = sem(f"step_{tag}")
            s.silu_done = sem(f"silu_done_{tag}")
            s.yT_even = sem(f"yT_even_{tag}")
            s.x_even = sem(f"x_even_{tag}")
            s.y_lo = sem(f"y_lo_{tag}")
            s.loaded = loaded or [sem(f"ring_loaded{i}_{tag}") for i in range(RING)]
            return s

        M = expert_sems("moe", S.loaded)
        OV = {l: expert_sems(f"more{l}") for l in range(2) if f"moe{l}" in stages}

        def mixer_views():
            c = Carve()
            b = Fields()
            b.q, b.kv = c(TT, 512), c(TT, 256)
            b.v = b.kv[:, :, P:256]
            b.qT, b.kT = c(4, SEQ), c(1, SEQ)
            b.ya, b.yc = c(TT, 512), c(4, SEQ)
            b.tmp = c(256)
            b.stat = c(4, 16)
            b.z = c(4, SEQ + 2)
            b.P = [c(4, SEQ) for _ in range(2)]
            b.Sm = [c(4, SEQ) for _ in range(2)]
            b.PT = [c(2, 4, P) for _ in range(2)]
            b.sq = hp[:, 0, :].rearrange("p (a b) -> p a b", a=4)
            b.gate_c = hp[:, 1, :].rearrange("p (a b) -> p a b", a=4)
            b.cv = b.P[0]
            b.yaT = b.Sm[0]
            b.junk = b.Sm[1]
            return b

        MB = mixer_views()

        def moe_views():
            c = Carve()
            b = Fields()
            b.xeT = c(KT, P)
            b.sE = c(2, 256)
            b.hE = c(2, 256)
            b.ysT = c(KT, P)
            b.y = c(D)
            b.OH = c(TT, P)
            b.OHg = c(TT, P)
            b.G = c(SEQ)
            b.pos = c(TT, NE + 2)
            b.gate = c(TT, NE + 2)
            b.posv = c(TT, MORE * NE + 2)
            b.gatev = c(TT, MORE * NE + 2)
            b.lg = c(TT, NG + NE)
            b.gd, b.ge, b.gh, b.gk = c(TT, NG), c(TT, NG), c(TT, NG), c(TT, NG)
            b.el, b.el3, b.key = c(TT, NE), c(TT, NE), c(TT, NE)
            b.oh1, b.oh2, b.mk = c(TT, NE), c(TT, NE), c(TT, NE)
            b.s = c(12, TT)
            return b

        EB = moe_views()

        def ffn_views():
            c = Carve()
            b = Fields()
            b.sF, b.hF = c(2, SEQ), c(4, SEQ)
            return b

        FB = ffn_views()
        pool_means = work[:, 0:2048].rearrange("p (a b c) -> p a b c", a=TT, b=4)
        pool_f = work[:, 2048:4096].rearrange("p (a b) -> p a b", a=TT)

        def nsa_views():
            c = Carve()
            b = Fields()
            b.qnT, b.qrT = c(8, SEQ), c(8, SEQ)
            b.kT = [c(2, SEQ) for _ in range(2)]
            b.kv = [c(TT, 512) for _ in range(2)]
            b.v = [kv[:, :, 256:512] for kv in b.kv]
            b.gts = c(TT, 48)
            b.tmp = c(256)
            b.stat = c(4, 16)
            b.KC = c(60)
            b.Vbd = c(4, 256)
            b.hc = c(2, 120)
            b.Sc, b.P32 = [c(16, NCMP) for _ in range(2)], c(TT, 16, 32)
            b.cs = c(6, 16)
            top = c.at
            b.qn, b.qr = c(TT, D), c(TT, D)
            b.kvc = c(TT, 512)
            c.at = top
            b.P = [c(4, SEQ) for _ in range(2)]
            b.Sm = [c(4, SEQ) for _ in range(2)]
            b.PT = [c(2, 4, P) for _ in range(2)]
            b.PcT = b.PT[0]
            b.Z = [hp[:, s, 0:960].rearrange("p (a b) -> p a b", a=16) for s in range(2)]
            return b

        NB = nsa_views()

        def z_view(s, g, r, h):
            src = PS[DH * (g % 2):DH * (g % 2 + 1), s, (g // 2) * SEQ:(g // 2 + 1) * SEQ]
            src = src.rearrange("p (n j r) -> p r j n", j=8, r=2)[:, r, :, h:h + NCMP]
            return NB.Z[s][DH * r:DH * (r + 1), 8 * h:8 * h + 8, g * NCMP:(g + 1) * NCMP], src

        def mixer_units():
            return [Unit(t=t, g=g, half=g, gp=0, tile=0, br=0, nk=2, qT=MB.qT, kT=MB.kT, v=MB.v,
                                    mask=const("band")[:, t * SEQ:(t + 1) * SEQ])
                    for t in range(TT) for g in range(2)]

        def nsa_units():
            return [Unit(t=t, g=g, half=g % 2, gp=g // 2, tile=4 * (g // 2), br=br, nk=t + 1,
                                    qT=NB.qrT, kT=NB.kT[br], v=NB.v[br],
                                    mask=const("causal")[:, P * (1 - t):SEQ])
                    for br in range(2) for t in range(TT) for g in range(4)]

        block = ctx.enter_context(nc.Block())

        @block.sync
        def _(sp):
            w = Follow()
            free = []
            n = [0]

            def load(dst, src, used, k):
                r = n[0] % RING
                if n[0] >= RING:
                    s, m = free[n[0] - RING]
                    sp.wait_ge(s, w.to(s, m))
                sp.dma_start(dst(r), src).then_inc(S.loaded[r], 16)
                free.append((used, k))
                n[0] += 1

            def cols(r_, k, width):
                return lambda r: ring[:, r, 0:k * width].rearrange("p (k n) -> p k n", k=k)

            def wide(src, lo, hi, used, k):
                load(cols(0, KT, hi - lo), src[:, lo:hi].rearrange("(p k) n -> p k n", k=KT), used, k)

            def rows(src, lo, hi, used, k):
                m = (hi - lo) // P
                load(cols(0, m, D), src[lo:hi, :].rearrange("(k p) n -> p k n", p=P), used, k)

            def expert_src(l, e, which):
                if which == "down":
                    return a["w_expert_down"][l, e].rearrange("(f p) n -> p f n", p=P)
                return a["w_expert_" + which][l, e].rearrange("(p k) n -> p k n", k=KT)

            PAIR = (("gate", 0), ("up", 0), ("gate", 1), ("up", 1), ("down", 0), ("down", 1))

            def pair_loads(l, s, e0, wait, ff):
                for j, (which, e) in enumerate(PAIR):
                    r = (n[0] + j) % RING
                    if wait:
                        used = {"gate": s.gate_used, "up": s.gu_done, "down": s.down_done}[which]
                        sp.wait_ge(used, ff.to(used))
                    k = 4 if which == "down" else KT
                    dst = ring[:, r, :].rearrange("p (k n) -> p k n", k=k)
                    sp.dma_start(dst, expert_src(l, e0 + e, which)).then_inc(s.loaded[r], 16)

            def moe_loads(l):
                used = {"gate": M.gate_used, "up": M.gu_done, "down": M.down_done}
                for which, e in PAIR:
                    load(cols(0, 4 if which == "down" else KT, D if which == "down" else DE),
                         expert_src(l, e, which), used[which], 1)
                per = {M.gate_used: 2, M.gu_done: 2, M.down_done: 2}
                with sp.Fori(1, PAIRS) as p:
                    w.enter(p, per, first=1)
                    pair_loads(l, M, 2 * p, True, w)
                    w.leave(PAIRS - 1)
                for which, e in PAIR:
                    free.append((used[which], 1))
                n[0] += RING

            def more_loads(l):
                s = OV[l]
                sp.wait_ge(S.flag_ready, w.to(S.flag_ready))
                most = sp.value_load(flag[0:1, 0:1], min_val=0, max_val=SEQ)
                with sp.If(most > CAP):
                    for q in (M.gate_used, M.gu_done, M.down_done):
                        sp.wait_ge(q, w.after(q, 2))
                    v = Follow()
                    pair_loads(l, s, 0, False, v)
                    with sp.Fori(1, MORE * PAIRS) as q:
                        v.enter(q, {s.gate_used: 2, s.gu_done: 2, s.down_done: 2}, first=1)
                        pair_loads(l, s, (q % PAIRS) * 2, True, v)
                        v.leave(MORE * PAIRS - 1)
                    for q in (s.gate_used, s.gu_done, s.down_done):
                        sp.wait_ge(q, v.to(q, 2))

            def mixer_loads(l):
                wi = a["w_in"][l]
                for lo, hi, k in ((0, 512, 2), (512, 768, 1), (1280, 1792, 2), (1792, 2304, 2), (768, 1280, 2)):
                    wide(wi, lo, hi, S.projected, k)
                rows(a["w_out"][l], 512, 1024, S.acc_done, 1)
                rows(a["w_out"][l], 0, 512, S.acc_done, 1)

            def chunk_loads(i, j, f, width, used, final, dyn=False):
                wg, wu, wd = a["ffn_w_gate_2"][i, j], a["ffn_w_up_2"][i, j], a["ffn_w_down_2"][i, j]
                m = width // P
                wide(wg, f, f + width, S.ffn_gu, m)
                wide(wu, f, f + width, S.ffn_gu, 0)
                rows(wd, f, f + width, S.acc_done if final else S.ffn_down, 1)

            def ffn_loads(i, j):
                for f in range(0, FF, 512):
                    width = min(512, FF - f)
                    chunk_loads(i, j, f, width, None, f + width == FF)

            def nsa_loads():
                wi = a["nsa_w_in_2"][0]
                for lo in range(0, 2560, 512):
                    wide(wi, lo, lo + 512, S.projected, 2)
                wide(wi, 2560, 2608, S.projected, 1)
                for name in ("nsa_cmp_wk1_2", "nsa_cmp_wv1_2"):
                    load(lambda r: ring[:, r, :].rearrange("p (k n) -> p k n", k=16),
                         a[name][0].rearrange("(j p) n -> p j n", p=P), S.hidden, 1)
                rows(a["nsa_w_o_2"][0], 0, 512, S.half_done, 1)
                rows(a["nsa_w_o_2"][0], 512, 1024, S.acc_done, 1)

            sp.dma_start(x[:, :, :], a["x"][0].rearrange("(t p) d -> p t d", p=P)).then_inc(S.x_loaded, 16)
            sp.dma_start(cst[:, :], a["consts"]).then_inc(S.const_loaded, 16)
            for name in stages:
                if name[:3] == "mix":
                    mixer_loads(int(name[3]))
                elif name[:3] == "moe":
                    moe_loads(int(name[3]))
                    more_loads(int(name[3]))
                elif name[:3] == "ffn":
                    ffn_loads(int(name[3]), int(name[4]))
                elif name == "pool":
                    load(lambda r: ring[:, r, 0:2048].rearrange("p (k n) -> p k n", k=8),
                         a["pool_w_2"][0].rearrange("g (c p) e -> p (g c) e", p=P), S.acc_done, 1)
                elif name == "nsa":
                    nsa_loads()
            sp.wait_ge(S.x_ready, len(stages))
            sp.dma_start(out[0].rearrange("(t p) d -> p t d", p=P), x[:, :, :]).then_inc(S.x_stored, 16)
            sp.wait_ge(S.x_stored, 16)

        gains = []

        def gain_list():
            g2 = a["norm_gains_2"]
            src = {"moe0": [a["norm_ffn"][0]], "moe1": [a["norm_ffn"][1]], "final": [a["norm_final"]],
                   "ffn00": [g2[0, 1]], "pool": [a["pool_scale_2"][0], g2[0, 3]], "ffn01": [g2[0, 5]],
                   "ffn10": [g2[1, 1]], "nsa": [g2[1, 3]], "ffn11": [g2[1, 5]]}
            return [(i, s) for i, name in enumerate(stages) for s in src.get(name, [])]

        gains = gain_list()
        N_PARAMS = [0]

        @block.gpsimd
        def _(pool):
            w = Follow()

            def par(dst, src):
                pool.dma_start(dst, src).then_inc(S.param_loaded, 16)
                N_PARAMS[0] += 16

            with nc.allow_non_contiguous_dma(reason="small parameters, transposed"):
                g2 = a["norm_gains_2"]
                for n, src in enumerate((a["norm_mix"][0], a["norm_mix"][1], g2[0, 0], g2[0, 4], g2[1, 0],
                                         g2[1, 2], g2[1, 4])):
                    par(gT[:, n, :], src.rearrange("(p k) -> p k", k=KT))
                par(gT[:, 7, :], g2[0, 2].rearrange("(k p) -> p k", p=P))
                for l in range(2):
                    for t in range(3):
                        par(cw[:, l, t, :], a["conv_w"][l, t].rearrange("(c p) -> p c", p=P))
                    par(gaT[:, l, :], a["norm_attn_out"][l].rearrange("(c p) -> p c", p=P))
                    par(gcT[:, l, :], a["norm_conv_out"][l].rearrange("(c p) -> p c", p=P))
                    par(wr[:, l, :, 0:NG], a["w_router_group"][l].rearrange("(p k) n -> p k n", k=KT))
                    par(wr[:, l, :, NG:], a["w_router_expert"][l].rearrange("(p k) n -> p k n", k=KT))
                    par(rbias[:, l, 0:NG], a["b_router_group"][l].partition_broadcast(P))
                    par(rbias[:, l, NG:], a["b_router_expert"][l].partition_broadcast(P))
                    par(sink[:, l, :], a["attn_sink"][l].partition_broadcast(P))
                par(pbias[:, :], a["pool_b_2"].rearrange("o g e -> o (g e)"))
                for h in range(2):
                    par(w2k[:, :, h * DH:(h + 1) * DH], a["nsa_cmp_wk2_2"][0].rearrange("(c p) d -> p c d", p=P))
                par(w2v[:, :, :], a["nsa_cmp_wv2_2"][0].rearrange("(c p) d -> p c d", p=P))
                for s, name in enumerate(("nsa_cmp_pos_k_2", "nsa_cmp_pos_v_2")):
                    for r in range(2):
                        par(cpos[r * DH:(r + 1) * DH, s, :],
                            a[name][0].rearrange("(j r) d -> r d j", r=2)[r])
            for i, (st, src) in enumerate(gains):
                if i >= 2:
                    pool.wait_ge(S.x_ready, gains[i - 2][0] + 1)
                pool.dma_start(gB[:, i % 2, :], src.partition_broadcast(P)).then_inc(S.gB_loaded[i % 2], 16)
                if i + 1 < len(gains) and st < stages.index("pool") <= gains[i + 1][0] if "pool" in stages else False:
                    pool.wait_ge(S.x_ready, stages.index("pool"))
                    pool.dma_start(pool_means, a["means"].rearrange("(t p) w q -> p t w q", p=P)) \
                        .then_inc(S.means_loaded, 16)

        PARAMS = N_PARAMS[0]

        @block.tensor
        def _(pe):
            w = Follow()
            n = [0]

            def slot():
                r = n[0] % RING
                n[0] += 1
                pe.wait_ge(S.loaded[r], w.to(S.loaded[r], 16))
                return r

            def view(r, k, width):
                return ring[:, r, 0:k * width].rearrange("p (k n) -> p k n", k=k)

            def transpose_h():
                for b in range(4):
                    for k in (2 * b, 2 * b + 1):
                        for t in range(TT):
                            if k == 0:
                                pe.wait_ge(S.h_ready, w.to(S.h_ready))
                            last = pe.transpose(PS[:, b, (k % 2) * SEQ + t * P:(k % 2) * SEQ + (t + 1) * P],
                                                hp[:, t, k * P:(k + 1) * P], ident)
                    last.then_inc(S.hT_psum, 1)
                pe.wait_ge(S.hT_even, w.to(S.hT_even, 2))
                pe.wait_ge(S.hT_odd, w.to(S.hT_odd, 2))

            def tokens_out(r, width, banks, offs=(0, 0), each=True):
                wv = view(r, KT, width)
                for t in range(TT):
                    for k in range(KT):
                        last = pe.matmul(PS[:, banks[t], offs[t]:offs[t] + width], hT[:, k, t * P:(t + 1) * P],
                                         wv[:, k, :], start=(k == 0), stop=(k == KT - 1))
                    if each:
                        last.then_inc(S.projected, 1)
                if not each:
                    last.then_inc(S.projected, 1)

            def channels_out(r, banks):
                wv = view(r, KT, 512)
                for c in range(4):
                    if c == 2 and banks[1] == 4:
                        pe.wait_ge(S.act_took, w.to(S.act_took))
                    for k in range(KT):
                        last = pe.matmul(PS[:, banks[c // 2], (c % 2) * SEQ:(c % 2 + 1) * SEQ],
                                         wv[:, k, c * P:(c + 1) * P], hT[:, k, :],
                                         start=(k == 0), stop=(k == KT - 1))
                    if c % 2:
                        last.then_inc(S.projected, 1)

            def attend(units, b):
                def scores(i):
                    u = units[i]
                    if i >= 2:
                        pe.wait_ge(S.masked, w.to(S.masked))
                    lo = DH * u.half
                    for r in range(4):
                        last = pe.matmul(PS[:, 2 * (i % 2) + r // 2, (r % 2) * SEQ:(r % 2) * SEQ + u.nk * P],
                                         u.qT[lo:lo + DH, u.tile + r, u.t * P:(u.t + 1) * P],
                                         u.kT[lo:lo + DH, u.gp, 0:u.nk * P], start=True, stop=True)
                    last.then_inc(S.scored, 1)

                def turn(i):
                    u = units[i]
                    pe.wait_ge(S.exped, w.to(S.exped))
                    if i:
                        pe.wait_ge(S.turned_taken, w.to(S.turned_taken))
                    for kt in range(u.nk):
                        for r in range(4):
                            last = pe.transpose(PS[:, 4 + kt, r * P:(r + 1) * P],
                                                b.P[i % 2][:, r, kt * P:(kt + 1) * P], ident)
                    last.then_inc(S.turned, 1)

                def values(i):
                    u = units[i]
                    if i >= 2:
                        pe.wait_ge(S.o_taken, w.to(S.o_taken))
                    for r in range(4):
                        lo = r * DH
                        for kt in range(u.nk):
                            last = pe.matmul(PS[:, 6 + i % 2, lo:lo + DH], b.PT[i % 2][:, kt, r, :],
                                             u.v[:, kt, u.g * DH:(u.g + 1) * DH],
                                             start=(kt == 0), stop=(kt == u.nk - 1))
                    last.then_inc(S.valued, 1)

                scores(0)
                for i in range(len(units)):
                    if i + 1 < len(units):
                        scores(i + 1)
                    turn(i)
                    if i:
                        values(i - 1)
                pe.wait_ge(S.turned_taken, w.to(S.turned_taken))
                values(len(units) - 1)
                pe.wait_ge(S.masked, w.to(S.masked, 2))
                pe.wait_ge(S.o_taken, w.to(S.o_taken, 2))

            def mixer(l):
                transpose_h()
                tokens_out(slot(), 512, (4, 5))
                tokens_out(slot(), 256, (6, 6), (0, 256), each=False)
                channels_out(slot(), (7, 0))
                channels_out(slot(), (1, 2))
                channels_out(slot(), (3, 4))
                pe.wait_ge(S.dve_took, w.to(S.dve_took, 3))
                pe.wait_ge(S.act_took, w.to(S.act_took, 4))
                for t in range(TT):
                    for m in range(4):
                        last = pe.transpose(PS[:, 5 + t, m * P:(m + 1) * P], MB.q[:, t, m * P:(m + 1) * P], ident)
                    last.then_inc(S.turned_q, 1)
                for t in range(TT):
                    last = pe.transpose(PS[:, 7, t * P:(t + 1) * P], MB.kv[:, t, 0:P], ident)
                last.then_inc(S.turned_q, 1)
                pe.wait_ge(S.q_turned_act, w.to(S.q_turned_act, 3))
                pe.wait_ge(S.dve_took, w.to(S.dve_took, 4))
                attend(mixer_units(), MB)
                pe.wait_ge(S.conv_gain, w.to(S.conv_gain, 5))
                for t in range(TT):
                    for c in range(4):
                        last = pe.matmul(PS[:, 7, t:t + 1], MB.sq[:, c, t * P:(t + 1) * P], ones[:, 0:1],
                                         start=(c == 0), stop=(c == 3))
                last.then_inc(S.conv_ss, 1)
                for part in range(2):
                    if part:
                        for c in range(4):
                            for t in range(TT):
                                last = pe.transpose(PS[:, 4 + c // 2, (c % 2) * SEQ + t * P:(c % 2) * SEQ + (t + 1) * P],
                                                    MB.ya[:, t, c * P:(c + 1) * P], ident)
                            if c % 2:
                                last.then_inc(S.ya_psum, 1)
                        pe.wait_ge(S.yaT_ready, w.to(S.yaT_ready, 4))
                        pe.wait_ge(S.conv_root, w.to(S.conv_root))
                    src = MB.yaT if part else MB.yc
                    wv = view(slot(), 4, D)
                    for t in range(TT):
                        for h in range(2):
                            for c in range(4):
                                last = pe.matmul(PS[:, 4 * part + 2 * t + h, :], src[:, c, t * P:(t + 1) * P],
                                                 wv[:, c, h * 512:(h + 1) * 512], start=(c == 0), stop=(c == 3))
                    last.then_inc(S.acc_done, 1)

            def clear_acc():
                for b in range(4):
                    pe.matmul(PS[:, b, :], zeros[:, 0:P], zeros[:, :], start=True, stop=False,
                              skip_group_check=True)

            def experts(s, f, first, passes):
                def take(r):
                    pe.wait_ge(s.loaded[r], f.to(s.loaded[r], 16))
                    return r

                def gather():
                    pe.wait_ge(s.onehot, f.to(s.onehot))
                    for b in range(2):
                        for k in range(4 * b, 4 * b + 4):
                            for t in range(TT):
                                last = pe.matmul(PS[:, 4 + b, (k % 4) * P:(k % 4 + 1) * P],
                                                 hp[:, t, k * P:(k + 1) * P], EB.OH[:, t, :],
                                                 start=(t == 0), stop=(t == 1))
                        last.then_inc(s.gathered, 1)

                clear_acc()
                gather()
                per = {s.loaded[r]: 16 for r in range(RING)}
                per.update({s.onehot: 1, s.x_even: 1, s.x_odd: 1, s.onehot_g: 1, s.g_taken: 1, s.h_made: 2,
                            s.yT_even: 1, s.yT_odd: 1, s.y_lo: 1, s.y_hi: 1})
                with pe.Fori(0, passes) as p:
                    f.enter(p, per)
                    for j in range(2):
                        for m in range(2):
                            wv = view(take((first + 2 * j + m) % RING), KT, DE)
                            if j == 0 and m == 0:
                                pe.wait_ge(s.x_even, f.to(s.x_even))
                                pe.wait_ge(s.x_odd, f.to(s.x_odd))
                            for ft in range(4):
                                lo = m * 256 + ft * CAP
                                for k in range(KT):
                                    last = pe.matmul(PS[:, 4 + j, lo:lo + CAP], wv[:, k, ft * P:(ft + 1) * P],
                                                     EB.xeT[:, k, j * CAP:(j + 1) * CAP],
                                                     start=(k == 0), stop=(k == KT - 1))
                            last.then_inc(s.gu_done if m else s.gate_used, 1)
                        if j == 0:
                            pe.wait_ge(s.onehot_g, f.to(s.onehot_g))
                            for t in range(TT):
                                last = pe.transpose(PS[:, 6, t * P:(t + 1) * P], EB.OHg[:, t, :], ident)
                            last.then_inc(s.oh_turned, 1)
                    for j in range(2):
                        wv = view(take((first + 4 + j) % RING), 4, D)
                        if j == 0:
                            pe.wait_ge(s.g_taken, f.to(s.g_taken))
                        pe.wait_ge(s.h_made, f.to(s.h_made))
                        for dt in range(KT):
                            for ft in range(4):
                                last = pe.matmul(PS[:, 6 + j, dt * CAP:(dt + 1) * CAP], wv[:, ft, dt * P:(dt + 1) * P],
                                                 EB.hE[:, j, ft * CAP:(ft + 1) * CAP],
                                                 start=(ft == 0), stop=(ft == 3))
                        last.then_inc(s.down_done, 1)
                    gather()
                    pe.wait_ge(s.yT_even, f.to(s.yT_even))
                    pe.wait_ge(s.yT_odd, f.to(s.yT_odd))
                    for b in range(2):
                        for k in range(4 * b, 4 * b + 4):
                            last = pe.transpose(PS[:, 6 + b, (k % 4) * P:(k % 4 + 1) * P], EB.ysT[:, k, :], ident)
                        last.then_inc(s.y_turned, 1)
                    pe.wait_ge(s.y_lo, f.to(s.y_lo))
                    pe.wait_ge(s.y_hi, f.to(s.y_hi))
                    for t in range(TT):
                        for h in range(2):
                            last = pe.matmul(PS[:, 2 * t + h, :], EB.G[:, t * P:(t + 1) * P],
                                             EB.y[:, h * 512:(h + 1) * 512], start=False, stop=False,
                                             skip_group_check=True)
                    last.then_inc(s.combined, 1)
                    f.leave(passes)
                f.past(s.x_even)
                f.past(s.x_odd)

            def moe(l):
                transpose_h()
                for t in range(TT):
                    for k in range(KT):
                        last = pe.matmul(PS[:, 4, t * 64:t * 64 + NG + NE], hT[:, k, t * P:(t + 1) * P],
                                         wr[:, l, k, :], start=(k == 0), stop=(k == KT - 1))
                last.then_inc(S.routed, 1)
                pe.wait_ge(S.marked, w.to(S.marked))
                pe.matmul(PS[:, 5, 0:NE], upper, EB.mk[:, 0, :], start=True, stop=True)
                pe.matmul(PS[:, 5, NE:2 * NE], ones, EB.mk[:, 0, :], start=True, stop=False)
                pe.matmul(PS[:, 5, NE:2 * NE], upper, EB.mk[:, 1, :], start=False, stop=True)
                pe.matmul(PS[:, 5, 2 * NE:3 * NE], ones, EB.mk[:, 0, :], start=True, stop=False)
                pe.matmul(PS[:, 5, 2 * NE:3 * NE], ones, EB.mk[:, 1, :], start=False, stop=True) \
                    .then_inc(S.ranked, 1)
                experts(M, w, n[0] % RING, PAIRS)
                n[0] += RING * PAIRS
                pe.wait_ge(S.flag_ready, w.to(S.flag_ready))
                pe.wait_ge(S.moe_added, w.to(S.moe_added))
                most = pe.value_load(flag[0:1, 0:1], min_val=0, max_val=SEQ)
                with pe.If(most > CAP):
                    experts(OV[l], Follow(), n[0] % RING, MORE * PAIRS)

            def ffn():
                transpose_h()
                clear_acc()

                def run(tiles, final):
                    taken = {}

                    def take(c, m):
                        if (c, m) not in taken:
                            taken[c, m] = slot_at(c, m)
                        return taken[c, m]

                    def gate_up(i):
                        c, ft, width, _ = tiles[i]
                        for m in range(2):
                            wv = view(take(c, m), KT, width)
                            for k in range(KT):
                                last = pe.matmul(PS[:, 4 + i % 4, m * SEQ:(m + 1) * SEQ],
                                                 wv[:, k, ft * P:(ft + 1) * P], hT[:, k, :],
                                                 start=(k == 0), stop=(k == KT - 1))
                        last.then_inc(S.ffn_gu, 1)

                    def down(i):
                        c, ft, width, end = tiles[i]
                        wv = view(take(c, 2), width // P, D)
                        pe.wait_ge(S.ffn_h, w.to(S.ffn_h))
                        for t in range(TT):
                            for h in range(2):
                                last = pe.matmul(PS[:, 2 * t + h, :], FB.hF[:, i % 4, t * P:(t + 1) * P],
                                                 wv[:, ft, h * 512:(h + 1) * 512], start=False, stop=False,
                                                 skip_group_check=True)
                        if end:
                            last.then_inc(S.acc_done if final and i == len(tiles) - 1 else S.ffn_down, 1)

                    base = n[0]

                    def slot_at(c, m):
                        r = (base + 3 * c + m) % RING
                        pe.wait_ge(S.loaded[r], w.to(S.loaded[r], 16))
                        return r

                    gate_up(0)
                    for i in range(len(tiles)):
                        if i + 1 < len(tiles):
                            gate_up(i + 1)
                        down(i)
                    n[0] += 3 * (tiles[-1][0] + 1)

                whole = [(c, ft, 512, ft == 3) for c in range(2) for ft in range(4)]
                per = {S.loaded[r]: 16 for r in range(RING)}
                per[S.ffn_h] = 8
                with pe.Fori(0, 2) as p:
                    w.enter(p, per)
                    run(whole, False)
                    w.leave(2)
                n[0] += RING
                run([(0, ft, 512, ft == 3) for ft in range(4)] + [(1, ft, 256, ft == 1) for ft in range(2)], True)

            def pool_mix():
                pe.wait_ge(S.means_loaded, w.to(S.means_loaded, 16))
                for c in range(KT):
                    for t in range(TT):
                        if c == 0:
                            pe.wait_ge(S.h_ready, w.to(S.h_ready))
                        last = pe.matmul(PS[:, c // 2, (c % 2) * SEQ:(c % 2 + 1) * SEQ], hp[:, t, c * P:(c + 1) * P],
                                         pool_means[:, t, c // 2, :], start=(t == 0), stop=(t == 1))
                    if c % 2:
                        last.then_inc(S.hT_psum, 1)
                pe.wait_ge(S.hT_even, w.to(S.hT_even, 2))
                pe.wait_ge(S.hT_odd, w.to(S.hT_odd, 2))
                wv = view(slot(), 8, 256)
                for t in range(TT):
                    for g in range(4):
                        o = PS[:, 2 * t + g // 2, (g % 2) * 256:(g % 2 + 1) * 256]
                        for c in range(2):
                            pe.matmul(o, hT[:, 2 * g + c, t * P:(t + 1) * P], wv[:, 2 * g + c, :],
                                      start=(c == 0), stop=False)
                        last = pe.matmul(o, ones[0:1, 0:P], pbias[0:1, g * 256:(g + 1) * 256],
                                         start=False, stop=True)
                last.then_inc(S.acc_done, 1)

            def nsa():
                transpose_h()
                tokens_out(slot(), 512, (4, 5))
                tokens_out(slot(), 512, (6, 7))
                tokens_out(slot(), 512, (0, 1))
                tokens_out(slot(), 512, (2, 3))
                pe.wait_ge(S.act_took, w.to(S.act_took, 2))
                tokens_out(slot(), 512, (4, 5))
                pe.wait_ge(S.act_took, w.to(S.act_took, 1))
                tokens_out(slot(), 48, (6, 6), (0, 48), each=False)
                pe.wait_ge(S.act_took, w.to(S.act_took, 8))
                pe.wait_ge(S.dve_took, w.to(S.dve_took, 8))
                for src, b0 in ((NB.qn, 0), (NB.qr, 4)):
                    for t in range(TT):
                        for gp in range(2):
                            for r in range(4):
                                m = gp * 4 + r
                                last = pe.transpose(PS[:, b0 + 2 * t + gp, r * P:(r + 1) * P],
                                                    src[:, t, m * P:(m + 1) * P], ident)
                            last.then_inc(S.turned_q, 1)
                pe.wait_ge(S.q_turned_act, w.to(S.q_turned_act, 4))
                for b, (src, off) in enumerate(((NB.kvc, 0), (NB.kvc, 256), (NB.kv[0], 0), (NB.kv[1], 0))):
                    for gp in range(2):
                        for t in range(TT):
                            last = pe.transpose(PS[:, b, gp * SEQ + t * P:gp * SEQ + (t + 1) * P],
                                                src[:, t, off + gp * P:off + (gp + 1) * P], ident)
                    last.then_inc(S.turned_q, 1)
                pe.wait_ge(S.q_turned_dve, w.to(S.q_turned_dve, 4))
                for s in range(2):
                    wv = view(slot(), 16, 256)
                    pe.wait_ge(S.z_pos, w.to(S.z_pos))
                    for c in range(2):
                        for j in range(16):
                            last = pe.matmul(PS[:, 4 + s, c * 60:(c + 1) * 60], wv[:, j, c * P:(c + 1) * P],
                                             NB.Z[s][:, j, :], start=(j == 0), stop=(j == 15))
                    last.then_inc(S.hidden, 1)
                pe.wait_ge(S.hc_ready, w.to(S.hc_ready, 2))
                for c in range(2):
                    pe.matmul(PS[:, 6, 0:60], w2k[:, c, :], NB.hc[:, 0, c * 60:(c + 1) * 60],
                              start=(c == 0), stop=(c == 1))
                for g in range(4):
                    for c in range(2):
                        last = pe.matmul(PS[0:NCMP, 7, g * DH:(g + 1) * DH],
                                         NB.hc[:, 1, c * 60 + g * NCMP:c * 60 + (g + 1) * NCMP], w2v[:, c, :],
                                         start=(c == 0), stop=(c == 1))
                last.then_inc(S.compressed, 1)
                pe.wait_ge(S.kc_ready, w.to(S.kc_ready))
                pe.wait_ge(S.q_turned_act, w.to(S.q_turned_act, 2))
                for t in range(TT):
                    for h in range(16):
                        g, r = h // 4, h % 4
                        lo = DH * (g % 2)
                        last = pe.matmul(PS[:, 2 * t + g % 2, h * 16:h * 16 + NCMP],
                                         NB.qnT[lo:lo + DH, 4 * (g // 2) + r, t * P:(t + 1) * P],
                                         NB.KC[lo:lo + DH, g * NCMP:(g + 1) * NCMP], start=True, stop=True)
                    last.then_inc(S.cscored, 1)
                for t in range(TT):
                    pe.wait_ge(S.p_ready, w.to(S.p_ready))
                    for g in range(4):
                        last = pe.transpose(PS[:, 2 + t, g * P:(g + 1) * P], NB.P32[:, t, 4 * g:4 * g + 4, :], ident)
                    last.then_inc(S.p_turned, 1)
                for t in range(TT):
                    pe.wait_ge(S.pT_ready, w.to(S.pT_ready))
                    for g in range(4):
                        last = pe.matmul(PS[:, 4 + 2 * t + g // 2, (g % 2) * 256:(g % 2 + 1) * 256],
                                         NB.PcT[:, t, g, :], NB.Vbd[:, g, :], start=True, stop=True)
                    last.then_inc(S.cvalued, 1)
                pe.wait_ge(S.o_first, w.to(S.o_first, 2))
                attend(nsa_units(), NB)
                transpose_h()
                for m in range(2):
                    wv = view(slot(), 4, D)
                    for t in range(TT):
                        for h in range(2):
                            for k in range(4):
                                last = pe.matmul(PS[:, 2 * t + h + 4, :], hT[:, 4 * m + k, t * P:(t + 1) * P],
                                                 wv[:, k, h * 512:(h + 1) * 512],
                                                 start=(m == 0 and k == 0), stop=(m == 1 and k == 3))
                    last.then_inc(S.acc_done if m else S.half_done, 1)

            pe.wait_ge(S.const_loaded, w.to(S.const_loaded, 16))
            pe.wait_ge(S.param_loaded, PARAMS)
            pe.wait_ge(S.set_up, w.to(S.set_up, 2))
            for name in stages:
                if name[:3] == "mix":
                    mixer(int(name[3]))
                elif name[:3] == "moe":
                    moe(int(name[3]))
                elif name[:3] == "ffn":
                    ffn()
                elif name == "pool":
                    pool_mix()
                elif name == "nsa":
                    nsa()

        @block.scalar
        def _(act):
            w = Follow(S.act_step)
            seen_x = [False]

            def copy(o, i):
                return act.activation(o, i, ACT.Copy)

            def squares(src, junk, sums):
                for t in range(TT):
                    last = act.activation(junk(t), src(t), ACT.Square, accum_out=sums[:, t:t + 1])
                last.then_inc(S.act_step, 1)
                act.wait_ge(S.act_step, w.to(S.act_step))

            def roots(o, i, width, s):
                act.activation(o, i, ACT.Sqrt, bias=epsb[:, 0:1], scale=1.0 / width).then_inc(s, 1)

            def x_now():
                if seen_x[0]:
                    act.wait_ge(S.x_ready, w.to(S.x_ready))
                else:
                    act.wait_ge(S.x_loaded, w.to(S.x_loaded, 16))
                    act.wait_ge(S.set_up, w.to(S.set_up, 2))
                    act.wait_ge(S.param_loaded, PARAMS)
                    seen_x[0] = True

            def norm():
                x_now()
                squares(lambda t: x[:, t, :], lambda t: hp[:, t, :], ss)
                roots(root, ss, D, S.root_ready)

            def take_hT(gain):
                for b in (0, 2):
                    act.wait_ge(S.hT_psum, w.to(S.hT_psum))
                    if gain is None:
                        i = copy(hT[:, 2 * b:2 * b + 2, :].rearrange("p a b -> p (a b)"), PS[:, b, :])
                    else:
                        for k in range(2):
                            i = act.activation(hT[:, 2 * b + k, :], PS[:, b, k * SEQ:(k + 1) * SEQ], ACT.Copy,
                                               scale=gT[:, gain, 2 * b + k:2 * b + k + 1])
                    i.then_inc(S.hT_even, 1)
                    w.past(S.hT_psum)

            def post(bank):
                squares(lambda t: PS[:, bank + 2 * t:bank + 2 * t + 2, :], lambda t: hp[:, t, :].rearrange(
                    "p (a b) -> p a b", a=2), ss)
                roots(root, ss, D, S.root_ready)

            def attend(units, b, sinks):
                def take(i):
                    act.wait_ge(S.turned, w.to(S.turned))
                    nk = units[i].nk
                    copy(b.PT[i % 2][:, 0:nk, :, :].rearrange("p k r q -> p k (r q)"), PS[:, 4:4 + nk, :]) \
                        .then_inc(S.turned_taken, 1)

                for i, u in enumerate(units):
                    act.wait_ge(S.maxed, w.to(S.maxed))
                    st = b.stat[:, i % 4, :]
                    if sinks:
                        act.activation(st[:, 8:12], st[:, 8:12], ACT.Exp)
                    for r in range(4):
                        last = act.activation(b.P[i % 2][:, r, 0:u.nk * P], b.Sm[i % 2][:, r, 0:u.nk * P], ACT.Exp,
                                              bias=st[:, r:r + 1], scale=SCALE, accum_out=st[:, 4 + r:5 + r])
                    last.then_inc(S.exped, 1)
                    if i:
                        take(i - 1)
                take(len(units) - 1)

            def mixer(l):
                norm()
                take_hT(l)
                for t in range(TT):
                    act.wait_ge(S.projected, w.to(S.projected))
                    copy(MB.q[:, t, :].rearrange("p (r h d) -> p h r d", h=2, r=4),
                         PS[:, 4 + t, :].rearrange("p (h r d) -> p h r d", h=2, r=4)).then_inc(S.act_took, 1)
                act.wait_ge(S.projected, w.to(S.projected))
                copy(MB.kv.rearrange("p a b -> p (a b)"), PS[:, 6, :]).then_inc(S.act_took, 1)
                for h in range(2):
                    act.wait_ge(S.projected, w.to(S.projected))
                    copy(MB.gate_c[:, 2 * h:2 * h + 2, :].rearrange("p a b -> p (a b)"), PS[:, (7, 0)[h], :]) \
                        .then_inc(S.act_took, 1)
                w.past(S.projected, 4)
                for t in range(TT):
                    act.wait_ge(S.turned_q, w.to(S.turned_q))
                    copy(MB.qT[:, :, t * P:(t + 1) * P], PS[:, 5 + t, :].rearrange("p (m q) -> p m q", m=4)) \
                        .then_inc(S.q_turned_act, 1)
                act.wait_ge(S.turned_q, w.to(S.turned_q))
                copy(MB.kT[:, 0, :], PS[:, 7, 0:SEQ]).then_inc(S.q_turned_act, 1)
                act.wait_ge(S.dve_took, w.to(S.dve_took, 7))
                attend(mixer_units(), MB, True)
                act.activation(MB.sq, MB.yc, ACT.Square).then_inc(S.conv_gain, 1)
                act.wait_ge(S.conv_gain, w.to(S.conv_gain))
                for c in range(4):
                    act.activation(MB.yc[:, c, :], MB.yc[:, c, :], ACT.Copy, scale=gcT[:, l, c:c + 1]) \
                        .then_inc(S.conv_gain, 1)
                w.past(S.conv_gain, 4)
                act.wait_ge(S.o_taken, w.to(S.o_taken, 4))
                squares(lambda t: MB.ya[:, t, :], lambda t: MB.junk[:, 2 * t:2 * t + 2, :].rearrange(
                    "p a b -> p (a b)"), ss)
                roots(root, ss, 512, S.ya_root)
                act.wait_ge(S.conv_ss, w.to(S.conv_ss))
                roots(rootc, PS[:, 7, 0:2], 512, S.conv_root)
                for c in range(4):
                    if c % 2 == 0:
                        act.wait_ge(S.ya_psum, w.to(S.ya_psum))
                    act.activation(MB.yaT[:, c, :], PS[:, 4 + c // 2, (c % 2) * SEQ:(c % 2 + 1) * SEQ], ACT.Copy,
                                   scale=gaT[:, l, c:c + 1]).then_inc(S.yaT_ready, 1)
                w.past(S.acc_done, 2)

            def experts(s, f, passes):
                def first_of(q, k=1):
                    act.wait_ge(q, f.to(q))
                    f.past(q, k)

                def take_x():
                    first_of(s.gathered)
                    copy(EB.xeT[:, 0:4, :].rearrange("p a b -> p (a b)"), PS[:, 4, :]).then_inc(s.x_even, 1)

                take_x()
                with act.Fori(0, passes) as p:
                    f.enter(p, {s.gathered: 2, s.gu_done: 2, s.down_done: 2, s.y_turned: 2})
                    for j in range(2):
                        act.wait_ge(s.gu_done, f.to(s.gu_done))
                        act.activation(EB.sE[:, j, :], PS[:, 4 + j, 0:256], ACT.Silu).then_inc(s.silu_done, 1)
                    first_of(s.down_done)
                    copy(EB.ysT[:, :, 0:CAP], PS[:, 6, :].rearrange("p (k q) -> p k q", k=KT)).then_inc(s.yT_even, 1)
                    take_x()
                    first_of(s.y_turned)
                    copy(EB.y[:, 0:512], PS[:, 6, :]).then_inc(s.y_lo, 1)
                    f.leave(passes)

            def moe(l):
                norm()
                take_hT(None)
                act.wait_ge(S.gate_e, w.to(S.gate_e))
                act.activation(EB.ge, EB.gd, ACT.Exp).then_inc(S.gate_exp, 1)
                act.wait_ge(S.gate_e, w.to(S.gate_e))
                act.activation(EB.s[:, 5, :], EB.s[:, 4, :], ACT.Exp).then_inc(S.gate_exp, 1)
                experts(M, w, PAIRS)
                act.wait_ge(S.flag_ready, w.to(S.flag_ready))
                most = act.value_load(flag[0:1, 0:1], min_val=0, max_val=SEQ)
                with act.If(most > CAP):
                    experts(OV[l], Follow(), MORE * PAIRS)

            def ffn(gain):
                norm()
                take_hT(gain)

                def run(n):
                    for i in range(n):
                        act.wait_ge(S.ffn_gu, w.to(S.ffn_gu))
                        act.activation(FB.sF[:, i % 2, :], PS[:, 4 + i % 4, 0:SEQ], ACT.Silu).then_inc(S.ffn_silu, 1)

                with act.Fori(0, 2) as p:
                    w.enter(p, {S.ffn_gu: 8})
                    run(8)
                    w.leave(2)
                run(6)
                act.wait_ge(S.acc_done, w.to(S.acc_done))
                post(0)

            def pool_mix():
                norm()
                take_hT(7)
                w.past(S.acc_done)
                act.wait_ge(S.scaled, w.to(S.scaled, 2))
                squares(lambda t: pool_f[:, t, :], lambda t: hp[:, t, :], ss)
                roots(root, ss, D, S.root_ready)

            def nsa():
                norm()
                take_hT(5)
                for gp in range(2):
                    for t in range(TT):
                        act.wait_ge(S.projected, w.to(S.projected))
                        copy(NB.qn[:, t, gp * 512:(gp + 1) * 512].rearrange("p (r h d) -> p h r d", r=4, h=2),
                             PS[:, 4 + 2 * gp + t, :].rearrange("p (h r d) -> p h r d", r=4, h=2)) \
                            .then_inc(S.act_took, 1)
                for t in range(TT):
                    act.wait_ge(S.projected, w.to(S.projected))
                    copy(NB.kvc[:, t, :], PS[:, t, :]).then_inc(S.act_took, 1)
                for br in range(2):
                    for t in range(TT):
                        act.wait_ge(S.projected, w.to(S.projected))
                        copy(NB.kv[br][:, t, :], PS[:, 2 + 2 * br + t, :]).then_inc(S.act_took, 1)
                act.wait_ge(S.projected, w.to(S.projected))
                act.activation(NB.gts.rearrange("p a b -> p (a b)"), PS[:, 6, 0:96], ACT.Sigmoid) \
                    .then_inc(S.act_took, 1)
                for t in range(TT):
                    for gp in range(2):
                        act.wait_ge(S.turned_q, w.to(S.turned_q))
                        copy(NB.qnT[:, 4 * gp:4 * gp + 4, t * P:(t + 1) * P],
                             PS[:, 2 * t + gp, :].rearrange("p (m q) -> p m q", m=4)).then_inc(S.q_turned_act, 1)
                w.past(S.turned_q, 5)
                act.wait_ge(S.turned_q, w.to(S.turned_q))
                for g in range(4):
                    for r in range(2):
                        for h in range(2):
                            last = copy(*z_view(1, g, r, h))
                last.then_inc(S.z_built, 1)
                for br in range(2):
                    act.wait_ge(S.turned_q, w.to(S.turned_q))
                    copy(NB.kT[br].rearrange("p a b -> p (a b)"), PS[:, 2 + br, :]).then_inc(S.q_turned_act, 1)
                for s in range(2):
                    act.wait_ge(S.hidden, w.to(S.hidden))
                    act.activation(NB.hc[:, s, :], PS[:, 4 + s, 0:120], ACT.Silu).then_inc(S.hc_ready, 1)
                for t in range(TT):
                    act.wait_ge(S.csub, w.to(S.csub))
                    act.activation(NB.Sc[t], NB.Sc[t], ACT.Exp, scale=SCALE).then_inc(S.cexp, 1)
                for t in range(TT):
                    act.wait_ge(S.p_turned, w.to(S.p_turned))
                    copy(NB.PcT[:, t, :, :].rearrange("p a b -> p (a b)"), PS[:, 2 + t, :]).then_inc(S.pT_ready, 1)
                for t in range(TT):
                    act.wait_ge(S.cvalued, w.to(S.cvalued))
                    copy(hp[:, t, :].rearrange("p (a b) -> p a b", a=2), PS[:, 4 + 2 * t:6 + 2 * t, :]) \
                        .then_inc(S.o_first, 1)
                attend(nsa_units(), NB, False)
                take_hT(None)
                act.wait_ge(S.acc_done, w.to(S.acc_done))
                post(4)

            FFN_GAIN = {"ffn00": 2, "ffn01": 3, "ffn10": 4, "ffn11": 6}
            for name in stages:
                if name[:3] == "mix":
                    mixer(int(name[3]))
                elif name[:3] == "moe":
                    moe(int(name[3]))
                elif name == "final":
                    norm()
                elif name[:3] == "ffn":
                    ffn(FFN_GAIN[name])
                elif name == "pool":
                    pool_mix()
                elif name == "nsa":
                    nsa()

        @block.vector
        def _(v):
            w = Follow(S.dve_step)
            gi = [0]

            def gain_rows():
                i = gi[0]
                gi[0] += 1
                v.wait_ge(S.gB_loaded[i % 2], w.to(S.gB_loaded[i % 2], 16))
                return gB[:, i % 2, :]

            def reciprocal(o, i):
                v.reciprocal(o, i).then_inc(S.dve_step, 1)
                v.wait_ge(S.dve_step, w.to(S.dve_step))

            def bc(ap, shape):
                return ap.to_broadcast(shape)

            def norm(permute=True, gain=None):
                v.wait_ge(S.root_ready, w.to(S.root_ready))
                reciprocal(rstd, root)
                for t in range(TT):
                    xi, o = x[:, t, :], hp[:, t, :]
                    if permute:
                        xi = xi.rearrange("p (q k) -> p k q", k=KT)
                        o = o.rearrange("p (k q) -> p k q", k=KT)
                    if gain is None:
                        i = v.tensor_scalar(o, xi, rstd[:, t:t + 1], None, ALU.mult)
                    else:
                        i = v.scalar_tensor_tensor(o, xi, rstd[:, t:t + 1],
                                                   gain.rearrange("p (q k) -> p k q", k=KT), ALU.mult, ALU.mult)
                    i.then_inc(S.h_ready, 1)

            def take_hT(gain):
                for b in (1, 3):
                    v.wait_ge(S.hT_psum, w.to(S.hT_psum, 2))
                    if gain is None:
                        i = v.tensor_copy(hT[:, 2 * b:2 * b + 2, :].rearrange("p a b -> p (a b)"), PS[:, b, :])
                    else:
                        for k in range(2):
                            i = v.tensor_scalar(hT[:, 2 * b + k, :], PS[:, b, k * SEQ:(k + 1) * SEQ],
                                                gT[:, gain, 2 * b + k:2 * b + k + 1], None, ALU.mult)
                    i.then_inc(S.hT_odd, 1)

            def post(src, factor):
                gain = gain_rows()
                v.wait_ge(S.root_ready, w.to(S.root_ready))
                reciprocal(rstd, root)
                for t in range(TT):
                    v.scalar_tensor_tensor(hp[:, t, :], src(t), rstd[:, t:t + 1], gain, ALU.mult, ALU.mult).then_inc(S.dve_step, 1)
                    v.wait_ge(S.dve_step, w.to(S.dve_step))
                    v.scalar_tensor_tensor(x[:, t, :], hp[:, t, :], factor, x[:, t, :], ALU.mult, ALU.add).then_inc(S.x_ready if t else S.dve_step, 1)
                    v.wait_ge(S.x_ready if t else S.dve_step, w.to(S.x_ready if t else S.dve_step))

            def psum_rows(bank):
                return lambda t: PS[:, bank + 2 * t:bank + 2 * t + 2, :].rearrange("p a b -> p (a b)")

            def rotate(src, dst, t, tmp):
                n = src.shape[1]
                A = tmp[:, 0:n * ROPE].rearrange("p (h c) -> p h c", c=ROPE)
                B = tmp[:, 128:128 + n * ROPE].rearrange("p (h c) -> p h c", c=ROPE)
                H2 = ROPE // 2

                def table(name, lo, hi):
                    c0 = CONSTS[name][0] + t * ROPE
                    return cst[:, c0 + lo:c0 + hi].unsqueeze(1).to_broadcast([P, n, hi - lo])

                v.tensor_tensor(A, src[:, :, 0:ROPE], table("rope_c", 0, ROPE), ALU.mult)
                v.tensor_tensor(B[:, :, 0:H2], src[:, :, H2:ROPE], table("rope_s", 0, H2), ALU.mult)
                v.tensor_tensor(B[:, :, H2:ROPE], src[:, :, 0:H2], table("rope_s", H2, ROPE), ALU.mult).then_inc(S.dve_step, 1)
                v.wait_ge(S.dve_step, w.to(S.dve_step))
                return v.tensor_tensor(dst[:, :, 0:ROPE], A, B, ALU.add)

            def attend(units, b, sinks, finish):
                def stats(i):
                    u = units[i]
                    st = b.stat[:, i % 4, :]
                    n = u.nk * P
                    v.wait_ge(S.scored, w.to(S.scored))
                    if i >= 2:
                        v.wait_ge(S.exped, w.to(S.exped))
                    s4 = PS[:, 2 * (i % 2):2 * (i % 2) + 2, :].rearrange("p a (r k) -> p (a r) k", r=2)[:, :, 0:n]
                    sm = b.Sm[i % 2][:, :, 0:n]
                    v.tensor_tensor(sm, s4, u.mask.unsqueeze(1).to_broadcast([P, 4, n]), ALU.add).then_inc(S.masked, 1)
                    v.wait_ge(S.masked, w.to(S.masked))
                    v.tensor_reduce(st[:, 0:4], sm, AX_X, ALU.max).then_inc(S.dve_step, 1)
                    v.wait_ge(S.dve_step, w.to(S.dve_step))
                    if sinks is None:
                        v.tensor_scalar(st[:, 0:4], st[:, 0:4], -SCALE, None, ALU.mult).then_inc(S.maxed, 1)
                    else:
                        sk = sinks[:, 4 * u.g:4 * u.g + 4]
                        v.scalar_tensor_tensor(st[:, 0:4], st[:, 0:4], SCALE, sk, ALU.mult, ALU.max).then_inc(S.dve_step, 1)
                        v.wait_ge(S.dve_step, w.to(S.dve_step))
                        v.tensor_scalar(st[:, 0:4], st[:, 0:4], -1.0, None, ALU.mult).then_inc(S.dve_step, 1)
                        v.wait_ge(S.dve_step, w.to(S.dve_step))
                        v.tensor_tensor(st[:, 8:12], st[:, 0:4], sk, ALU.add).then_inc(S.maxed, 1)

                def output(i):
                    u = units[i]
                    st = b.stat[:, i % 4, :]
                    v.wait_ge(S.valued, w.to(S.valued))
                    if sinks is not None:
                        v.tensor_tensor(st[:, 4:8], st[:, 4:8], st[:, 8:12], ALU.add).then_inc(S.dve_step, 1)
                        v.wait_ge(S.dve_step, w.to(S.dve_step))
                    reciprocal(st[:, 12:16], st[:, 4:8])
                    finish(i, u, PS[:, 6 + i % 2, 0:SEQ].rearrange("p (r d) -> p r d", r=4),
                           st[:, 12:16])

                for i in range(len(units)):
                    stats(i)
                    if i >= 2:
                        output(i - 2)
                output(len(units) - 2)
                output(len(units) - 1)
                w.past(S.exped, 2)

            def mixer(l):
                norm()
                take_hT(l)
                v.memset(MB.z[:, :, 0:1], 0.0)
                v.memset(MB.z[:, :, SEQ + 1:SEQ + 2], 0.0)
                for t in range(TT):
                    v.wait_ge(S.act_took, w.to(S.act_took))
                    q = MB.q[:, t, :].rearrange("p (h d) -> p h d", d=DH)
                    rotate(q, q, t, MB.tmp).then_inc(S.dve_took, 1)
                    v.wait_ge(S.dve_took, w.to(S.dve_took))
                v.wait_ge(S.act_took, w.to(S.act_took))
                for t in range(TT):
                    k = MB.kv[:, t, 0:P].rearrange("p (h d) -> p h d", d=DH)
                    rotate(k, k, t, MB.tmp).then_inc(S.dve_took if t else S.dve_step, 1)
                    v.wait_ge(S.dve_took if t else S.dve_step, w.to(S.dve_took if t else S.dve_step))
                w.past(S.projected, 5)
                v.wait_ge(S.act_took, w.to(S.act_took, 2))
                for h in range(2):
                    v.wait_ge(S.projected, w.to(S.projected))
                    i = v.tensor_tensor(MB.z[:, 2 * h:2 * h + 2, 1:SEQ + 1],
                                        PS[:, 1 + h, :].rearrange("p (a b) -> p a b", a=2),
                                        MB.gate_c[:, 2 * h:2 * h + 2, :], ALU.mult)
                    i.then_inc(S.dve_took, 1)
                    v.wait_ge(S.dve_took, w.to(S.dve_took))
                for c in range(4):
                    v.tensor_scalar(MB.cv[:, c, :], MB.z[:, c, 0:SEQ], cw[:, l, 0, c:c + 1], None, ALU.mult).then_inc(S.dve_step, 1)
                    v.wait_ge(S.dve_step, w.to(S.dve_step))
                    for tap in (1, 2):
                        v.scalar_tensor_tensor(MB.cv[:, c, :], MB.z[:, c, tap:tap + SEQ],
                                               cw[:, l, tap, c:c + 1], MB.cv[:, c, :], ALU.mult, ALU.add).then_inc(S.dve_step, 1)
                        v.wait_ge(S.dve_step, w.to(S.dve_step))
                for h in range(2):
                    v.wait_ge(S.projected, w.to(S.projected))
                    i = v.tensor_tensor(MB.yc[:, 2 * h:2 * h + 2, :],
                                        PS[:, 3 + h, :].rearrange("p (a b) -> p a b", a=2),
                                        MB.cv[:, 2 * h:2 * h + 2, :], ALU.mult)
                    i.then_inc(S.dve_took, 1)
                    v.wait_ge(S.dve_took, w.to(S.dve_took))

                def finish(i, u, o, fac):
                    v.tensor_tensor(MB.ya[:, u.t, u.g * 256:(u.g + 1) * 256].rearrange("p (r d) -> p r d", r=4),
                                    o, fac.unsqueeze(2).to_broadcast([P, 4, DH]), ALU.mult).then_inc(S.o_taken, 1)
                    w.past(S.o_taken)

                w.past(S.turned_q, 3)
                attend(mixer_units(), MB, sink[:, l, :], finish)
                for root_sem, o, i, bank in ((S.conv_root, rstdc, rootc, 0), (S.ya_root, rstd, root, 4)):
                    v.wait_ge(root_sem, w.to(root_sem))
                    reciprocal(o, i)
                    v.wait_ge(S.acc_done, w.to(S.acc_done))
                    for t in range(TT):
                        v.scalar_tensor_tensor(x[:, t, :], psum_rows(bank)(t), o[:, t:t + 1], x[:, t, :],
                                               ALU.mult, ALU.add).then_inc(S.x_ready if bank and t else S.dve_step, 1)
                        v.wait_ge(S.x_ready if bank and t else S.dve_step, w.to(S.x_ready if bank and t else S.dve_step))

            def experts(s, f, passes, pos, gate):
                f.step = s.step
                iota = const("iota").unsqueeze(1).to_broadcast([P, 2, CAP])

                def tokens_of(e):
                    for t in range(TT):
                        last = v.tensor_tensor(EB.OH[:, t, :].rearrange("p (e s) -> p e s", e=2), iota,
                                               pos[:, t, bass.ds(e, 2)].unsqueeze(2).to_broadcast([P, 2, CAP]),
                                               ALU.is_equal)
                    last.then_inc(s.onehot, 1)
                    v.wait_ge(s.onehot, f.to(s.onehot))

                def take_x():
                    v.wait_ge(s.gathered, f.to(s.gathered, 2))
                    v.tensor_copy(EB.xeT[:, 4:8, :].rearrange("p a b -> p (a b)"), PS[:, 5, :]).then_inc(s.x_odd, 1)

                tokens_of(0)
                take_x()
                with v.Fori(0, passes) as p:
                    f.enter(p, {s.onehot: 1, s.gathered: 2, s.oh_turned: 1, s.silu_done: 2, s.down_done: 2,
                                s.y_turned: 2})
                    for t in range(TT):
                        last = v.tensor_tensor(EB.OHg[:, t, :].rearrange("p (e s) -> p e s", e=2),
                                               EB.OH[:, t, :].rearrange("p (e s) -> p e s", e=2),
                                               gate[:, t, bass.ds(2 * p, 2)].unsqueeze(2).to_broadcast([P, 2, CAP]),
                                               ALU.mult)
                    last.then_inc(s.onehot_g, 1)
                    v.wait_ge(s.oh_turned, f.to(s.oh_turned))
                    v.tensor_copy(EB.G, PS[:, 6, 0:SEQ]).then_inc(s.g_taken, 1)
                    tokens_of(2 * p + 2)
                    for j in range(2):
                        v.wait_ge(s.silu_done, f.to(s.silu_done))
                        v.tensor_tensor(EB.hE[:, j, :], PS[:, 4 + j, 256:512], EB.sE[:, j, :], ALU.mult) \
                            .then_inc(s.h_made, 1)
                    v.wait_ge(s.down_done, f.to(s.down_done, 2))
                    v.tensor_copy(EB.ysT[:, :, CAP:P], PS[:, 7, :].rearrange("p (k q) -> p k q", k=KT)) \
                        .then_inc(s.yT_odd, 1)
                    take_x()
                    v.wait_ge(s.y_turned, f.to(s.y_turned, 2))
                    v.tensor_copy(EB.y[:, 512:1024], PS[:, 7, :]).then_inc(s.y_hi, 1)
                    f.leave(passes)
                v.wait_ge(s.combined, f.to(s.combined, passes))
                for t in range(TT):
                    last = v.tensor_tensor(x[:, t, :], psum_rows(0)(t), x[:, t, :], ALU.add)
                return last

            def first_best(vals, n, key, best, hot, tie, top):
                v.tensor_reduce(top, vals, AX_X, ALU.max).then_inc(S.dve_step, 1)
                v.wait_ge(S.dve_step, w.to(S.dve_step))
                v.tensor_tensor(key, vals, top.unsqueeze(2).to_broadcast([P, TT, n]), ALU.is_equal).then_inc(S.dve_step, 1)
                v.wait_ge(S.dve_step, w.to(S.dve_step))
                v.tensor_tensor(key, key, tie.unsqueeze(1).to_broadcast([P, TT, n]), ALU.mult).then_inc(S.dve_step, 1)
                v.wait_ge(S.dve_step, w.to(S.dve_step))
                v.tensor_reduce(best, key, AX_X, ALU.max).then_inc(S.dve_step, 1)
                v.wait_ge(S.dve_step, w.to(S.dve_step))
                v.tensor_tensor(hot, key, best.unsqueeze(2).to_broadcast([P, TT, n]), ALU.is_equal).then_inc(S.dve_step, 1)
                v.wait_ge(S.dve_step, w.to(S.dve_step))

            def moe(l):
                norm(gain=gain_rows())
                take_hT(None)
                B = EB
                tie = const("tie")
                gm, gs, pg, m1, d, e2, m2, g1, g2, best = (B.s[:, i, :] for i in (0, 1, 2, 3, 4, 5, 6, 7, 8, 9))

                def over(ap, n):
                    return ap.unsqueeze(2).to_broadcast([P, TT, n])

                v.wait_ge(S.routed, w.to(S.routed))
                v.tensor_tensor(B.lg, PS[:, 4, 0:P].rearrange("p (t n) -> p t n", t=TT)[:, :, 0:NG + NE],
                                rbias[:, l, :].unsqueeze(1).to_broadcast([P, TT, NG + NE]), ALU.add).then_inc(S.dve_step, 1)
                v.wait_ge(S.dve_step, w.to(S.dve_step))
                gl, el = B.lg[:, :, 0:NG], B.lg[:, :, NG:]
                first_best(gl, NG, B.gk, best, B.gh, tie[:, 0:NG], gm)
                v.tensor_tensor(B.gd, gl, over(gm, NG), ALU.subtract).then_inc(S.gate_e, 1)
                v.tensor_scalar(B.gk, B.gh, 1.0, BIG, ALU.subtract, ALU.mult).then_inc(S.dve_step, 1)
                v.wait_ge(S.dve_step, w.to(S.dve_step))
                for t in range(TT):
                    last = v.tensor_tensor(B.el[:, t, :].rearrange("p (g e) -> p g e", g=NG),
                                           el[:, t, :].rearrange("p (g e) -> p g e", g=NG),
                                           B.gk[:, t, :].unsqueeze(2).to_broadcast([P, NG, NE // NG]), ALU.add)
                last.then_inc(S.dve_step, 1)
                v.wait_ge(S.dve_step, w.to(S.dve_step))
                first_best(B.el, NE, B.key, best, B.oh1, tie[:, NG:], m1)
                v.scalar_tensor_tensor(B.el3, B.oh1, -2 * BIG, B.el, ALU.mult, ALU.add).then_inc(S.dve_step, 1)
                v.wait_ge(S.dve_step, w.to(S.dve_step))
                first_best(B.el3, NE, B.key, best, B.oh2, tie[:, NG:], m2)
                v.tensor_tensor(B.mk, B.oh1, B.oh2, ALU.add).then_inc(S.marked, 1)
                v.wait_ge(S.marked, w.to(S.marked))
                v.tensor_tensor(d, m2, m1, ALU.subtract).then_inc(S.gate_e, 1)
                v.wait_ge(S.gate_exp, w.to(S.gate_exp))
                v.tensor_reduce(gs, B.ge, AX_X, ALU.add).then_inc(S.dve_step, 1)
                v.wait_ge(S.dve_step, w.to(S.dve_step))
                reciprocal(pg, gs)
                v.wait_ge(S.gate_exp, w.to(S.gate_exp))
                v.tensor_scalar(g1, e2, 1.0, None, ALU.add).then_inc(S.dve_step, 1)
                v.wait_ge(S.dve_step, w.to(S.dve_step))
                reciprocal(g2, g1)
                v.tensor_tensor(g1, g2, pg, ALU.mult).then_inc(S.dve_step, 1)
                v.wait_ge(S.dve_step, w.to(S.dve_step))
                v.tensor_tensor(g2, g1, e2, ALU.mult).then_inc(S.dve_step, 1)
                v.wait_ge(S.dve_step, w.to(S.dve_step))
                v.memset(B.gate[:, :, NE:NE + 2], 0.0).then_inc(S.dve_step, 1)
                v.wait_ge(S.dve_step, w.to(S.dve_step))
                v.memset(B.pos[:, :, NE:NE + 2], FAR).then_inc(S.dve_step, 1)
                v.wait_ge(S.dve_step, w.to(S.dve_step))
                v.tensor_tensor(B.oh1, B.oh1, over(g1, NE), ALU.mult).then_inc(S.dve_step, 1)
                v.wait_ge(S.dve_step, w.to(S.dve_step))
                v.tensor_tensor(B.oh2, B.oh2, over(g2, NE), ALU.mult).then_inc(S.dve_step, 1)
                v.wait_ge(S.dve_step, w.to(S.dve_step))
                v.tensor_tensor(B.gate[:, :, 0:NE], B.oh1, B.oh2, ALU.add).then_inc(S.dve_step, 1)
                v.wait_ge(S.dve_step, w.to(S.dve_step))
                v.tensor_scalar(B.key, B.mk, -FAR, FAR, ALU.mult, ALU.add).then_inc(S.dve_step, 1)
                v.wait_ge(S.dve_step, w.to(S.dve_step))
                v.wait_ge(S.ranked, w.to(S.ranked))
                v.tensor_tensor(B.pos[:, :, 0:NE], PS[:, 5, 0:2 * NE].rearrange("p (t n) -> p t n", t=TT),
                                B.key, ALU.add).then_inc(S.dve_step, 1)
                v.wait_ge(S.dve_step, w.to(S.dve_step))
                v.tensor_reduce(flag_f[:, :], PS[:, 5, 2 * NE:3 * NE], AX_X, ALU.max).then_inc(S.dve_step, 1)
                v.wait_ge(S.dve_step, w.to(S.dve_step))
                v.tensor_copy(flag[:, :], flag_f[:, :]).then_inc(S.flag_ready, 1)
                v.wait_ge(S.flag_ready, w.to(S.flag_ready))
                experts(M, w, PAIRS, B.pos, B.gate).then_inc(S.moe_added, 1)
                v.wait_ge(S.moe_added, w.to(S.moe_added))
                w.step = S.dve_step
                most = v.value_load(flag[0:1, 0:1], min_val=0, max_val=SEQ)
                with v.If(most > CAP):
                    f = Follow(OV[l].step)
                    v.memset(B.gatev[:, :, MORE * NE:], 0.0).then_inc(f.step, 1)
                    v.wait_ge(f.step, f.to(f.step))
                    v.memset(B.posv[:, :, MORE * NE:], FAR).then_inc(f.step, 1)
                    v.wait_ge(f.step, f.to(f.step))
                    for r in range(MORE):
                        v.tensor_copy(B.gatev[:, :, r * NE:(r + 1) * NE], B.gate[:, :, 0:NE]).then_inc(f.step, 1)
                        v.wait_ge(f.step, f.to(f.step))
                        v.tensor_scalar(B.posv[:, :, r * NE:(r + 1) * NE], B.pos[:, :, 0:NE],
                                        float(CAP * (r + 1)), None, ALU.subtract).then_inc(f.step, 1)
                        v.wait_ge(f.step, f.to(f.step))
                    experts(OV[l], f, MORE * PAIRS, B.posv, B.gatev).then_inc(f.step, 1)
                    v.wait_ge(f.step, f.to(f.step))
                v.tensor_copy(flag_f[:, :], rstd[:, 0:1]).then_inc(S.x_ready, 1)
                v.wait_ge(S.x_ready, w.to(S.x_ready))

            FG = {"ffn00": 2, "ffn01": 3, "ffn10": 4, "ffn11": 6}

            def ffn(gain):
                norm()
                take_hT(gain)

                def run(n):
                    for i in range(n):
                        v.wait_ge(S.ffn_silu, w.to(S.ffn_silu))
                        v.tensor_tensor(FB.hF[:, i % 4, :], PS[:, 4 + i % 4, SEQ:2 * SEQ], FB.sF[:, i % 2, :],
                                        ALU.mult).then_inc(S.ffn_h, 1)

                with v.Fori(0, 2) as p:
                    w.enter(p, {S.ffn_silu: 8})
                    run(8)
                    w.leave(2)
                run(6)
                w.past(S.acc_done)
                post(psum_rows(0), 0.5)

            def pool_mix():
                norm(permute=False)
                take_hT(7)
                scale = gain_rows()
                v.wait_ge(S.acc_done, w.to(S.acc_done))
                for t in range(TT):
                    v.tensor_tensor(pool_f[:, t, :], psum_rows(0)(t), scale, ALU.mult).then_inc(S.scaled, 1)
                    v.wait_ge(S.scaled, w.to(S.scaled))
                post(lambda t: pool_f[:, t, :], 1.0)

            def nsa():
                norm()
                take_hT(5)
                w.past(S.projected, 11)
                for gp in range(2):
                    for t in range(TT):
                        v.wait_ge(S.act_took, w.to(S.act_took))
                        q = NB.qn[:, t, gp * 512:(gp + 1) * 512].rearrange("p (h d) -> p h d", d=DH)
                        r = NB.qr[:, t, gp * 512:(gp + 1) * 512].rearrange("p (h d) -> p h d", d=DH)
                        v.tensor_copy(r[:, :, ROPE:DH], q[:, :, ROPE:DH])
                        rotate(q, r, t, NB.tmp).then_inc(S.dve_took, 1)
                        v.wait_ge(S.dve_took, w.to(S.dve_took))
                w.past(S.act_took, 2)
                for br in range(2):
                    for t in range(TT):
                        v.wait_ge(S.act_took, w.to(S.act_took))
                        k = NB.kv[br][:, t, 0:256].rearrange("p (h d) -> p h d", d=DH)
                        rotate(k, k, t, NB.tmp).then_inc(S.dve_took, 1)
                        v.wait_ge(S.dve_took, w.to(S.dve_took))
                v.memset(NB.Vbd, 0.0)
                v.memset(NB.P32, 0.0).then_inc(S.dve_step, 1)
                v.wait_ge(S.dve_step, w.to(S.dve_step))
                w.past(S.turned_q, 4)
                for t in range(TT):
                    for gp in range(2):
                        v.wait_ge(S.turned_q, w.to(S.turned_q))
                        v.tensor_copy(NB.qrT[:, 4 * gp:4 * gp + 4, t * P:(t + 1) * P],
                                      PS[:, 4 + 2 * t + gp, :].rearrange("p (m q) -> p m q", m=4)) \
                            .then_inc(S.q_turned_dve, 1)
                v.wait_ge(S.turned_q, w.to(S.turned_q))
                for g in range(4):
                    for r in range(2):
                        for h in range(2):
                            last = v.tensor_copy(*z_view(0, g, r, h))
                last.then_inc(S.dve_step, 1)
                v.wait_ge(S.dve_step, w.to(S.dve_step))
                for s in range(2):
                    if s:
                        v.wait_ge(S.z_built, w.to(S.z_built))
                    v.tensor_tensor(NB.Z[s], NB.Z[s], cpos[:, s, :].unsqueeze(2).to_broadcast([P, 16, 60]),
                                    ALU.add).then_inc(S.z_pos, 1)
                w.past(S.turned_q, 3)
                v.wait_ge(S.compressed, w.to(S.compressed))
                v.tensor_copy(NB.KC, PS[:, 6, 0:60])
                for r in range(4):
                    last = v.tensor_copy(NB.Vbd[32 * r:32 * r + NCMP, :, r * DH:(r + 1) * DH],
                                         PS[0:NCMP, 7, 0:256].rearrange("p (g d) -> p g d", g=4))
                last.then_inc(S.kc_ready, 1)
                mask, some = const("cmp_mask"), const("cmp_any")
                for t in range(TT):
                    v.wait_ge(S.cscored, w.to(S.cscored))
                    for g in range(4):
                        last = v.tensor_tensor(NB.Sc[t][:, 4 * g:4 * g + 4, :],
                                               PS[:, 2 * t + g % 2, 64 * g:64 * g + 64]
                                               .rearrange("p (h n) -> p h n", h=4)[:, :, 0:NCMP],
                                               mask[:, t * NCMP:(t + 1) * NCMP].unsqueeze(1)
                                               .to_broadcast([P, 4, NCMP]), ALU.add)
                    last.then_inc(S.dve_step, 1)
                    v.wait_ge(S.dve_step, w.to(S.dve_step))
                    v.tensor_reduce(NB.cs[:, t, :], NB.Sc[t], AX_X, ALU.max).then_inc(S.dve_step, 1)
                    v.wait_ge(S.dve_step, w.to(S.dve_step))
                    v.tensor_tensor(NB.Sc[t], NB.Sc[t], NB.cs[:, t, :].unsqueeze(2)
                                    .to_broadcast([P, 16, NCMP]), ALU.subtract).then_inc(S.csub, 1)
                    v.wait_ge(S.csub, w.to(S.csub))
                v.wait_ge(S.act_took, w.to(S.act_took))
                for t in range(TT):
                    v.wait_ge(S.cexp, w.to(S.cexp))
                    cs = NB.cs[:, 2 + 2 * t, :]
                    fac = NB.cs[:, 3 + 2 * t, :]
                    v.tensor_reduce(cs, NB.Sc[t], AX_X, ALU.add).then_inc(S.dve_step, 1)
                    v.wait_ge(S.dve_step, w.to(S.dve_step))
                    reciprocal(fac, cs)
                    v.scalar_tensor_tensor(fac, fac, some[:, t:t + 1], NB.gts[:, t, 0:16], ALU.mult, ALU.mult).then_inc(S.dve_step, 1)
                    v.wait_ge(S.dve_step, w.to(S.dve_step))
                    v.tensor_tensor(NB.P32[:, t, :, 0:NCMP], NB.Sc[t], fac.unsqueeze(2)
                                    .to_broadcast([P, 16, NCMP]), ALU.mult).then_inc(S.p_ready, 1)
                v.wait_ge(S.o_first, w.to(S.o_first, 2))
                units = nsa_units()

                def finish(i, u, o, fac):
                    lo = (1 + u.br) * 16 + 4 * u.g
                    v.tensor_tensor(fac, fac, NB.gts[:, u.t, lo:lo + 4], ALU.mult).then_inc(S.dve_step, 1)
                    v.wait_ge(S.dve_step, w.to(S.dve_step))
                    tmp = NB.tmp.rearrange("p (r d) -> p r d", r=4)
                    v.tensor_tensor(tmp, o, fac.unsqueeze(2).to_broadcast([P, 4, DH]), ALU.mult).then_inc(S.o_taken, 1)
                    v.wait_ge(S.o_taken, w.to(S.o_taken))
                    dst = hp[:, u.t, u.g * 256:(u.g + 1) * 256]
                    add = v.tensor_tensor(dst, dst, NB.tmp, ALU.add)
                    if i >= len(units) - 2:
                        add.then_inc(S.h_ready, 1)
                    else:
                        add.then_inc(S.dve_step, 1)
                        v.wait_ge(S.dve_step, w.to(S.dve_step))

                attend(units, NB, None, finish)
                take_hT(None)
                w.past(S.acc_done)
                post(psum_rows(4), 1.0)

            v.memset(epsb[:, :], EPS).then_inc(S.set_up, 1)
            v.memset(zeros, 0.0).then_inc(S.set_up, 1)
            v.wait_ge(S.x_loaded, w.to(S.x_loaded, 16))
            v.wait_ge(S.const_loaded, w.to(S.const_loaded, 16))
            v.wait_ge(S.param_loaded, PARAMS)
            for name in stages:
                if name[:3] == "mix":
                    mixer(int(name[3]))
                elif name[:3] == "moe":
                    moe(int(name[3]))
                elif name == "final":
                    gain = gain_rows()
                    v.wait_ge(S.root_ready, w.to(S.root_ready))
                    reciprocal(rstd, root)
                    for t in range(TT):
                        v.scalar_tensor_tensor(x[:, t, :], x[:, t, :], rstd[:, t:t + 1], gain,
                                               ALU.mult, ALU.mult).then_inc(S.x_ready if t else S.dve_step, 1)
                        v.wait_ge(S.x_ready if t else S.dve_step, w.to(S.x_ready if t else S.dve_step))
                elif name[:3] == "ffn":
                    ffn(FG[name])
                elif name == "pool":
                    pool_mix()
                elif name == "nsa":
                    nsa()


NAMES = ["x", "norm_mix", "w_in", "attn_sink", "conv_w", "norm_attn_out", "norm_conv_out", "w_out", "norm_ffn",
         "w_router_group", "b_router_group", "w_router_expert", "b_router_expert", "w_expert_gate", "w_expert_up",
         "w_expert_down", "norm_final", "norm_gains_2", "ffn_w_gate_2", "ffn_w_up_2", "ffn_w_down_2", "pool_w_2",
         "pool_b_2", "pool_scale_2", "nsa_w_in_2", "nsa_cmp_pos_k_2", "nsa_cmp_pos_v_2", "nsa_cmp_wk1_2",
         "nsa_cmp_wk2_2", "nsa_cmp_wv1_2", "nsa_cmp_wv2_2", "nsa_w_o_2"]


def kernel(**inputs):
    import concourse.bacc as bacc
    from concourse.bass_utils import run_bass_kernel_spmd

    nc = bacc.Bacc("TRN2", target_bir_lowering=False, num_devices=1)
    table, means = constants()
    arrays = {name: np.ascontiguousarray(inputs[name]) for name in NAMES}
    arrays["consts"], arrays["means"] = table, means
    aps = {}
    feed = {}
    for name, v in arrays.items():
        feed[f"in_{name}"] = v
        aps[name] = nc.dram_tensor(f"in_{name}", v.shape, mybir.dt.from_np(v.dtype), kind="ExternalInput").ap()
    out = nc.dram_tensor("out_x", (1, SEQ, D), F32, kind="ExternalOutput").ap()
    build(nc, aps, out, STAGES)
    r = run_bass_kernel_spmd(nc, [feed], core_ids=[0])
    return r.results[0]["out_x"]
```

```python
from contextlib import ExitStack

import numpy as np

import concourse.bass as bass
from concourse import mybir

F32 = mybir.dt.float32
F32R = mybir.dt.float32r
I32 = mybir.dt.int32
ALU = mybir.AluOpType
ACT = mybir.ActivationFunctionType
AX_X = mybir.AxisListType.X

P = 128
SEQ, D = 256, 1024
TT = SEQ // P
KT = D // P
EPS = 1e-6
DH = 64
SCALE = DH ** -0.5
BIG = 1e30
NE, NG = 32, 4
DE = 512
CAP = 64
PAIRS = NE // 2
MORE = SEQ // CAP - 1
FAR = 1e4
FF = 2816
NCMP = 15
ROPE = 16
THETA = 500000.0
RING = 6
HALF = 2048
SPLIT = 3
UNITS = 2 * RING
WORK = 15904
STAGES = ["mix0", "moe0", "mix1", "moe1", "final", "ffn00", "pool", "ffn01", "ffn10", "nsa", "ffn11"]

LOADS = {"mix": 7, "moe": RING * PAIRS, "fin": 0, "ffn": 18, "poo": 1, "nsa": 10}

CONSTS = {}
_at = 0
for _n, _w in (("ident", P), ("upper", P), ("ones", P), ("fold", CAP), ("iota", CAP), ("tie", NG + NE), ("rope_c", TT * ROPE),
               ("rope_s", TT * ROPE), ("band", TT * SEQ), ("causal", SEQ), ("cmp_mask", TT * NCMP), ("cmp_any", TT)):
    CONSTS[_n] = (_at, _at + _w)
    _at += _w
N_CONSTS = _at


def constants():
    c = np.zeros((P, N_CONSTS), np.float32)

    def put(name, a):
        lo, hi = CONSTS[name]
        c[:, lo:hi] = np.asarray(a, np.float32).reshape(P, -1)

    i = np.arange(P)
    tok = i[:, None] + P * np.arange(TT)[None, :]
    put("ident", np.eye(P))
    put("upper", i[:, None] < i[None, :])
    put("ones", np.ones((P, P)))
    put("fold", i[:, None] % CAP == np.arange(CAP)[None, :])
    put("iota", np.broadcast_to(np.arange(CAP), (P, CAP)))
    put("tie", np.broadcast_to(np.concatenate([np.arange(NG, 0, -1), np.arange(NE, 0, -1)]), (P, NG + NE)))
    inv = np.float32(THETA) ** (-np.arange(0, ROPE, 2, dtype=np.float32) / np.float32(ROPE))
    ang = tok.astype(np.float32)[:, :, None] * inv.astype(np.float32)
    cos, sin = np.cos(ang), np.sin(ang)
    put("rope_c", np.concatenate([cos, cos], -1))
    put("rope_s", np.concatenate([-sin, sin], -1))
    keys = np.arange(SEQ)
    put("band", np.where(np.abs(keys[None, None, :] - tok[:, :, None]) <= 128, 0.0, -BIG))
    put("causal", np.where(keys[None, :] <= P + i[:, None], 0.0, -BIG))
    ends = np.arange(NCMP) * 16 + 31
    ok = ends[None, None, :] <= tok[:, :, None]
    put("cmp_mask", np.where(ok, 0.0, -BIG))
    put("cmp_any", ok.any(-1))
    q = np.arange(SEQ)
    means = np.zeros((SEQ, 4, SEQ), np.float32)
    for n, w in enumerate((2, 4, 8, 16)):
        gap = q[None, :] - q[:, None]
        means[:, n, :] = ((gap >= 0) & (gap < w)) / np.minimum(q + 1, w)[None, :] - (gap == 0)
    return c, means.astype(np.float32)


class Fields:
    pass


class Unit:

    def __init__(self, t, g, half, gp, tile, br, nk, qT, kT, v, mask):
        self.t, self.g, self.half, self.gp, self.tile, self.br, self.nk = t, g, half, gp, tile, br, nk
        self.qT, self.kT, self.v, self.mask = qT, kT, v, mask


class Follow:

    def __init__(self, step=None):
        self.step, self.n, self.p, self.per = step, {}, None, {}

    def past(self, sem, k=1):
        self.n[sem.name] = (sem, self.n.get(sem.name, (sem, 0))[1] + k)

    def to(self, sem, k=1):
        self.past(sem, k)
        v = self.n[sem.name][1]
        if self.p is not None:
            v = self.p * self.per[sem.name] + (v - self.per[sem.name] * self.first)
        return v

    def after(self, sem, k):
        return self.n[sem.name][1] + k

    def enter(self, p, per, first=0):
        self.p, self.per, self.first = p, {s.name: k for s, k in per.items()}, first
        self.was = {k: v for k, v in self.n.items()}

    def leave(self, passes):
        got = {k: v[1] - self.was.get(k, (0, 0))[1] for k, v in self.n.items()}
        got = {k: v for k, v in got.items() if v}
        want = {k: v for k, v in self.per.items() if v}
        assert got == want, (got, want)
        for k, v in got.items():
            self.n[k] = (self.n[k][0], self.n[k][1] + v * (passes - 1))
        self.p = None


def build(nc, a, out, stages):
    ctx = ExitStack()
    with ctx:
        def sb(name, shape, dt=F32):
            return ctx.enter_context(nc.sbuf_tensor(name, shape, dt))

        def sem(name):
            return ctx.enter_context(nc.semaphore(name))

        PS = ctx.enter_context(nc.psum_tensor("PS", [P, 8, 512], F32))

        ring = sb("ring", [P, RING, 4096])
        x = sb("x", [P, TT, D])
        hp = sb("hp", [P, TT, D])
        hT = sb("hT", [P, KT, SEQ])
        hT_at = nc.sbuf_base - 4 * KT * SEQ
        gB = sb("gB", [P, 2, D])
        cst = sb("cst", [P, N_CONSTS])
        work = sb("work", [P, WORK])
        work_at = nc.sbuf_base - 4 * WORK
        split = nc.alloc_sbuf_tensor_at("split", [P, SPLIT, 2, HALF], F32R, offset=work_at)
        S_COLS = SPLIT * 2 * HALF
        hid = nc.alloc_sbuf_tensor_at("hid", [P, 4, 2 * CAP], F32R, offset=work_at + 4 * S_COLS)
        H_COLS = 4 * 2 * CAP
        xs = nc.alloc_sbuf_tensor_at("xs", [P, 2, KT, 2 * CAP], F32R, offset=hT_at)
        gT = sb("gT", [P, 9, KT])
        cw = sb("cw", [P, 2, 3, 4])
        gaT = sb("gaT", [P, 2, 4])
        gcT = sb("gcT", [P, 2, 4])
        wr = sb("wr", [P, 2, KT, NG + NE])
        rbias = sb("rbias", [P, 2, NG + NE])
        sink = sb("sink", [P, 2, 8])
        rows1 = sb("rows1", [33, D])
        pbias, zeros = rows1[0:1, :], rows1[32:33, 0:512]
        w2k = sb("w2k", [P, 2, 2 * DH])
        w2v = sb("w2v", [P, 2, DH])
        cpos = sb("cpos", [P, 2, 16])
        small = sb("small", [P, 64])
        epsb = sb("epsb", [P, 1])
        flag_f = sb("flag_f", [P, 1])
        flag = sb("flag", [P, 1], I32)

        def const(name, parts=P):
            lo, hi = CONSTS[name]
            return cst[0:parts, lo:hi]

        ident, upper, ones = const("ident"), const("upper"), const("ones")
        ss, root, rstd = small[:, 0:2], small[:, 2:4], small[:, 4:6]
        ssc, rootc, rstdc = small[:, 6:8], small[:, 8:10], small[:, 10:12]

        class Carve:
            def __init__(self, start=0):
                self.at = start

            def __call__(self, *shape):
                n = int(np.prod(shape))
                v = work[:, self.at:self.at + n]
                self.at += n
                assert self.at <= WORK, self.at
                if len(shape) == 2:
                    v = v.rearrange("p (a b) -> p a b", a=shape[0])
                if len(shape) == 3:
                    v = v.rearrange("p (a b c) -> p a b c", a=shape[0], b=shape[1])
                return v

        S = Fields()
        S.set_up = sem("set_up")
        S.const_loaded = sem("const_loaded")
        S.x_loaded = sem("x_loaded")
        S.param_loaded = sem("param_loaded")
        S.means_loaded = sem("means_loaded")
        S.x_stored = sem("x_stored")
        S.dve_step = sem("dve_step")
        S.act_step = sem("act_step")
        S.x_ready = sem("x_ready")
        S.root_ready = sem("root_ready")
        S.h_ready = sem("h_ready")
        S.hT_psum = sem("hT_psum")
        S.hT_even = sem("hT_even")
        S.hT_odd = sem("hT_odd")
        S.projected = sem("projected")
        S.act_took = sem("act_took")
        S.dve_took = sem("dve_took")
        S.turned_q = sem("turned_q")
        S.q_turned_act = sem("q_turned_act")
        S.q_turned_dve = sem("q_turned_dve")
        S.scored = sem("scored")
        S.masked = sem("masked")
        S.maxed = sem("maxed")
        S.exped = sem("exped")
        S.turned = sem("turned")
        S.turned_taken = sem("turned_taken")
        S.valued = sem("valued")
        S.o_taken = sem("o_taken")
        S.conv_gain = sem("conv_gain")
        S.conv_ss = sem("conv_ss")
        S.conv_root = sem("conv_root")
        S.ya_root = sem("ya_root")
        S.ya_psum = sem("ya_psum")
        S.yaT_ready = sem("yaT_ready")
        S.half_done = sem("half_done")
        S.acc_done = sem("acc_done")
        S.routed = sem("routed")
        S.gate_e = sem("gate_e")
        S.gate_exp = sem("gate_exp")
        S.marked = sem("marked")
        S.ranked = sem("ranked")
        S.flag_ready = sem("flag_ready")
        S.moe_added = sem("moe_added")
        S.ffn_gu = sem("ffn_gu")
        S.ffn_silu = sem("ffn_silu")
        S.ffn_h = sem("ffn_h")
        S.ffn_down = sem("ffn_down")
        S.scaled = sem("scaled")
        S.z_built = sem("z_built")
        S.z_pos = sem("z_pos")
        S.hidden = sem("hidden")
        S.hc_ready = sem("hc_ready")
        S.compressed = sem("compressed")
        S.kc_ready = sem("kc_ready")
        S.cscored = sem("cscored")
        S.csub = sem("csub")
        S.cexp = sem("cexp")
        S.p_ready = sem("p_ready")
        S.p_turned = sem("p_turned")
        S.pT_ready = sem("pT_ready")
        S.cvalued = sem("cvalued")
        S.o_first = sem("o_first")
        S.gB_loaded = [sem(f"gB_loaded{i}") for i in range(2)]
        S.loaded = [sem(f"ring_loaded{i}") for i in range(RING)]

        def expert_sems(tag, loaded=None):
            s = Fields()
            s.high_made = sem(f"high_made_{tag}")
            s.low_made = sem(f"low_made_{tag}")
            s.half_used = sem(f"half_used_{tag}")
            s.gathered = sem(f"gathered_{tag}")
            s.x_high = sem(f"x_high_{tag}")
            s.x_made = sem(f"x_made_{tag}")
            s.gu_taken = sem(f"gu_taken_{tag}")
            s.gu_turned = sem(f"gu_turned_{tag}")
            s.silu_done = sem(f"silu_done_{tag}")
            s.h_made = sem(f"h_made_{tag}")
            s.y_taken = sem(f"y_taken_{tag}")
            s.oh_turned = sem(f"oh_turned_{tag}")
            s.g_taken = sem(f"g_taken_{tag}")
            s.combined = sem(f"combined_{tag}")
            s.onehot = sem(f"onehot_{tag}")
            s.onehot_g = sem(f"onehot_g_{tag}")
            s.step = sem(f"step_{tag}")
            s.loaded = loaded or [sem(f"ring_loaded{i}_{tag}") for i in range(RING)]
            return s

        M = expert_sems("moe", S.loaded)
        OV = {l: expert_sems(f"more{l}") for l in range(2) if f"moe{l}" in stages}

        def mixer_views():
            c = Carve()
            b = Fields()
            b.q, b.kv = c(TT, 512), c(TT, 256)
            b.v = b.kv[:, :, P:256]
            b.qT, b.kT = c(4, SEQ), c(1, SEQ)
            b.ya, b.yc = c(TT, 512), c(4, SEQ)
            b.tmp = c(256)
            b.stat = c(4, 16)
            b.z = c(4, SEQ + 2)
            b.P = [c(4, SEQ) for _ in range(2)]
            b.Sm = [c(4, SEQ) for _ in range(2)]
            b.PT = [c(2, 4, P) for _ in range(2)]
            b.sq = hp[:, 0, :].rearrange("p (a b) -> p a b", a=4)
            b.gate_c = hp[:, 1, :].rearrange("p (a b) -> p a b", a=4)
            b.cv = b.P[0]
            b.yaT = b.Sm[0]
            b.junk = b.Sm[1]
            return b

        MB = mixer_views()

        def moe_views():
            c = Carve(S_COLS + H_COLS)
            b = Fields()
            top = c.at
            b.gu = c(2, DE)
            b.sE = c(4, CAP)
            b.G = c(2, SEQ)
            b.OH = c(TT, P)
            b.OHg = c(TT, 2, P)
            b.pos = c(TT, NE + 2)
            b.gate = c(TT, NE + 2)
            b.posv = c(TT, MORE * NE + 2)
            b.gatev = c(TT, MORE * NE + 2)
            c.at = top
            b.lg = c(TT, NG + NE)
            b.gd, b.ge, b.gh, b.gk = c(TT, NG), c(TT, NG), c(TT, NG), c(TT, NG)
            b.el, b.el3, b.key = c(TT, NE), c(TT, NE), c(TT, NE)
            b.oh1, b.oh2, b.mk = c(TT, NE), c(TT, NE), c(TT, NE)
            b.s = c(12, TT)
            return b

        EB = moe_views()

        def ffn_views():
            c = Carve()
            b = Fields()
            b.sF, b.hF = c(2, SEQ), c(4, SEQ)
            return b

        FB = ffn_views()
        pool_means = work[:, 0:2048].rearrange("p (a b c) -> p a b c", a=TT, b=4)
        pool_f = work[:, 2048:4096].rearrange("p (a b) -> p a b", a=TT)

        def nsa_views():
            c = Carve()
            b = Fields()
            b.qnT, b.qrT = c(8, SEQ), c(8, SEQ)
            b.kT = [c(2, SEQ) for _ in range(2)]
            b.kv = [c(TT, 512) for _ in range(2)]
            b.v = [kv[:, :, 256:512] for kv in b.kv]
            b.gts = c(TT, 48)
            b.tmp = c(256)
            b.stat = c(4, 16)
            b.KC = c(60)
            b.Vbd = c(4, 256)
            b.hc = c(2, 120)
            b.Sc = [c(16, NCMP) for _ in range(2)]
            b.cs = c(6, 16)
            top = c.at
            b.qn, b.qr = c(TT, D), c(TT, D)
            b.kvc = c(TT, 512)
            c.at = top
            b.P = [c(4, SEQ) for _ in range(2)]
            b.Sm = [c(4, SEQ) for _ in range(2)]
            b.PT = [c(2, 4, P) for _ in range(2)]
            b.PcT = b.PT[0]
            b.P32 = b.PT[1].rearrange("p a b c -> p (a b c)").rearrange("p (t h n) -> p t h n", t=TT, h=16)
            b.Z = [hp[:, s, 0:960].rearrange("p (a b) -> p a b", a=16) for s in range(2)]
            return b

        NB = nsa_views()

        def z_view(s, g, r, h):
            src = PS[DH * (g % 2):DH * (g % 2 + 1), s, (g // 2) * SEQ:(g // 2 + 1) * SEQ]
            src = src.rearrange("p (n j r) -> p r j n", j=8, r=2)[:, r, :, h:h + NCMP]
            return NB.Z[s][DH * r:DH * (r + 1), 8 * h:8 * h + 8, g * NCMP:(g + 1) * NCMP], src

        def mixer_units():
            return [Unit(t=t, g=g, half=g, gp=0, tile=0, br=0, nk=2, qT=MB.qT, kT=MB.kT, v=MB.v,
                                    mask=const("band")[:, t * SEQ:(t + 1) * SEQ])
                    for t in range(TT) for g in range(2)]

        def nsa_units():
            return [Unit(t=t, g=g, half=g % 2, gp=g // 2, tile=4 * (g // 2), br=br, nk=t + 1,
                                    qT=NB.qrT, kT=NB.kT[br], v=NB.v[br],
                                    mask=const("causal")[:, P * (1 - t):SEQ])
                    for br in range(2) for t in range(TT) for g in range(4)]

        def first_slot(stage):
            return sum(LOADS[name[:3]] for name in stages[:stages.index(stage)])

        block = ctx.enter_context(nc.Block())

        @block.sync
        def _(sp):
            w = Follow()
            free = []
            n = [0]

            def load(dst, src, used, k):
                r = n[0] % RING
                if n[0] >= RING:
                    s, m = free[n[0] - RING]
                    sp.wait_ge(s, w.to(s, m))
                sp.dma_start(dst(r), src).then_inc(S.loaded[r], 16)
                free.append((used, k))
                n[0] += 1

            def cols(r_, k, width):
                return lambda r: ring[:, r, 0:k * width].rearrange("p (k n) -> p k n", k=k)

            def wide(src, lo, hi, used, k):
                load(cols(0, KT, hi - lo), src[:, lo:hi].rearrange("(p k) n -> p k n", k=KT), used, k)

            def rows(src, lo, hi, used, k):
                m = (hi - lo) // P
                load(cols(0, m, D), src[lo:hi, :].rearrange("(k p) n -> p k n", p=P), used, k)

            def expert_src(l, e, which):
                if which == "down":
                    return a["w_expert_down"][l, e].rearrange("(f p) n -> p f n", p=P)
                return a["w_expert_" + which][l, e].rearrange("(p k) n -> p k n", k=KT)

            PAIR = (("gate", 0), ("up", 0), ("gate", 1), ("down", 0), ("up", 1), ("down", 1))

            def pair_loads(l, s, e0, wait, ff):
                for j, (which, e) in enumerate(PAIR):
                    r = (n[0] + j) % RING
                    if wait:
                        sp.wait_ge(s.low_made, ff.to(s.low_made, 2))
                    k = 4 if which == "down" else KT
                    dst = ring[:, r, :].rearrange("p (k n) -> p k n", k=k)
                    sp.dma_start(dst, expert_src(l, e0 + e, which)).then_inc(s.loaded[r], 16)

            def moe_loads(l):
                for which, e in PAIR:
                    load(cols(0, 4 if which == "down" else KT, D if which == "down" else DE),
                         expert_src(l, e, which), M.low_made, 2)
                per = {M.low_made: UNITS}
                with sp.Fori(1, PAIRS) as p:
                    w.enter(p, per, first=1)
                    pair_loads(l, M, 2 * p, True, w)
                    w.leave(PAIRS - 1)
                for which, e in PAIR:
                    free.append((M.low_made, 2))
                n[0] += RING

            def more_loads(l):
                s = OV[l]
                sp.wait_ge(S.flag_ready, w.to(S.flag_ready))
                most = sp.value_load(flag[0:1, 0:1], min_val=0, max_val=SEQ)
                with sp.If(most > CAP):
                    sp.wait_ge(M.low_made, w.after(M.low_made, UNITS))
                    v = Follow()
                    pair_loads(l, s, 0, False, v)
                    with sp.Fori(1, MORE * PAIRS) as q:
                        v.enter(q, {s.low_made: UNITS}, first=1)
                        pair_loads(l, s, (q % PAIRS) * 2, True, v)
                        v.leave(MORE * PAIRS - 1)
                    sp.wait_ge(s.low_made, v.to(s.low_made, UNITS))

            def mixer_loads(l):
                wi = a["w_in"][l]
                for lo, hi, k in ((0, 512, 2), (512, 768, 1), (1280, 1792, 2), (1792, 2304, 2), (768, 1280, 2)):
                    wide(wi, lo, hi, S.projected, k)
                rows(a["w_out"][l], 512, 1024, S.acc_done, 1)
                rows(a["w_out"][l], 0, 512, S.acc_done, 1)

            def chunk_loads(i, j, f, width, used, final, dyn=False):
                wg, wu, wd = a["ffn_w_gate_2"][i, j], a["ffn_w_up_2"][i, j], a["ffn_w_down_2"][i, j]
                m = width // P
                wide(wg, f, f + width, S.ffn_gu, m)
                wide(wu, f, f + width, S.ffn_gu, 0)
                rows(wd, f, f + width, S.acc_done if final else S.ffn_down, 1)

            def ffn_loads(i, j):
                for f in range(0, FF, 512):
                    width = min(512, FF - f)
                    chunk_loads(i, j, f, width, None, f + width == FF)

            def nsa_loads():
                wi = a["nsa_w_in_2"][0]
                for lo in range(0, 2560, 512):
                    wide(wi, lo, lo + 512, S.projected, 2)
                wide(wi, 2560, 2608, S.projected, 1)
                for name in ("nsa_cmp_wk1_2", "nsa_cmp_wv1_2"):
                    load(lambda r: ring[:, r, :].rearrange("p (k n) -> p k n", k=16),
                         a[name][0].rearrange("(j p) n -> p j n", p=P), S.hidden, 1)
                rows(a["nsa_w_o_2"][0], 0, 512, S.half_done, 1)
                rows(a["nsa_w_o_2"][0], 512, 1024, S.acc_done, 1)

            sp.dma_start(x[:, :, :], a["x"][0].rearrange("(t p) d -> p t d", p=P)).then_inc(S.x_loaded, 16)
            sp.dma_start(cst[:, :], a["consts"]).then_inc(S.const_loaded, 16)
            for name in stages:
                if name[:3] == "mix":
                    mixer_loads(int(name[3]))
                elif name[:3] == "moe":
                    moe_loads(int(name[3]))
                    more_loads(int(name[3]))
                elif name[:3] == "ffn":
                    ffn_loads(int(name[3]), int(name[4]))
                elif name == "pool":
                    load(lambda r: ring[:, r, 0:2048].rearrange("p (k n) -> p k n", k=8),
                         a["pool_w_2"][0].rearrange("g (c p) e -> p (g c) e", p=P), S.acc_done, 1)
                elif name == "nsa":
                    nsa_loads()
            sp.wait_ge(S.x_ready, len(stages))
            sp.dma_start(out[0].rearrange("(t p) d -> p t d", p=P), x[:, :, :]).then_inc(S.x_stored, 16)
            sp.wait_ge(S.x_stored, 16)

        gains = []

        def gain_list():
            g2 = a["norm_gains_2"]
            src = {"moe0": [a["norm_ffn"][0]], "moe1": [a["norm_ffn"][1]], "final": [a["norm_final"]],
                   "ffn00": [g2[0, 1]], "pool": [a["pool_scale_2"][0], g2[0, 3]], "ffn01": [g2[0, 5]],
                   "ffn10": [g2[1, 1]], "nsa": [g2[1, 3]], "ffn11": [g2[1, 5]]}
            return [(i, s) for i, name in enumerate(stages) for s in src.get(name, [])]

        gains = gain_list()
        N_PARAMS = [0]

        @block.gpsimd
        def _(pool):
            w = Follow()

            def par(dst, src):
                pool.dma_start(dst, src).then_inc(S.param_loaded, 16)
                N_PARAMS[0] += 16

            with nc.allow_non_contiguous_dma(reason="small parameters, transposed"):
                g2 = a["norm_gains_2"]
                for n, src in enumerate((a["norm_mix"][0], a["norm_mix"][1], g2[0, 0], g2[0, 4], g2[1, 0],
                                         g2[1, 2], g2[1, 4])):
                    par(gT[:, n, :], src.rearrange("(p k) -> p k", k=KT))
                par(gT[:, 7, :], g2[0, 2].rearrange("(k p) -> p k", p=P))
                for l in range(2):
                    for t in range(3):
                        par(cw[:, l, t, :], a["conv_w"][l, t].rearrange("(c p) -> p c", p=P))
                    par(gaT[:, l, :], a["norm_attn_out"][l].rearrange("(c p) -> p c", p=P))
                    par(gcT[:, l, :], a["norm_conv_out"][l].rearrange("(c p) -> p c", p=P))
                    par(wr[:, l, :, 0:NG], a["w_router_group"][l].rearrange("(p k) n -> p k n", k=KT))
                    par(wr[:, l, :, NG:], a["w_router_expert"][l].rearrange("(p k) n -> p k n", k=KT))
                    par(rbias[:, l, 0:NG], a["b_router_group"][l].partition_broadcast(P))
                    par(rbias[:, l, NG:], a["b_router_expert"][l].partition_broadcast(P))
                    par(sink[:, l, :], a["attn_sink"][l].partition_broadcast(P))
                par(pbias[:, :], a["pool_b_2"].rearrange("o g e -> o (g e)"))
                for h in range(2):
                    par(w2k[:, :, h * DH:(h + 1) * DH], a["nsa_cmp_wk2_2"][0].rearrange("(c p) d -> p c d", p=P))
                par(w2v[:, :, :], a["nsa_cmp_wv2_2"][0].rearrange("(c p) d -> p c d", p=P))
                for s, name in enumerate(("nsa_cmp_pos_k_2", "nsa_cmp_pos_v_2")):
                    for r in range(2):
                        par(cpos[r * DH:(r + 1) * DH, s, :],
                            a[name][0].rearrange("(j r) d -> r d j", r=2)[r])
            for i, (st, src) in enumerate(gains):
                if i >= 2:
                    pool.wait_ge(S.x_ready, gains[i - 2][0] + 1)
                pool.dma_start(gB[:, i % 2, :], src.partition_broadcast(P)).then_inc(S.gB_loaded[i % 2], 16)
                if i + 1 < len(gains) and st < stages.index("pool") <= gains[i + 1][0] if "pool" in stages else False:
                    pool.wait_ge(S.x_ready, stages.index("pool"))
                    pool.dma_start(pool_means, a["means"].rearrange("(t p) w q -> p t w q", p=P)) \
                        .then_inc(S.means_loaded, 16)

        PARAMS = N_PARAMS[0]

        @block.tensor
        def _(pe):
            w = Follow()
            n = [0]

            def slot():
                r = n[0] % RING
                n[0] += 1
                pe.wait_ge(S.loaded[r], w.to(S.loaded[r], 16))
                return r

            def view(r, k, width):
                return ring[:, r, 0:k * width].rearrange("p (k n) -> p k n", k=k)

            def transpose_h():
                for b in range(4):
                    for k in (2 * b, 2 * b + 1):
                        for t in range(TT):
                            if k == 0:
                                pe.wait_ge(S.h_ready, w.to(S.h_ready))
                            last = pe.transpose(PS[:, b, (k % 2) * SEQ + t * P:(k % 2) * SEQ + (t + 1) * P],
                                                hp[:, t, k * P:(k + 1) * P], ident)
                    last.then_inc(S.hT_psum, 1)
                pe.wait_ge(S.hT_even, w.to(S.hT_even, 2))
                pe.wait_ge(S.hT_odd, w.to(S.hT_odd, 2))

            def tokens_out(r, width, banks, offs=(0, 0), each=True):
                wv = view(r, KT, width)
                for t in range(TT):
                    for k in range(KT):
                        last = pe.matmul(PS[:, banks[t], offs[t]:offs[t] + width], hT[:, k, t * P:(t + 1) * P],
                                         wv[:, k, :], start=(k == 0), stop=(k == KT - 1))
                    if each:
                        last.then_inc(S.projected, 1)
                if not each:
                    last.then_inc(S.projected, 1)

            def channels_out(r, banks):
                wv = view(r, KT, 512)
                for c in range(4):
                    if c == 2 and banks[1] == 4:
                        pe.wait_ge(S.act_took, w.to(S.act_took))
                    for k in range(KT):
                        last = pe.matmul(PS[:, banks[c // 2], (c % 2) * SEQ:(c % 2 + 1) * SEQ],
                                         wv[:, k, c * P:(c + 1) * P], hT[:, k, :],
                                         start=(k == 0), stop=(k == KT - 1))
                    if c % 2:
                        last.then_inc(S.projected, 1)

            def attend(units, b):
                def scores(i):
                    u = units[i]
                    if i >= 2:
                        pe.wait_ge(S.masked, w.to(S.masked))
                    lo = DH * u.half
                    for r in range(4):
                        last = pe.matmul(PS[:, 2 * (i % 2) + r // 2, (r % 2) * SEQ:(r % 2) * SEQ + u.nk * P],
                                         u.qT[lo:lo + DH, u.tile + r, u.t * P:(u.t + 1) * P],
                                         u.kT[lo:lo + DH, u.gp, 0:u.nk * P], start=True, stop=True)
                    last.then_inc(S.scored, 1)

                def turn(i):
                    u = units[i]
                    pe.wait_ge(S.exped, w.to(S.exped))
                    if i:
                        pe.wait_ge(S.turned_taken, w.to(S.turned_taken))
                    for kt in range(u.nk):
                        for r in range(4):
                            last = pe.transpose(PS[:, 4 + kt, r * P:(r + 1) * P],
                                                b.P[i % 2][:, r, kt * P:(kt + 1) * P], ident)
                    last.then_inc(S.turned, 1)

                def values(i):
                    u = units[i]
                    if i >= 2:
                        pe.wait_ge(S.o_taken, w.to(S.o_taken))
                    for r in range(4):
                        lo = r * DH
                        for kt in range(u.nk):
                            last = pe.matmul(PS[:, 6 + i % 2, lo:lo + DH], b.PT[i % 2][:, kt, r, :],
                                             u.v[:, kt, u.g * DH:(u.g + 1) * DH],
                                             start=(kt == 0), stop=(kt == u.nk - 1))
                    last.then_inc(S.valued, 1)

                scores(0)
                for i in range(len(units)):
                    if i + 1 < len(units):
                        scores(i + 1)
                    turn(i)
                    if i:
                        values(i - 1)
                pe.wait_ge(S.turned_taken, w.to(S.turned_taken))
                values(len(units) - 1)
                pe.wait_ge(S.masked, w.to(S.masked, 2))
                pe.wait_ge(S.o_taken, w.to(S.o_taken, 2))

            def mixer(l):
                transpose_h()
                tokens_out(slot(), 512, (4, 5))
                tokens_out(slot(), 256, (6, 6), (0, 256), each=False)
                channels_out(slot(), (7, 0))
                channels_out(slot(), (1, 2))
                channels_out(slot(), (3, 4))
                pe.wait_ge(S.dve_took, w.to(S.dve_took, 3))
                pe.wait_ge(S.act_took, w.to(S.act_took, 4))
                for t in range(TT):
                    for m in range(4):
                        last = pe.transpose(PS[:, 5 + t, m * P:(m + 1) * P], MB.q[:, t, m * P:(m + 1) * P], ident)
                    last.then_inc(S.turned_q, 1)
                for t in range(TT):
                    last = pe.transpose(PS[:, 7, t * P:(t + 1) * P], MB.kv[:, t, 0:P], ident)
                last.then_inc(S.turned_q, 1)
                pe.wait_ge(S.q_turned_act, w.to(S.q_turned_act, 3))
                pe.wait_ge(S.dve_took, w.to(S.dve_took, 4))
                attend(mixer_units(), MB)
                pe.wait_ge(S.conv_gain, w.to(S.conv_gain, 5))
                for t in range(TT):
                    for c in range(4):
                        last = pe.matmul(PS[:, 7, t:t + 1], MB.sq[:, c, t * P:(t + 1) * P], ones[:, 0:1],
                                         start=(c == 0), stop=(c == 3))
                last.then_inc(S.conv_ss, 1)
                for part in range(2):
                    if part:
                        for c in range(4):
                            for t in range(TT):
                                last = pe.transpose(PS[:, 4 + c // 2, (c % 2) * SEQ + t * P:(c % 2) * SEQ + (t + 1) * P],
                                                    MB.ya[:, t, c * P:(c + 1) * P], ident)
                            if c % 2:
                                last.then_inc(S.ya_psum, 1)
                        pe.wait_ge(S.yaT_ready, w.to(S.yaT_ready, 4))
                        pe.wait_ge(S.conv_root, w.to(S.conv_root))
                    src = MB.yaT if part else MB.yc
                    wv = view(slot(), 4, D)
                    for t in range(TT):
                        for h in range(2):
                            for c in range(4):
                                last = pe.matmul(PS[:, 4 * part + 2 * t + h, :], src[:, c, t * P:(t + 1) * P],
                                                 wv[:, c, h * 512:(h + 1) * 512], start=(c == 0), stop=(c == 3))
                    last.then_inc(S.acc_done, 1)

            def clear_acc():
                for b in range(4):
                    pe.matmul(PS[:, b, :], zeros[:, 0:P], zeros[:, :], start=True, stop=False,
                              skip_group_check=True)

            def experts(s, f, passes, y):
                def gather(b):
                    for k in range(4 * b, 4 * b + 4):
                        for t in range(TT):
                            last = pe.matmul(PS[:, 4 + b, (k % 4) * P:(k % 4 + 1) * P],
                                             hp[:, t, k * P:(k + 1) * P], EB.OH[:, t, :],
                                             start=(t == 0), stop=(t == 1))
                    last.then_inc(s.gathered, 1)

                def wide_sums(e, m, u):
                    for h in range(2):
                        pe.wait_ge(s.low_made, f.to(s.low_made))
                        for k in range(4):
                            for part in range(2):
                                wv = split[:, (u + h) % SPLIT, part, :].rearrange("p (k n) -> p k n", k=4)
                                last = pe.matmul(PS[:, 4 + m, :], xs[:, e, 4 * h + k, :], wv[:, k, :],
                                                 start=(h == 0 and k == 0 and part == 0),
                                                 stop=(h == 1 and k == 3 and part == 1))
                        last.then_inc(s.half_used, 1)

                def turn_sums():
                    for m in range(2):
                        for ft in range(4):
                            lo = (4 * m + ft) * CAP
                            last = pe.matmul(PS[:, 6, lo:lo + CAP], EB.gu[:, m, ft * P:(ft + 1) * P], const("fold"),
                                             start=True, stop=True)
                    last.then_inc(s.gu_turned, 1)

                def down(u):
                    for h in range(2):
                        pe.wait_ge(s.low_made, f.to(s.low_made))
                        for k in range(2):
                            for part in range(2):
                                wv = split[:, (u + h) % SPLIT, part, :].rearrange("p (k n) -> p k n", k=2)
                                for c in range(2):
                                    last = pe.matmul(PS[:, 6 + c, :], hid[:, 2 * h + k, :],
                                                     wv[:, k, c * 512:(c + 1) * 512],
                                                     start=(h == 0 and k == 0 and part == 0),
                                                     stop=(h == 1 and k == 1 and part == 1))
                        last.then_inc(s.half_used, 1)

                def combine(e):
                    pe.wait_ge(s.y_taken, f.to(s.y_taken))
                    for t in range(TT):
                        for c in range(2):
                            last = pe.matmul(PS[:, 2 * t + c, :], EB.G[:, e, t * P:(t + 1) * P],
                                             y[:, c * 512:(c + 1) * 512], start=False, stop=False,
                                             skip_group_check=True)
                    return last

                clear_acc()
                pe.wait_ge(s.onehot, f.to(s.onehot))
                gather(0)
                gather(1)
                per = {s.onehot: 1, s.x_made: 2, s.low_made: UNITS, s.onehot_g: 1, s.g_taken: 1, s.gu_taken: 4,
                       s.h_made: 2, s.y_taken: 2}
                with pe.Fori(0, passes) as p:
                    f.enter(p, per)
                    pe.wait_ge(s.x_made, f.to(s.x_made, 2))
                    wide_sums(0, 0, 0)
                    wide_sums(0, 1, 2)
                    pe.wait_ge(s.onehot_g, f.to(s.onehot_g))
                    for e in range(2):
                        for t in range(TT):
                            last = pe.transpose(PS[:, 7, e * SEQ + t * P:e * SEQ + (t + 1) * P],
                                                EB.OHg[:, t, e, :], ident)
                    last.then_inc(s.oh_turned, 1)
                    pe.wait_ge(s.gu_taken, f.to(s.gu_taken, 2))
                    turn_sums()
                    wide_sums(1, 0, 4)
                    pe.wait_ge(s.g_taken, f.to(s.g_taken))
                    pe.wait_ge(s.h_made, f.to(s.h_made))
                    down(6)
                    wide_sums(1, 1, 8)
                    combine(0)
                    pe.wait_ge(s.gu_taken, f.to(s.gu_taken, 2))
                    turn_sums()
                    pe.wait_ge(s.onehot, f.to(s.onehot))
                    gather(0)
                    pe.wait_ge(s.h_made, f.to(s.h_made))
                    down(10)
                    gather(1)
                    combine(1).then_inc(s.combined, 1)
                    f.leave(passes)
                f.past(s.x_made, 2)

            def moe(l):
                transpose_h()
                for t in range(TT):
                    for k in range(KT):
                        last = pe.matmul(PS[:, 4, t * 64:t * 64 + NG + NE], hT[:, k, t * P:(t + 1) * P],
                                         wr[:, l, k, :], start=(k == 0), stop=(k == KT - 1))
                last.then_inc(S.routed, 1)
                pe.wait_ge(S.marked, w.to(S.marked))
                pe.matmul(PS[:, 5, 0:NE], upper, EB.mk[:, 0, :], start=True, stop=True)
                pe.matmul(PS[:, 5, NE:2 * NE], ones, EB.mk[:, 0, :], start=True, stop=False)
                pe.matmul(PS[:, 5, NE:2 * NE], upper, EB.mk[:, 1, :], start=False, stop=True)
                pe.matmul(PS[:, 5, 2 * NE:3 * NE], ones, EB.mk[:, 0, :], start=True, stop=False)
                pe.matmul(PS[:, 5, 2 * NE:3 * NE], ones, EB.mk[:, 1, :], start=False, stop=True) \
                    .then_inc(S.ranked, 1)
                experts(M, w, PAIRS, gB[:, l, :])
                n[0] += RING * PAIRS
                for r in range(RING):
                    w.past(S.loaded[r], 16 * PAIRS)
                pe.wait_ge(S.flag_ready, w.to(S.flag_ready))
                pe.wait_ge(S.moe_added, w.to(S.moe_added))
                most = pe.value_load(flag[0:1, 0:1], min_val=0, max_val=SEQ)
                with pe.If(most > CAP):
                    experts(OV[l], Follow(), MORE * PAIRS, gB[:, l, :])

            def ffn():
                transpose_h()
                clear_acc()

                def run(tiles, final):
                    taken = {}

                    def take(c, m):
                        if (c, m) not in taken:
                            taken[c, m] = slot_at(c, m)
                        return taken[c, m]

                    def gate_up(i):
                        c, ft, width, _ = tiles[i]
                        for m in range(2):
                            wv = view(take(c, m), KT, width)
                            for k in range(KT):
                                last = pe.matmul(PS[:, 4 + i % 4, m * SEQ:(m + 1) * SEQ],
                                                 wv[:, k, ft * P:(ft + 1) * P], hT[:, k, :],
                                                 start=(k == 0), stop=(k == KT - 1))
                        last.then_inc(S.ffn_gu, 1)

                    def down(i):
                        c, ft, width, end = tiles[i]
                        wv = view(take(c, 2), width // P, D)
                        pe.wait_ge(S.ffn_h, w.to(S.ffn_h))
                        for t in range(TT):
                            for h in range(2):
                                last = pe.matmul(PS[:, 2 * t + h, :], FB.hF[:, i % 4, t * P:(t + 1) * P],
                                                 wv[:, ft, h * 512:(h + 1) * 512], start=False, stop=False,
                                                 skip_group_check=True)
                        if end:
                            last.then_inc(S.acc_done if final and i == len(tiles) - 1 else S.ffn_down, 1)

                    base = n[0]

                    def slot_at(c, m):
                        r = (base + 3 * c + m) % RING
                        pe.wait_ge(S.loaded[r], w.to(S.loaded[r], 16))
                        return r

                    gate_up(0)
                    for i in range(len(tiles)):
                        if i + 1 < len(tiles):
                            gate_up(i + 1)
                        down(i)
                    n[0] += 3 * (tiles[-1][0] + 1)

                whole = [(c, ft, 512, ft == 3) for c in range(2) for ft in range(4)]
                per = {S.loaded[r]: 16 for r in range(RING)}
                per[S.ffn_h] = 8
                with pe.Fori(0, 2) as p:
                    w.enter(p, per)
                    run(whole, False)
                    w.leave(2)
                n[0] += RING
                run([(0, ft, 512, ft == 3) for ft in range(4)] + [(1, ft, 256, ft == 1) for ft in range(2)], True)

            def pool_mix():
                pe.wait_ge(S.means_loaded, w.to(S.means_loaded, 16))
                for c in range(KT):
                    for t in range(TT):
                        if c == 0:
                            pe.wait_ge(S.h_ready, w.to(S.h_ready))
                        last = pe.matmul(PS[:, c // 2, (c % 2) * SEQ:(c % 2 + 1) * SEQ], hp[:, t, c * P:(c + 1) * P],
                                         pool_means[:, t, c // 2, :], start=(t == 0), stop=(t == 1))
                    if c % 2:
                        last.then_inc(S.hT_psum, 1)
                pe.wait_ge(S.hT_even, w.to(S.hT_even, 2))
                pe.wait_ge(S.hT_odd, w.to(S.hT_odd, 2))
                wv = view(slot(), 8, 256)
                for t in range(TT):
                    for g in range(4):
                        o = PS[:, 2 * t + g // 2, (g % 2) * 256:(g % 2 + 1) * 256]
                        for c in range(2):
                            pe.matmul(o, hT[:, 2 * g + c, t * P:(t + 1) * P], wv[:, 2 * g + c, :],
                                      start=(c == 0), stop=False)
                        last = pe.matmul(o, ones[0:1, 0:P], pbias[0:1, g * 256:(g + 1) * 256],
                                         start=False, stop=True)
                last.then_inc(S.acc_done, 1)

            def nsa():
                transpose_h()
                tokens_out(slot(), 512, (4, 5))
                tokens_out(slot(), 512, (6, 7))
                tokens_out(slot(), 512, (0, 1))
                tokens_out(slot(), 512, (2, 3))
                pe.wait_ge(S.act_took, w.to(S.act_took, 2))
                tokens_out(slot(), 512, (4, 5))
                pe.wait_ge(S.act_took, w.to(S.act_took, 1))
                tokens_out(slot(), 48, (6, 6), (0, 48), each=False)
                pe.wait_ge(S.act_took, w.to(S.act_took, 8))
                pe.wait_ge(S.dve_took, w.to(S.dve_took, 8))
                for src, b0 in ((NB.qn, 0), (NB.qr, 4)):
                    for t in range(TT):
                        for gp in range(2):
                            for r in range(4):
                                m = gp * 4 + r
                                last = pe.transpose(PS[:, b0 + 2 * t + gp, r * P:(r + 1) * P],
                                                    src[:, t, m * P:(m + 1) * P], ident)
                            last.then_inc(S.turned_q, 1)
                pe.wait_ge(S.q_turned_act, w.to(S.q_turned_act, 4))
                for b, (src, off) in enumerate(((NB.kvc, 0), (NB.kvc, 256), (NB.kv[0], 0), (NB.kv[1], 0))):
                    for gp in range(2):
                        for t in range(TT):
                            last = pe.transpose(PS[:, b, gp * SEQ + t * P:gp * SEQ + (t + 1) * P],
                                                src[:, t, off + gp * P:off + (gp + 1) * P], ident)
                    last.then_inc(S.turned_q, 1)
                pe.wait_ge(S.q_turned_dve, w.to(S.q_turned_dve, 4))
                for s in range(2):
                    wv = view(slot(), 16, 256)
                    pe.wait_ge(S.z_pos, w.to(S.z_pos))
                    for c in range(2):
                        for j in range(16):
                            last = pe.matmul(PS[:, 4 + s, c * 60:(c + 1) * 60], wv[:, j, c * P:(c + 1) * P],
                                             NB.Z[s][:, j, :], start=(j == 0), stop=(j == 15))
                    last.then_inc(S.hidden, 1)
                pe.wait_ge(S.hc_ready, w.to(S.hc_ready, 2))
                for c in range(2):
                    pe.matmul(PS[:, 6, 0:60], w2k[:, c, :], NB.hc[:, 0, c * 60:(c + 1) * 60],
                              start=(c == 0), stop=(c == 1))
                for g in range(4):
                    for c in range(2):
                        last = pe.matmul(PS[0:NCMP, 7, g * DH:(g + 1) * DH],
                                         NB.hc[:, 1, c * 60 + g * NCMP:c * 60 + (g + 1) * NCMP], w2v[:, c, :],
                                         start=(c == 0), stop=(c == 1))
                last.then_inc(S.compressed, 1)
                pe.wait_ge(S.kc_ready, w.to(S.kc_ready))
                pe.wait_ge(S.q_turned_act, w.to(S.q_turned_act, 2))
                for t in range(TT):
                    for h in range(16):
                        g, r = h // 4, h % 4
                        lo = DH * (g % 2)
                        last = pe.matmul(PS[:, 2 * t + g % 2, h * 16:h * 16 + NCMP],
                                         NB.qnT[lo:lo + DH, 4 * (g // 2) + r, t * P:(t + 1) * P],
                                         NB.KC[lo:lo + DH, g * NCMP:(g + 1) * NCMP], start=True, stop=True)
                    last.then_inc(S.cscored, 1)
                for t in range(TT):
                    pe.wait_ge(S.p_ready, w.to(S.p_ready))
                    for g in range(4):
                        last = pe.transpose(PS[:, 2 + t, g * P:(g + 1) * P], NB.P32[:, t, 4 * g:4 * g + 4, :], ident)
                    last.then_inc(S.p_turned, 1)
                for t in range(TT):
                    pe.wait_ge(S.pT_ready, w.to(S.pT_ready))
                    for g in range(4):
                        last = pe.matmul(PS[:, 4 + 2 * t + g // 2, (g % 2) * 256:(g % 2 + 1) * 256],
                                         NB.PcT[:, t, g, :], NB.Vbd[:, g, :], start=True, stop=True)
                    last.then_inc(S.cvalued, 1)
                pe.wait_ge(S.o_first, w.to(S.o_first, 2))
                attend(nsa_units(), NB)
                transpose_h()
                for m in range(2):
                    wv = view(slot(), 4, D)
                    for t in range(TT):
                        for h in range(2):
                            for k in range(4):
                                last = pe.matmul(PS[:, 2 * t + h + 4, :], hT[:, 4 * m + k, t * P:(t + 1) * P],
                                                 wv[:, k, h * 512:(h + 1) * 512],
                                                 start=(m == 0 and k == 0), stop=(m == 1 and k == 3))
                    last.then_inc(S.acc_done if m else S.half_done, 1)

            pe.wait_ge(S.const_loaded, w.to(S.const_loaded, 16))
            pe.wait_ge(S.param_loaded, PARAMS)
            pe.wait_ge(S.set_up, w.to(S.set_up, 2))
            for name in stages:
                if name[:3] == "mix":
                    mixer(int(name[3]))
                elif name[:3] == "moe":
                    moe(int(name[3]))
                elif name[:3] == "ffn":
                    ffn()
                elif name == "pool":
                    pool_mix()
                elif name == "nsa":
                    nsa()

        @block.scalar
        def _(act):
            w = Follow(S.act_step)
            seen_x = [False]
            counted = [0]

            def copy(o, i):
                return act.activation(o, i, ACT.Copy)

            def squares(src, junk, sums):
                for t in range(TT):
                    last = act.activation(junk(t), src(t), ACT.Square, accum_out=sums[:, t:t + 1])
                last.then_inc(S.act_step, 1)
                act.wait_ge(S.act_step, w.to(S.act_step))

            def roots(o, i, width, s):
                act.activation(o, i, ACT.Sqrt, bias=epsb[:, 0:1], scale=1.0 / width).then_inc(s, 1)

            def x_now():
                if seen_x[0]:
                    act.wait_ge(S.x_ready, w.to(S.x_ready))
                else:
                    act.wait_ge(S.x_loaded, w.to(S.x_loaded, 16))
                    act.wait_ge(S.set_up, w.to(S.set_up, 2))
                    act.wait_ge(S.param_loaded, PARAMS)
                    seen_x[0] = True

            def norm():
                x_now()
                squares(lambda t: x[:, t, :], lambda t: hp[:, t, :], ss)
                roots(root, ss, D, S.root_ready)

            def take_hT(gain):
                for b in (0, 2):
                    act.wait_ge(S.hT_psum, w.to(S.hT_psum))
                    if gain is None:
                        i = copy(hT[:, 2 * b:2 * b + 2, :].rearrange("p a b -> p (a b)"), PS[:, b, :])
                    else:
                        for k in range(2):
                            i = act.activation(hT[:, 2 * b + k, :], PS[:, b, k * SEQ:(k + 1) * SEQ], ACT.Copy,
                                               scale=gT[:, gain, 2 * b + k:2 * b + k + 1])
                    i.then_inc(S.hT_even, 1)
                    w.past(S.hT_psum)

            def post(bank):
                squares(lambda t: PS[:, bank + 2 * t:bank + 2 * t + 2, :], lambda t: hp[:, t, :].rearrange(
                    "p (a b) -> p a b", a=2), ss)
                roots(root, ss, D, S.root_ready)

            def attend(units, b, sinks):
                def take(i):
                    act.wait_ge(S.turned, w.to(S.turned))
                    nk = units[i].nk
                    copy(b.PT[i % 2][:, 0:nk, :, :].rearrange("p k r q -> p k (r q)"), PS[:, 4:4 + nk, :]) \
                        .then_inc(S.turned_taken, 1)

                for i, u in enumerate(units):
                    act.wait_ge(S.maxed, w.to(S.maxed))
                    st = b.stat[:, i % 4, :]
                    if sinks:
                        act.activation(st[:, 8:12], st[:, 8:12], ACT.Exp)
                    for r in range(4):
                        last = act.activation(b.P[i % 2][:, r, 0:u.nk * P], b.Sm[i % 2][:, r, 0:u.nk * P], ACT.Exp,
                                              bias=st[:, r:r + 1], scale=SCALE, accum_out=st[:, 4 + r:5 + r])
                    last.then_inc(S.exped, 1)
                    if i:
                        take(i - 1)
                take(len(units) - 1)

            def mixer(l):
                norm()
                take_hT(l)
                for t in range(TT):
                    act.wait_ge(S.projected, w.to(S.projected))
                    copy(MB.q[:, t, :].rearrange("p (r h d) -> p h r d", h=2, r=4),
                         PS[:, 4 + t, :].rearrange("p (h r d) -> p h r d", h=2, r=4)).then_inc(S.act_took, 1)
                act.wait_ge(S.projected, w.to(S.projected))
                copy(MB.kv.rearrange("p a b -> p (a b)"), PS[:, 6, :]).then_inc(S.act_took, 1)
                for h in range(2):
                    act.wait_ge(S.projected, w.to(S.projected))
                    copy(MB.gate_c[:, 2 * h:2 * h + 2, :].rearrange("p a b -> p (a b)"), PS[:, (7, 0)[h], :]) \
                        .then_inc(S.act_took, 1)
                w.past(S.projected, 4)
                for t in range(TT):
                    act.wait_ge(S.turned_q, w.to(S.turned_q))
                    copy(MB.qT[:, :, t * P:(t + 1) * P], PS[:, 5 + t, :].rearrange("p (m q) -> p m q", m=4)) \
                        .then_inc(S.q_turned_act, 1)
                act.wait_ge(S.turned_q, w.to(S.turned_q))
                copy(MB.kT[:, 0, :], PS[:, 7, 0:SEQ]).then_inc(S.q_turned_act, 1)
                act.wait_ge(S.dve_took, w.to(S.dve_took, 7))
                attend(mixer_units(), MB, True)
                act.activation(MB.sq, MB.yc, ACT.Square).then_inc(S.conv_gain, 1)
                act.wait_ge(S.conv_gain, w.to(S.conv_gain))
                for c in range(4):
                    act.activation(MB.yc[:, c, :], MB.yc[:, c, :], ACT.Copy, scale=gcT[:, l, c:c + 1]) \
                        .then_inc(S.conv_gain, 1)
                w.past(S.conv_gain, 4)
                act.wait_ge(S.o_taken, w.to(S.o_taken, 4))
                squares(lambda t: MB.ya[:, t, :], lambda t: MB.junk[:, 2 * t:2 * t + 2, :].rearrange(
                    "p a b -> p (a b)"), ss)
                roots(root, ss, 512, S.ya_root)
                act.wait_ge(S.conv_ss, w.to(S.conv_ss))
                roots(rootc, PS[:, 7, 0:2], 512, S.conv_root)
                for c in range(4):
                    if c % 2 == 0:
                        act.wait_ge(S.ya_psum, w.to(S.ya_psum))
                    act.activation(MB.yaT[:, c, :], PS[:, 4 + c // 2, (c % 2) * SEQ:(c % 2 + 1) * SEQ], ACT.Copy,
                                   scale=gaT[:, l, c:c + 1]).then_inc(S.yaT_ready, 1)
                w.past(S.acc_done, 2)

            def experts(s, f, first, passes, y):
                def high(u):
                    r = (first + u // 2) % RING
                    if u % 2 == 0:
                        act.wait_ge(s.loaded[r], f.to(s.loaded[r], 16))
                    copy(split[:, u % SPLIT, 0, :], ring[:, r, (u % 2) * HALF:(u % 2 + 1) * HALF]) \
                        .then_inc(s.high_made, 1)

                def high_x(b):
                    act.wait_ge(s.gathered, f.to(s.gathered))
                    copy(xs[:, :, 4 * b:4 * b + 4, 0:CAP].rearrange("p e k s -> p k e s"),
                         PS[:, 4 + b, :].rearrange("p (k e s) -> p k e s", k=4, e=2)).then_inc(s.x_high, 1)

                def silu():
                    act.wait_ge(s.gu_turned, f.to(s.gu_turned))
                    act.activation(EB.sE.rearrange("p a b -> p (a b)"), PS[:, 6, 0:4 * CAP], ACT.Silu) \
                        .then_inc(s.silu_done, 1)

                def take_gate():
                    copy(EB.gu[:, 0, :], PS[:, 4, :]).then_inc(s.gu_taken, 1)

                def take_up():
                    copy(EB.gu[:, 1, :], PS[:, 5, :]).then_inc(s.gu_taken, 1)

                def take_y():
                    copy(y.rearrange("p (c n) -> p c n", c=2), PS[:, 6:8, :]).then_inc(s.y_taken, 1)

                def one_pair(more):
                    act.wait_ge(s.half_used, f.to(s.half_used))
                    high(3)
                    act.wait_ge(s.half_used, f.to(s.half_used))
                    high(4)
                    take_gate()
                    act.wait_ge(s.half_used, f.to(s.half_used))
                    high(5)
                    act.wait_ge(s.half_used, f.to(s.half_used))
                    take_up()
                    high(6)
                    silu()
                    act.wait_ge(s.half_used, f.to(s.half_used))
                    high(7)
                    act.wait_ge(s.half_used, f.to(s.half_used))
                    high(8)
                    take_gate()
                    act.wait_ge(s.half_used, f.to(s.half_used))
                    high(9)
                    act.wait_ge(s.half_used, f.to(s.half_used))
                    take_y()
                    high(10)
                    act.wait_ge(s.half_used, f.to(s.half_used))
                    high(11)
                    act.wait_ge(s.half_used, f.to(s.half_used))
                    take_up()
                    if more:
                        high(12)
                    silu()
                    high_x(0)
                    act.wait_ge(s.half_used, f.to(s.half_used))
                    if more:
                        high(13)
                    act.wait_ge(s.half_used, f.to(s.half_used))
                    take_y()
                    high_x(1)
                    if more:
                        high(14)

                for u in range(SPLIT):
                    high(u)
                high_x(0)
                high_x(1)
                per = {s.half_used: UNITS, s.gathered: 2, s.gu_turned: 2}
                per.update({s.loaded[r]: 16 for r in range(RING)})
                with act.Fori(0, passes - 1) as p:
                    f.enter(p, per)
                    one_pair(True)
                    f.leave(passes - 1)
                one_pair(False)

            def moe(l):
                norm()
                take_hT(None)
                act.wait_ge(S.gate_e, w.to(S.gate_e))
                act.activation(EB.ge, EB.gd, ACT.Exp).then_inc(S.gate_exp, 1)
                act.wait_ge(S.gate_e, w.to(S.gate_e))
                act.activation(EB.s[:, 5, :], EB.s[:, 4, :], ACT.Exp).then_inc(S.gate_exp, 1)
                experts(M, w, first_slot(f"moe{l}"), PAIRS, gB[:, l, :])
                act.wait_ge(S.flag_ready, w.to(S.flag_ready))
                most = act.value_load(flag[0:1, 0:1], min_val=0, max_val=SEQ)
                with act.If(most > CAP):
                    experts(OV[l], Follow(), first_slot(f"moe{l}"), MORE * PAIRS, gB[:, l, :])

            def count_loads(name):
                for k in range(counted[0], first_slot(name)):
                    w.past(S.loaded[k % RING], 16)
                counted[0] = first_slot(name)

            def ffn(gain):
                norm()
                take_hT(gain)

                def run(n):
                    for i in range(n):
                        act.wait_ge(S.ffn_gu, w.to(S.ffn_gu))
                        act.activation(FB.sF[:, i % 2, :], PS[:, 4 + i % 4, 0:SEQ], ACT.Silu).then_inc(S.ffn_silu, 1)

                with act.Fori(0, 2) as p:
                    w.enter(p, {S.ffn_gu: 8})
                    run(8)
                    w.leave(2)
                run(6)
                act.wait_ge(S.acc_done, w.to(S.acc_done))
                post(0)

            def pool_mix():
                norm()
                take_hT(7)
                w.past(S.acc_done)
                act.wait_ge(S.scaled, w.to(S.scaled, 2))
                squares(lambda t: pool_f[:, t, :], lambda t: hp[:, t, :], ss)
                roots(root, ss, D, S.root_ready)

            def nsa():
                norm()
                take_hT(5)
                for gp in range(2):
                    for t in range(TT):
                        act.wait_ge(S.projected, w.to(S.projected))
                        copy(NB.qn[:, t, gp * 512:(gp + 1) * 512].rearrange("p (r h d) -> p h r d", r=4, h=2),
                             PS[:, 4 + 2 * gp + t, :].rearrange("p (h r d) -> p h r d", r=4, h=2)) \
                            .then_inc(S.act_took, 1)
                for t in range(TT):
                    act.wait_ge(S.projected, w.to(S.projected))
                    copy(NB.kvc[:, t, :], PS[:, t, :]).then_inc(S.act_took, 1)
                for br in range(2):
                    for t in range(TT):
                        act.wait_ge(S.projected, w.to(S.projected))
                        copy(NB.kv[br][:, t, :], PS[:, 2 + 2 * br + t, :]).then_inc(S.act_took, 1)
                act.wait_ge(S.projected, w.to(S.projected))
                act.activation(NB.gts.rearrange("p a b -> p (a b)"), PS[:, 6, 0:96], ACT.Sigmoid) \
                    .then_inc(S.act_took, 1)
                for t in range(TT):
                    for gp in range(2):
                        act.wait_ge(S.turned_q, w.to(S.turned_q))
                        copy(NB.qnT[:, 4 * gp:4 * gp + 4, t * P:(t + 1) * P],
                             PS[:, 2 * t + gp, :].rearrange("p (m q) -> p m q", m=4)).then_inc(S.q_turned_act, 1)
                w.past(S.turned_q, 5)
                act.wait_ge(S.turned_q, w.to(S.turned_q))
                for g in range(4):
                    for r in range(2):
                        for h in range(2):
                            last = copy(*z_view(1, g, r, h))
                last.then_inc(S.z_built, 1)
                for br in range(2):
                    act.wait_ge(S.turned_q, w.to(S.turned_q))
                    copy(NB.kT[br].rearrange("p a b -> p (a b)"), PS[:, 2 + br, :]).then_inc(S.q_turned_act, 1)
                for s in range(2):
                    act.wait_ge(S.hidden, w.to(S.hidden))
                    act.activation(NB.hc[:, s, :], PS[:, 4 + s, 0:120], ACT.Silu).then_inc(S.hc_ready, 1)
                for t in range(TT):
                    act.wait_ge(S.csub, w.to(S.csub))
                    act.activation(NB.Sc[t], NB.Sc[t], ACT.Exp, scale=SCALE).then_inc(S.cexp, 1)
                for t in range(TT):
                    act.wait_ge(S.p_turned, w.to(S.p_turned))
                    copy(NB.PcT[:, t, :, :].rearrange("p a b -> p (a b)"), PS[:, 2 + t, :]).then_inc(S.pT_ready, 1)
                for t in range(TT):
                    act.wait_ge(S.cvalued, w.to(S.cvalued))
                    copy(hp[:, t, :].rearrange("p (a b) -> p a b", a=2), PS[:, 4 + 2 * t:6 + 2 * t, :]) \
                        .then_inc(S.o_first, 1)
                attend(nsa_units(), NB, False)
                take_hT(None)
                act.wait_ge(S.acc_done, w.to(S.acc_done))
                post(4)

            FFN_GAIN = {"ffn00": 2, "ffn01": 3, "ffn10": 4, "ffn11": 6}
            for name in stages:
                if name[:3] == "mix":
                    mixer(int(name[3]))
                elif name[:3] == "moe":
                    count_loads(name)
                    moe(int(name[3]))
                    counted[0] += RING * PAIRS
                elif name == "final":
                    norm()
                elif name[:3] == "ffn":
                    ffn(FFN_GAIN[name])
                elif name == "pool":
                    pool_mix()
                elif name == "nsa":
                    nsa()

        @block.vector
        def _(v):
            w = Follow(S.dve_step)
            gi = [0]

            def gain_rows():
                i = gi[0]
                gi[0] += 1
                v.wait_ge(S.gB_loaded[i % 2], w.to(S.gB_loaded[i % 2], 16))
                return gB[:, i % 2, :]

            def reciprocal(o, i):
                v.reciprocal(o, i).then_inc(S.dve_step, 1)
                v.wait_ge(S.dve_step, w.to(S.dve_step))

            def bc(ap, shape):
                return ap.to_broadcast(shape)

            def norm(permute=True, gain=None):
                v.wait_ge(S.root_ready, w.to(S.root_ready))
                reciprocal(rstd, root)
                for t in range(TT):
                    xi, o = x[:, t, :], hp[:, t, :]
                    if permute:
                        xi = xi.rearrange("p (q k) -> p k q", k=KT)
                        o = o.rearrange("p (k q) -> p k q", k=KT)
                    if gain is None:
                        i = v.tensor_scalar(o, xi, rstd[:, t:t + 1], None, ALU.mult)
                    else:
                        i = v.scalar_tensor_tensor(o, xi, rstd[:, t:t + 1],
                                                   gain.rearrange("p (q k) -> p k q", k=KT), ALU.mult, ALU.mult)
                    i.then_inc(S.h_ready, 1)

            def take_hT(gain):
                for b in (1, 3):
                    v.wait_ge(S.hT_psum, w.to(S.hT_psum, 2))
                    if gain is None:
                        i = v.tensor_copy(hT[:, 2 * b:2 * b + 2, :].rearrange("p a b -> p (a b)"), PS[:, b, :])
                    else:
                        for k in range(2):
                            i = v.tensor_scalar(hT[:, 2 * b + k, :], PS[:, b, k * SEQ:(k + 1) * SEQ],
                                                gT[:, gain, 2 * b + k:2 * b + k + 1], None, ALU.mult)
                    i.then_inc(S.hT_odd, 1)

            def post(src, factor):
                gain = gain_rows()
                v.wait_ge(S.root_ready, w.to(S.root_ready))
                reciprocal(rstd, root)
                for t in range(TT):
                    v.scalar_tensor_tensor(hp[:, t, :], src(t), rstd[:, t:t + 1], gain, ALU.mult, ALU.mult).then_inc(S.dve_step, 1)
                    v.wait_ge(S.dve_step, w.to(S.dve_step))
                    v.scalar_tensor_tensor(x[:, t, :], hp[:, t, :], factor, x[:, t, :], ALU.mult, ALU.add).then_inc(S.x_ready if t else S.dve_step, 1)
                    v.wait_ge(S.x_ready if t else S.dve_step, w.to(S.x_ready if t else S.dve_step))

            def psum_rows(bank):
                return lambda t: PS[:, bank + 2 * t:bank + 2 * t + 2, :].rearrange("p a b -> p (a b)")

            def rotate(src, dst, t, tmp):
                n = src.shape[1]
                A = tmp[:, 0:n * ROPE].rearrange("p (h c) -> p h c", c=ROPE)
                B = tmp[:, 128:128 + n * ROPE].rearrange("p (h c) -> p h c", c=ROPE)
                H2 = ROPE // 2

                def table(name, lo, hi):
                    c0 = CONSTS[name][0] + t * ROPE
                    return cst[:, c0 + lo:c0 + hi].unsqueeze(1).to_broadcast([P, n, hi - lo])

                v.tensor_tensor(A, src[:, :, 0:ROPE], table("rope_c", 0, ROPE), ALU.mult)
                v.tensor_tensor(B[:, :, 0:H2], src[:, :, H2:ROPE], table("rope_s", 0, H2), ALU.mult)
                v.tensor_tensor(B[:, :, H2:ROPE], src[:, :, 0:H2], table("rope_s", H2, ROPE), ALU.mult).then_inc(S.dve_step, 1)
                v.wait_ge(S.dve_step, w.to(S.dve_step))
                return v.tensor_tensor(dst[:, :, 0:ROPE], A, B, ALU.add)

            def attend(units, b, sinks, finish):
                def stats(i):
                    u = units[i]
                    st = b.stat[:, i % 4, :]
                    n = u.nk * P
                    v.wait_ge(S.scored, w.to(S.scored))
                    if i >= 2:
                        v.wait_ge(S.exped, w.to(S.exped))
                    s4 = PS[:, 2 * (i % 2):2 * (i % 2) + 2, :].rearrange("p a (r k) -> p (a r) k", r=2)[:, :, 0:n]
                    sm = b.Sm[i % 2][:, :, 0:n]
                    v.tensor_tensor(sm, s4, u.mask.unsqueeze(1).to_broadcast([P, 4, n]), ALU.add).then_inc(S.masked, 1)
                    v.wait_ge(S.masked, w.to(S.masked))
                    v.tensor_reduce(st[:, 0:4], sm, AX_X, ALU.max).then_inc(S.dve_step, 1)
                    v.wait_ge(S.dve_step, w.to(S.dve_step))
                    if sinks is None:
                        v.tensor_scalar(st[:, 0:4], st[:, 0:4], -SCALE, None, ALU.mult).then_inc(S.maxed, 1)
                    else:
                        sk = sinks[:, 4 * u.g:4 * u.g + 4]
                        v.scalar_tensor_tensor(st[:, 0:4], st[:, 0:4], SCALE, sk, ALU.mult, ALU.max).then_inc(S.dve_step, 1)
                        v.wait_ge(S.dve_step, w.to(S.dve_step))
                        v.tensor_scalar(st[:, 0:4], st[:, 0:4], -1.0, None, ALU.mult).then_inc(S.dve_step, 1)
                        v.wait_ge(S.dve_step, w.to(S.dve_step))
                        v.tensor_tensor(st[:, 8:12], st[:, 0:4], sk, ALU.add).then_inc(S.maxed, 1)

                def output(i):
                    u = units[i]
                    st = b.stat[:, i % 4, :]
                    v.wait_ge(S.valued, w.to(S.valued))
                    if sinks is not None:
                        v.tensor_tensor(st[:, 4:8], st[:, 4:8], st[:, 8:12], ALU.add).then_inc(S.dve_step, 1)
                        v.wait_ge(S.dve_step, w.to(S.dve_step))
                    reciprocal(st[:, 12:16], st[:, 4:8])
                    finish(i, u, PS[:, 6 + i % 2, 0:SEQ].rearrange("p (r d) -> p r d", r=4),
                           st[:, 12:16])

                for i in range(len(units)):
                    stats(i)
                    if i >= 2:
                        output(i - 2)
                output(len(units) - 2)
                output(len(units) - 1)
                w.past(S.exped, 2)

            def mixer(l):
                norm()
                take_hT(l)
                v.memset(MB.z[:, :, 0:1], 0.0)
                v.memset(MB.z[:, :, SEQ + 1:SEQ + 2], 0.0)
                for t in range(TT):
                    v.wait_ge(S.act_took, w.to(S.act_took))
                    q = MB.q[:, t, :].rearrange("p (h d) -> p h d", d=DH)
                    rotate(q, q, t, MB.tmp).then_inc(S.dve_took, 1)
                    v.wait_ge(S.dve_took, w.to(S.dve_took))
                v.wait_ge(S.act_took, w.to(S.act_took))
                for t in range(TT):
                    k = MB.kv[:, t, 0:P].rearrange("p (h d) -> p h d", d=DH)
                    rotate(k, k, t, MB.tmp).then_inc(S.dve_took if t else S.dve_step, 1)
                    v.wait_ge(S.dve_took if t else S.dve_step, w.to(S.dve_took if t else S.dve_step))
                w.past(S.projected, 5)
                v.wait_ge(S.act_took, w.to(S.act_took, 2))
                for h in range(2):
                    v.wait_ge(S.projected, w.to(S.projected))
                    i = v.tensor_tensor(MB.z[:, 2 * h:2 * h + 2, 1:SEQ + 1],
                                        PS[:, 1 + h, :].rearrange("p (a b) -> p a b", a=2),
                                        MB.gate_c[:, 2 * h:2 * h + 2, :], ALU.mult)
                    i.then_inc(S.dve_took, 1)
                    v.wait_ge(S.dve_took, w.to(S.dve_took))
                for c in range(4):
                    v.tensor_scalar(MB.cv[:, c, :], MB.z[:, c, 0:SEQ], cw[:, l, 0, c:c + 1], None, ALU.mult).then_inc(S.dve_step, 1)
                    v.wait_ge(S.dve_step, w.to(S.dve_step))
                    for tap in (1, 2):
                        v.scalar_tensor_tensor(MB.cv[:, c, :], MB.z[:, c, tap:tap + SEQ],
                                               cw[:, l, tap, c:c + 1], MB.cv[:, c, :], ALU.mult, ALU.add).then_inc(S.dve_step, 1)
                        v.wait_ge(S.dve_step, w.to(S.dve_step))
                for h in range(2):
                    v.wait_ge(S.projected, w.to(S.projected))
                    i = v.tensor_tensor(MB.yc[:, 2 * h:2 * h + 2, :],
                                        PS[:, 3 + h, :].rearrange("p (a b) -> p a b", a=2),
                                        MB.cv[:, 2 * h:2 * h + 2, :], ALU.mult)
                    i.then_inc(S.dve_took, 1)
                    v.wait_ge(S.dve_took, w.to(S.dve_took))

                def finish(i, u, o, fac):
                    v.tensor_tensor(MB.ya[:, u.t, u.g * 256:(u.g + 1) * 256].rearrange("p (r d) -> p r d", r=4),
                                    o, fac.unsqueeze(2).to_broadcast([P, 4, DH]), ALU.mult).then_inc(S.o_taken, 1)
                    w.past(S.o_taken)

                w.past(S.turned_q, 3)
                attend(mixer_units(), MB, sink[:, l, :], finish)
                for root_sem, o, i, bank in ((S.conv_root, rstdc, rootc, 0), (S.ya_root, rstd, root, 4)):
                    v.wait_ge(root_sem, w.to(root_sem))
                    reciprocal(o, i)
                    v.wait_ge(S.acc_done, w.to(S.acc_done))
                    for t in range(TT):
                        v.scalar_tensor_tensor(x[:, t, :], psum_rows(bank)(t), o[:, t:t + 1], x[:, t, :],
                                               ALU.mult, ALU.add).then_inc(S.x_ready if bank and t else S.dve_step, 1)
                        v.wait_ge(S.x_ready if bank and t else S.dve_step, w.to(S.x_ready if bank and t else S.dve_step))

            def experts(s, f, first, passes, pos, gate):
                f.step = s.step
                iota = const("iota").unsqueeze(1).to_broadcast([P, 2, CAP])

                def tokens_of(e):
                    for t in range(TT):
                        last = v.tensor_tensor(EB.OH[:, t, :].rearrange("p (e s) -> p e s", e=2), iota,
                                               pos[:, t, bass.ds(e, 2)].unsqueeze(2).to_broadcast([P, 2, CAP]),
                                               ALU.is_equal)
                    last.then_inc(s.onehot, 1)
                    v.wait_ge(s.onehot, f.to(s.onehot))

                def low(u):
                    r = (first + u // 2) % RING
                    v.wait_ge(s.high_made, f.to(s.high_made))
                    v.tensor_tensor(split[:, u % SPLIT, 1, :], ring[:, r, (u % 2) * HALF:(u % 2 + 1) * HALF],
                                    split[:, u % SPLIT, 0, :], ALU.subtract).then_inc(s.low_made, 1)

                def low_x(b):
                    v.wait_ge(s.x_high, f.to(s.x_high))
                    at = xs[:, :, 4 * b:4 * b + 4, :].rearrange("p e k s -> p k e s")
                    v.tensor_tensor(at[:, :, :, CAP:], PS[:, 4 + b, :].rearrange("p (k e s) -> p k e s", k=4, e=2),
                                    at[:, :, :, 0:CAP], ALU.subtract).then_inc(s.x_made, 1)

                def hidden():
                    v.wait_ge(s.silu_done, f.to(s.silu_done))
                    v.tensor_tensor(EB.sE, PS[:, 6, 4 * CAP:].rearrange("p (k s) -> p k s", k=4), EB.sE, ALU.mult) \
                        .then_inc(s.step, 1)
                    v.wait_ge(s.step, f.to(s.step))
                    v.tensor_copy(hid[:, :, 0:CAP], EB.sE).then_inc(s.step, 1)
                    v.wait_ge(s.step, f.to(s.step))
                    v.tensor_tensor(hid[:, :, CAP:], EB.sE, hid[:, :, 0:CAP], ALU.subtract).then_inc(s.h_made, 1)

                def one_pair(e, more):
                    low(3)
                    for t in range(TT):
                        for part in range(2):
                            last = v.tensor_tensor(EB.OHg[:, t, :, part * CAP:(part + 1) * CAP],
                                                   EB.OH[:, t, :].rearrange("p (e s) -> p e s", e=2),
                                                   gate[:, t, bass.ds(e, 2)].unsqueeze(2).to_broadcast([P, 2, CAP]),
                                                   ALU.mult)
                    last.then_inc(s.onehot_g, 1)
                    low(4)
                    low(5)
                    v.wait_ge(s.oh_turned, f.to(s.oh_turned))
                    v.tensor_copy(EB.G.rearrange("p a b -> p (a b)"), PS[:, 7, :]).then_inc(s.g_taken, 1)
                    low(6)
                    hidden()
                    low(7)
                    tokens_of(e + 2)
                    for u in (8, 9, 10, 11):
                        low(u)
                    if more:
                        low(12)
                    hidden()
                    low_x(0)
                    if more:
                        low(13)
                    low_x(1)
                    if more:
                        low(14)

                tokens_of(0)
                low(0)
                low(1)
                low(2)
                low_x(0)
                low_x(1)
                with v.Fori(0, passes - 1) as p:
                    f.enter(p, {s.high_made: UNITS, s.onehot: 1, s.x_high: 2, s.oh_turned: 1, s.silu_done: 2,
                                s.step: 4})
                    one_pair(2 * p, True)
                    f.leave(passes - 1)
                one_pair(2 * (passes - 1), False)
                v.wait_ge(s.combined, f.to(s.combined, passes))
                for t in range(TT):
                    last = v.tensor_tensor(x[:, t, :], psum_rows(0)(t), x[:, t, :], ALU.add)
                return last

            def first_best(vals, n, key, best, hot, tie, top):
                v.tensor_reduce(top, vals, AX_X, ALU.max).then_inc(S.dve_step, 1)
                v.wait_ge(S.dve_step, w.to(S.dve_step))
                v.tensor_tensor(key, vals, top.unsqueeze(2).to_broadcast([P, TT, n]), ALU.is_equal).then_inc(S.dve_step, 1)
                v.wait_ge(S.dve_step, w.to(S.dve_step))
                v.tensor_tensor(key, key, tie.unsqueeze(1).to_broadcast([P, TT, n]), ALU.mult).then_inc(S.dve_step, 1)
                v.wait_ge(S.dve_step, w.to(S.dve_step))
                v.tensor_reduce(best, key, AX_X, ALU.max).then_inc(S.dve_step, 1)
                v.wait_ge(S.dve_step, w.to(S.dve_step))
                v.tensor_tensor(hot, key, best.unsqueeze(2).to_broadcast([P, TT, n]), ALU.is_equal).then_inc(S.dve_step, 1)
                v.wait_ge(S.dve_step, w.to(S.dve_step))

            def moe(l):
                norm(gain=gain_rows())
                take_hT(None)
                B = EB
                tie = const("tie")
                gm, gs, pg, m1, d, e2, m2, g1, g2, best = (B.s[:, i, :] for i in (0, 1, 2, 3, 4, 5, 6, 7, 8, 9))

                def over(ap, n):
                    return ap.unsqueeze(2).to_broadcast([P, TT, n])

                v.wait_ge(S.routed, w.to(S.routed))
                v.tensor_tensor(B.lg, PS[:, 4, 0:P].rearrange("p (t n) -> p t n", t=TT)[:, :, 0:NG + NE],
                                rbias[:, l, :].unsqueeze(1).to_broadcast([P, TT, NG + NE]), ALU.add).then_inc(S.dve_step, 1)
                v.wait_ge(S.dve_step, w.to(S.dve_step))
                gl, el = B.lg[:, :, 0:NG], B.lg[:, :, NG:]
                first_best(gl, NG, B.gk, best, B.gh, tie[:, 0:NG], gm)
                v.tensor_tensor(B.gd, gl, over(gm, NG), ALU.subtract).then_inc(S.gate_e, 1)
                v.tensor_scalar(B.gk, B.gh, 1.0, BIG, ALU.subtract, ALU.mult).then_inc(S.dve_step, 1)
                v.wait_ge(S.dve_step, w.to(S.dve_step))
                for t in range(TT):
                    last = v.tensor_tensor(B.el[:, t, :].rearrange("p (g e) -> p g e", g=NG),
                                           el[:, t, :].rearrange("p (g e) -> p g e", g=NG),
                                           B.gk[:, t, :].unsqueeze(2).to_broadcast([P, NG, NE // NG]), ALU.add)
                last.then_inc(S.dve_step, 1)
                v.wait_ge(S.dve_step, w.to(S.dve_step))
                first_best(B.el, NE, B.key, best, B.oh1, tie[:, NG:], m1)
                v.scalar_tensor_tensor(B.el3, B.oh1, -2 * BIG, B.el, ALU.mult, ALU.add).then_inc(S.dve_step, 1)
                v.wait_ge(S.dve_step, w.to(S.dve_step))
                first_best(B.el3, NE, B.key, best, B.oh2, tie[:, NG:], m2)
                v.tensor_tensor(B.mk, B.oh1, B.oh2, ALU.add).then_inc(S.marked, 1)
                v.wait_ge(S.marked, w.to(S.marked))
                v.tensor_tensor(d, m2, m1, ALU.subtract).then_inc(S.gate_e, 1)
                v.wait_ge(S.gate_exp, w.to(S.gate_exp))
                v.tensor_reduce(gs, B.ge, AX_X, ALU.add).then_inc(S.dve_step, 1)
                v.wait_ge(S.dve_step, w.to(S.dve_step))
                reciprocal(pg, gs)
                v.wait_ge(S.gate_exp, w.to(S.gate_exp))
                v.tensor_scalar(g1, e2, 1.0, None, ALU.add).then_inc(S.dve_step, 1)
                v.wait_ge(S.dve_step, w.to(S.dve_step))
                reciprocal(g2, g1)
                v.tensor_tensor(g1, g2, pg, ALU.mult).then_inc(S.dve_step, 1)
                v.wait_ge(S.dve_step, w.to(S.dve_step))
                v.tensor_tensor(g2, g1, e2, ALU.mult).then_inc(S.dve_step, 1)
                v.wait_ge(S.dve_step, w.to(S.dve_step))
                v.memset(B.gate[:, :, NE:NE + 2], 0.0).then_inc(S.dve_step, 1)
                v.wait_ge(S.dve_step, w.to(S.dve_step))
                v.memset(B.pos[:, :, NE:NE + 2], FAR).then_inc(S.dve_step, 1)
                v.wait_ge(S.dve_step, w.to(S.dve_step))
                v.tensor_tensor(B.oh1, B.oh1, over(g1, NE), ALU.mult).then_inc(S.dve_step, 1)
                v.wait_ge(S.dve_step, w.to(S.dve_step))
                v.tensor_tensor(B.oh2, B.oh2, over(g2, NE), ALU.mult).then_inc(S.dve_step, 1)
                v.wait_ge(S.dve_step, w.to(S.dve_step))
                v.tensor_tensor(B.gate[:, :, 0:NE], B.oh1, B.oh2, ALU.add).then_inc(S.dve_step, 1)
                v.wait_ge(S.dve_step, w.to(S.dve_step))
                v.tensor_scalar(B.key, B.mk, -FAR, FAR, ALU.mult, ALU.add).then_inc(S.dve_step, 1)
                v.wait_ge(S.dve_step, w.to(S.dve_step))
                v.wait_ge(S.ranked, w.to(S.ranked))
                v.tensor_tensor(B.pos[:, :, 0:NE], PS[:, 5, 0:2 * NE].rearrange("p (t n) -> p t n", t=TT),
                                B.key, ALU.add).then_inc(S.dve_step, 1)
                v.wait_ge(S.dve_step, w.to(S.dve_step))
                v.tensor_reduce(flag_f[:, :], PS[:, 5, 2 * NE:3 * NE], AX_X, ALU.max).then_inc(S.dve_step, 1)
                v.wait_ge(S.dve_step, w.to(S.dve_step))
                v.tensor_copy(flag[:, :], flag_f[:, :]).then_inc(S.flag_ready, 1)
                v.wait_ge(S.flag_ready, w.to(S.flag_ready))
                experts(M, w, first_slot(f"moe{l}"), PAIRS, B.pos, B.gate).then_inc(S.moe_added, 1)
                v.wait_ge(S.moe_added, w.to(S.moe_added))
                w.step = S.dve_step
                most = v.value_load(flag[0:1, 0:1], min_val=0, max_val=SEQ)
                with v.If(most > CAP):
                    f = Follow(OV[l].step)
                    v.memset(B.gatev[:, :, MORE * NE:], 0.0).then_inc(f.step, 1)
                    v.wait_ge(f.step, f.to(f.step))
                    v.memset(B.posv[:, :, MORE * NE:], FAR).then_inc(f.step, 1)
                    v.wait_ge(f.step, f.to(f.step))
                    for r in range(MORE):
                        v.tensor_copy(B.gatev[:, :, r * NE:(r + 1) * NE], B.gate[:, :, 0:NE]).then_inc(f.step, 1)
                        v.wait_ge(f.step, f.to(f.step))
                        v.tensor_scalar(B.posv[:, :, r * NE:(r + 1) * NE], B.pos[:, :, 0:NE],
                                        float(CAP * (r + 1)), None, ALU.subtract).then_inc(f.step, 1)
                        v.wait_ge(f.step, f.to(f.step))
                    experts(OV[l], f, first_slot(f"moe{l}"), MORE * PAIRS, B.posv, B.gatev).then_inc(f.step, 1)
                    v.wait_ge(f.step, f.to(f.step))
                v.tensor_copy(flag_f[:, :], rstd[:, 0:1]).then_inc(S.x_ready, 1)
                v.wait_ge(S.x_ready, w.to(S.x_ready))

            FG = {"ffn00": 2, "ffn01": 3, "ffn10": 4, "ffn11": 6}

            def ffn(gain):
                norm()
                take_hT(gain)

                def run(n):
                    for i in range(n):
                        v.wait_ge(S.ffn_silu, w.to(S.ffn_silu))
                        v.tensor_tensor(FB.hF[:, i % 4, :], PS[:, 4 + i % 4, SEQ:2 * SEQ], FB.sF[:, i % 2, :],
                                        ALU.mult).then_inc(S.ffn_h, 1)

                with v.Fori(0, 2) as p:
                    w.enter(p, {S.ffn_silu: 8})
                    run(8)
                    w.leave(2)
                run(6)
                w.past(S.acc_done)
                post(psum_rows(0), 0.5)

            def pool_mix():
                norm(permute=False)
                take_hT(7)
                scale = gain_rows()
                v.wait_ge(S.acc_done, w.to(S.acc_done))
                for t in range(TT):
                    v.tensor_tensor(pool_f[:, t, :], psum_rows(0)(t), scale, ALU.mult).then_inc(S.scaled, 1)
                    v.wait_ge(S.scaled, w.to(S.scaled))
                post(lambda t: pool_f[:, t, :], 1.0)

            def nsa():
                norm()
                take_hT(5)
                w.past(S.projected, 11)
                for gp in range(2):
                    for t in range(TT):
                        v.wait_ge(S.act_took, w.to(S.act_took))
                        q = NB.qn[:, t, gp * 512:(gp + 1) * 512].rearrange("p (h d) -> p h d", d=DH)
                        r = NB.qr[:, t, gp * 512:(gp + 1) * 512].rearrange("p (h d) -> p h d", d=DH)
                        v.tensor_copy(r[:, :, ROPE:DH], q[:, :, ROPE:DH])
                        rotate(q, r, t, NB.tmp).then_inc(S.dve_took, 1)
                        v.wait_ge(S.dve_took, w.to(S.dve_took))
                w.past(S.act_took, 2)
                for br in range(2):
                    for t in range(TT):
                        v.wait_ge(S.act_took, w.to(S.act_took))
                        k = NB.kv[br][:, t, 0:256].rearrange("p (h d) -> p h d", d=DH)
                        rotate(k, k, t, NB.tmp).then_inc(S.dve_took, 1)
                        v.wait_ge(S.dve_took, w.to(S.dve_took))
                v.memset(NB.Vbd, 0.0)
                v.memset(NB.P32, 0.0).then_inc(S.dve_step, 1)
                v.wait_ge(S.dve_step, w.to(S.dve_step))
                w.past(S.turned_q, 4)
                for t in range(TT):
                    for gp in range(2):
                        v.wait_ge(S.turned_q, w.to(S.turned_q))
                        v.tensor_copy(NB.qrT[:, 4 * gp:4 * gp + 4, t * P:(t + 1) * P],
                                      PS[:, 4 + 2 * t + gp, :].rearrange("p (m q) -> p m q", m=4)) \
                            .then_inc(S.q_turned_dve, 1)
                v.wait_ge(S.turned_q, w.to(S.turned_q))
                for g in range(4):
                    for r in range(2):
                        for h in range(2):
                            last = v.tensor_copy(*z_view(0, g, r, h))
                last.then_inc(S.dve_step, 1)
                v.wait_ge(S.dve_step, w.to(S.dve_step))
                for s in range(2):
                    if s:
                        v.wait_ge(S.z_built, w.to(S.z_built))
                    v.tensor_tensor(NB.Z[s], NB.Z[s], cpos[:, s, :].unsqueeze(2).to_broadcast([P, 16, 60]),
                                    ALU.add).then_inc(S.z_pos, 1)
                w.past(S.turned_q, 3)
                v.wait_ge(S.compressed, w.to(S.compressed))
                v.tensor_copy(NB.KC, PS[:, 6, 0:60])
                for r in range(4):
                    last = v.tensor_copy(NB.Vbd[32 * r:32 * r + NCMP, :, r * DH:(r + 1) * DH],
                                         PS[0:NCMP, 7, 0:256].rearrange("p (g d) -> p g d", g=4))
                last.then_inc(S.kc_ready, 1)
                mask, some = const("cmp_mask"), const("cmp_any")
                for t in range(TT):
                    v.wait_ge(S.cscored, w.to(S.cscored))
                    for g in range(4):
                        last = v.tensor_tensor(NB.Sc[t][:, 4 * g:4 * g + 4, :],
                                               PS[:, 2 * t + g % 2, 64 * g:64 * g + 64]
                                               .rearrange("p (h n) -> p h n", h=4)[:, :, 0:NCMP],
                                               mask[:, t * NCMP:(t + 1) * NCMP].unsqueeze(1)
                                               .to_broadcast([P, 4, NCMP]), ALU.add)
                    last.then_inc(S.dve_step, 1)
                    v.wait_ge(S.dve_step, w.to(S.dve_step))
                    v.tensor_reduce(NB.cs[:, t, :], NB.Sc[t], AX_X, ALU.max).then_inc(S.dve_step, 1)
                    v.wait_ge(S.dve_step, w.to(S.dve_step))
                    v.tensor_tensor(NB.Sc[t], NB.Sc[t], NB.cs[:, t, :].unsqueeze(2)
                                    .to_broadcast([P, 16, NCMP]), ALU.subtract).then_inc(S.csub, 1)
                    v.wait_ge(S.csub, w.to(S.csub))
                v.wait_ge(S.act_took, w.to(S.act_took))
                for t in range(TT):
                    v.wait_ge(S.cexp, w.to(S.cexp))
                    cs = NB.cs[:, 2 + 2 * t, :]
                    fac = NB.cs[:, 3 + 2 * t, :]
                    v.tensor_reduce(cs, NB.Sc[t], AX_X, ALU.add).then_inc(S.dve_step, 1)
                    v.wait_ge(S.dve_step, w.to(S.dve_step))
                    reciprocal(fac, cs)
                    v.scalar_tensor_tensor(fac, fac, some[:, t:t + 1], NB.gts[:, t, 0:16], ALU.mult, ALU.mult).then_inc(S.dve_step, 1)
                    v.wait_ge(S.dve_step, w.to(S.dve_step))
                    v.tensor_tensor(NB.P32[:, t, :, 0:NCMP], NB.Sc[t], fac.unsqueeze(2)
                                    .to_broadcast([P, 16, NCMP]), ALU.mult).then_inc(S.p_ready, 1)
                v.wait_ge(S.o_first, w.to(S.o_first, 2))
                units = nsa_units()

                def finish(i, u, o, fac):
                    lo = (1 + u.br) * 16 + 4 * u.g
                    v.tensor_tensor(fac, fac, NB.gts[:, u.t, lo:lo + 4], ALU.mult).then_inc(S.dve_step, 1)
                    v.wait_ge(S.dve_step, w.to(S.dve_step))
                    tmp = NB.tmp.rearrange("p (r d) -> p r d", r=4)
                    v.tensor_tensor(tmp, o, fac.unsqueeze(2).to_broadcast([P, 4, DH]), ALU.mult).then_inc(S.o_taken, 1)
                    v.wait_ge(S.o_taken, w.to(S.o_taken))
                    dst = hp[:, u.t, u.g * 256:(u.g + 1) * 256]
                    add = v.tensor_tensor(dst, dst, NB.tmp, ALU.add)
                    if i >= len(units) - 2:
                        add.then_inc(S.h_ready, 1)
                    else:
                        add.then_inc(S.dve_step, 1)
                        v.wait_ge(S.dve_step, w.to(S.dve_step))

                attend(units, NB, None, finish)
                take_hT(None)
                w.past(S.acc_done)
                post(psum_rows(4), 1.0)

            v.memset(epsb[:, :], EPS).then_inc(S.set_up, 1)
            v.memset(zeros, 0.0).then_inc(S.set_up, 1)
            v.wait_ge(S.x_loaded, w.to(S.x_loaded, 16))
            v.wait_ge(S.const_loaded, w.to(S.const_loaded, 16))
            v.wait_ge(S.param_loaded, PARAMS)
            for name in stages:
                if name[:3] == "mix":
                    mixer(int(name[3]))
                elif name[:3] == "moe":
                    moe(int(name[3]))
                elif name == "final":
                    gain = gain_rows()
                    v.wait_ge(S.root_ready, w.to(S.root_ready))
                    reciprocal(rstd, root)
                    for t in range(TT):
                        v.scalar_tensor_tensor(x[:, t, :], x[:, t, :], rstd[:, t:t + 1], gain,
                                               ALU.mult, ALU.mult).then_inc(S.x_ready if t else S.dve_step, 1)
                        v.wait_ge(S.x_ready if t else S.dve_step, w.to(S.x_ready if t else S.dve_step))
                elif name[:3] == "ffn":
                    ffn(FG[name])
                elif name == "pool":
                    pool_mix()
                elif name == "nsa":
                    nsa()


NAMES = ["x", "norm_mix", "w_in", "attn_sink", "conv_w", "norm_attn_out", "norm_conv_out", "w_out", "norm_ffn",
         "w_router_group", "b_router_group", "w_router_expert", "b_router_expert", "w_expert_gate", "w_expert_up",
         "w_expert_down", "norm_final", "norm_gains_2", "ffn_w_gate_2", "ffn_w_up_2", "ffn_w_down_2", "pool_w_2",
         "pool_b_2", "pool_scale_2", "nsa_w_in_2", "nsa_cmp_pos_k_2", "nsa_cmp_pos_v_2", "nsa_cmp_wk1_2",
         "nsa_cmp_wk2_2", "nsa_cmp_wv1_2", "nsa_cmp_wv2_2", "nsa_w_o_2"]


def kernel(**inputs):
    import concourse.bacc as bacc
    from concourse.bass_utils import run_bass_kernel_spmd

    nc = bacc.Bacc("TRN2", target_bir_lowering=False, num_devices=1)
    table, means = constants()
    arrays = {name: np.ascontiguousarray(inputs[name]) for name in NAMES}
    arrays["consts"], arrays["means"] = table, means
    aps = {}
    feed = {}
    for name, v in arrays.items():
        feed[f"in_{name}"] = v
        aps[name] = nc.dram_tensor(f"in_{name}", v.shape, mybir.dt.from_np(v.dtype), kind="ExternalInput").ap()
    out = nc.dram_tensor("out_x", (1, SEQ, D), F32, kind="ExternalOutput").ap()
    build(nc, aps, out, STAGES)
    r = run_bass_kernel_spmd(nc, [feed], core_ids=[0])
    return r.results[0]["out_x"]
```

```python
from contextlib import ExitStack

import numpy as np

import concourse.bass as bass
from concourse import mybir

F32 = mybir.dt.float32
F32R = mybir.dt.float32r
I32 = mybir.dt.int32
ALU = mybir.AluOpType
ACT = mybir.ActivationFunctionType
AX_X = mybir.AxisListType.X

P = 128
SEQ, D = 256, 1024
TT = SEQ // P
KT = D // P
EPS = 1e-6
DH = 64
SCALE = DH ** -0.5
BIG = 1e30
NE, NG = 32, 4
DE = 512
CAP = 64
PAIRS = NE // 2
MORE = SEQ // CAP - 1
FAR = 1e4
FF = 2816
NCMP = 15
ROPE = 16
THETA = 500000.0
RING = 6
HALF = 2048
SPLIT = 3
LOW_V = 1408
UNITS = 2 * RING
BLOCK = 256
BLOCKS = FF // BLOCK
WORK = 16928
STAGES = ["mix0", "moe0", "mix1", "moe1", "final", "ffn00", "pool", "ffn01", "ffn10", "nsa", "ffn11"]

LOADS = {"mix": 7, "moe": RING * PAIRS, "fin": 0, "ffn": 18, "poo": 1, "nsa": 10}

CONSTS = {}
_at = 0
for _n, _w in (("ident", P), ("upper", P), ("ones", P), ("fold", CAP), ("iota", CAP), ("tie", NG + NE), ("rope_c", TT * ROPE),
               ("rope_s", TT * ROPE), ("band", TT * SEQ), ("causal", SEQ), ("cmp_mask", TT * NCMP), ("cmp_any", TT)):
    CONSTS[_n] = (_at, _at + _w)
    _at += _w
N_CONSTS = _at


def constants():
    c = np.zeros((P, N_CONSTS), np.float32)

    def put(name, a):
        lo, hi = CONSTS[name]
        c[:, lo:hi] = np.asarray(a, np.float32).reshape(P, -1)

    i = np.arange(P)
    tok = i[:, None] + P * np.arange(TT)[None, :]
    put("ident", np.eye(P))
    put("upper", i[:, None] < i[None, :])
    put("ones", np.ones((P, P)))
    put("fold", i[:, None] % CAP == np.arange(CAP)[None, :])
    put("iota", np.broadcast_to(np.arange(CAP), (P, CAP)))
    put("tie", np.broadcast_to(np.concatenate([np.arange(NG, 0, -1), np.arange(NE, 0, -1)]), (P, NG + NE)))
    inv = np.float32(THETA) ** (-np.arange(0, ROPE, 2, dtype=np.float32) / np.float32(ROPE))
    ang = tok.astype(np.float32)[:, :, None] * inv.astype(np.float32)
    cos, sin = np.cos(ang), np.sin(ang)
    put("rope_c", np.concatenate([cos, cos], -1))
    put("rope_s", np.concatenate([-sin, sin], -1))
    keys = np.arange(SEQ)
    put("band", np.where(np.abs(keys[None, None, :] - tok[:, :, None]) <= 128, 0.0, -BIG))
    put("causal", np.where(keys[None, :] <= P + i[:, None], 0.0, -BIG))
    ends = np.arange(NCMP) * 16 + 31
    ok = ends[None, None, :] <= tok[:, :, None]
    put("cmp_mask", np.where(ok, 0.0, -BIG))
    put("cmp_any", ok.any(-1))
    q = np.arange(SEQ)
    means = np.zeros((SEQ, 4, SEQ), np.float32)
    for n, w in enumerate((2, 4, 8, 16)):
        gap = q[None, :] - q[:, None]
        means[:, n, :] = ((gap >= 0) & (gap < w)) / np.minimum(q + 1, w)[None, :] - (gap == 0)
    return c, means.astype(np.float32)


class Fields:
    pass


class Unit:

    def __init__(self, t, g, half, gp, tile, br, nk, qT, kT, v, mask):
        self.t, self.g, self.half, self.gp, self.tile, self.br, self.nk = t, g, half, gp, tile, br, nk
        self.qT, self.kT, self.v, self.mask = qT, kT, v, mask


class Follow:

    def __init__(self, step=None):
        self.step, self.n, self.p, self.per = step, {}, None, {}

    def past(self, sem, k=1):
        self.n[sem.name] = (sem, self.n.get(sem.name, (sem, 0))[1] + k)

    def to(self, sem, k=1):
        self.past(sem, k)
        v = self.n[sem.name][1]
        if self.p is not None:
            v = self.p * self.per[sem.name] + (v - self.per[sem.name] * self.first)
        return v

    def after(self, sem, k):
        return self.n.get(sem.name, (sem, 0))[1] + k

    def enter(self, p, per, first=0):
        self.p, self.per, self.first = p, {s.name: k for s, k in per.items()}, first
        self.was = {k: v for k, v in self.n.items()}

    def leave(self, passes):
        got = {k: v[1] - self.was.get(k, (0, 0))[1] for k, v in self.n.items()}
        got = {k: v for k, v in got.items() if v}
        want = {k: v for k, v in self.per.items() if v}
        assert got == want, (got, want)
        for k, v in got.items():
            self.n[k] = (self.n[k][0], self.n[k][1] + v * (passes - 1))
        self.p = None


def build(nc, a, out, stages):
    ctx = ExitStack()
    with ctx:
        def sb(name, shape, dt=F32):
            return ctx.enter_context(nc.sbuf_tensor(name, shape, dt))

        def sem(name):
            return ctx.enter_context(nc.semaphore(name))

        PS = ctx.enter_context(nc.psum_tensor("PS", [P, 8, 512], F32))

        ring = sb("ring", [P, RING, 4096])
        x = sb("x", [P, TT, D])
        hp = sb("hp", [P, TT, D])
        hT = sb("hT", [P, KT, SEQ])
        hT_at = nc.sbuf_base - 4 * KT * SEQ
        gB = sb("gB", [P, 2, D])
        gB_at = nc.sbuf_base - 4 * 2 * D
        cst = sb("cst", [P, N_CONSTS])
        work = sb("work", [P, WORK])
        work_at = nc.sbuf_base - 4 * WORK
        split = nc.alloc_sbuf_tensor_at("split", [P, SPLIT, 2, HALF], F32R, offset=work_at)
        S_COLS = SPLIT * 2 * HALF
        hid = nc.alloc_sbuf_tensor_at("hid", [P, 4, 2 * CAP], F32R, offset=work_at + 4 * S_COLS)
        H_COLS = 4 * 2 * CAP
        hT_high = nc.alloc_sbuf_tensor_at("hT_high", [P, KT, SEQ], F32R, offset=hT_at)
        hT_low = nc.alloc_sbuf_tensor_at("hT_low", [P, KT, SEQ], F32R, offset=work_at + 4 * S_COLS)
        ffn_hid = nc.alloc_sbuf_tensor_at("ffn_hid", [P, 2, 2, SEQ], F32R,
                                          offset=work_at + 4 * (S_COLS + KT * SEQ))
        xs = nc.alloc_sbuf_tensor_at("xs", [P, 2, KT, 2 * CAP], F32R, offset=hT_at)
        gT = sb("gT", [P, 9, KT])
        cw = sb("cw", [P, 2, 3, 4])
        gaT = sb("gaT", [P, 2, 4])
        gcT = sb("gcT", [P, 2, 4])
        wr = sb("wr", [P, 2, KT, NG + NE])
        rbias = sb("rbias", [P, 2, NG + NE])
        sink = sb("sink", [P, 2, 8])
        zeros = sb("zeros", [1, P])[:, :]
        w2k = sb("w2k", [P, 2, 2 * DH])
        w2v = sb("w2v", [P, 2, DH])
        cpos = sb("cpos", [P, 2, 16])
        small = sb("small", [P, 64])
        epsb = sb("epsb", [P, 1])
        flag_f = sb("flag_f", [P, 1])
        flag = sb("flag", [P, 2], I32)

        def const(name, parts=P):
            lo, hi = CONSTS[name]
            return cst[0:parts, lo:hi]

        ident, upper, ones = const("ident"), const("upper"), const("ones")
        ss, root, rstd = small[:, 0:2], small[:, 2:4], small[:, 4:6]
        ssc, rootc, rstdc = small[:, 6:8], small[:, 8:10], small[:, 10:12]

        class Carve:
            def __init__(self, start=0):
                self.at = start

            def __call__(self, *shape):
                n = int(np.prod(shape))
                v = work[:, self.at:self.at + n]
                self.at += n
                assert self.at <= WORK, self.at
                if len(shape) == 2:
                    v = v.rearrange("p (a b) -> p a b", a=shape[0])
                if len(shape) == 3:
                    v = v.rearrange("p (a b c) -> p a b c", a=shape[0], b=shape[1])
                return v

        S = Fields()
        S.set_up = sem("set_up")
        S.const_loaded = sem("const_loaded")
        S.x_loaded = sem("x_loaded")
        S.mix_param_loaded = sem("mix_param_loaded")
        S.param_loaded = sem("param_loaded")
        S.means_loaded = sem("means_loaded")
        S.x_stored = sem("x_stored")
        S.dve_step = sem("dve_step")
        S.act_step = sem("act_step")
        S.x_ready = sem("x_ready")
        S.root_ready = sem("root_ready")
        S.h_ready = sem("h_ready")
        S.hT_psum = sem("hT_psum")
        S.hT_even = sem("hT_even")
        S.hT_odd = sem("hT_odd")
        S.projected = sem("projected")
        S.act_took = sem("act_took")
        S.dve_took = sem("dve_took")
        S.turned_q = sem("turned_q")
        S.q_turned_act = sem("q_turned_act")
        S.q_turned_dve = sem("q_turned_dve")
        S.scored = sem("scored")
        S.masked = sem("masked")
        S.maxed = sem("maxed")
        S.exped = sem("exped")
        S.turned = sem("turned")
        S.turned_taken = sem("turned_taken")
        S.valued = sem("valued")
        S.o_taken = sem("o_taken")
        S.conv_gain = sem("conv_gain")
        S.conv_ss = sem("conv_ss")
        S.conv_root = sem("conv_root")
        S.ya_root = sem("ya_root")
        S.ya_psum = sem("ya_psum")
        S.yaT_ready = sem("yaT_ready")
        S.half_done = sem("half_done")
        S.acc_done = sem("acc_done")
        S.routed = sem("routed")
        S.gate_e = sem("gate_e")
        S.gate_exp = sem("gate_exp")
        S.marked = sem("marked")
        S.ranked = sem("ranked")
        S.flag_ready = sem("flag_ready")
        S.moe_added = sem("moe_added")
        S.ffn_high = sem("ffn_high")
        S.ffn_low = sem("ffn_low")
        S.ffn_used = sem("ffn_used")
        S.ffn_silu = sem("ffn_silu")
        S.ffn_step = sem("ffn_step")
        S.ffn_h = sem("ffn_h")
        S.hT_low = sem("hT_low")
        S.scaled = sem("scaled")
        S.z_built = sem("z_built")
        S.z_pos = sem("z_pos")
        S.hidden = sem("hidden")
        S.hc_ready = sem("hc_ready")
        S.compressed = sem("compressed")
        S.kc_ready = sem("kc_ready")
        S.cscored = sem("cscored")
        S.csub = sem("csub")
        S.cexp = sem("cexp")
        S.p_ready = sem("p_ready")
        S.p_turned = sem("p_turned")
        S.pT_ready = sem("pT_ready")
        S.cvalued = sem("cvalued")
        S.o_first = sem("o_first")
        S.gB_loaded = [sem(f"gB_loaded{i}") for i in range(2)]
        S.loaded = [sem(f"ring_loaded{i}") for i in range(RING)]

        def expert_sems(tag, loaded=None):
            s = Fields()
            s.high_made = sem(f"high_made_{tag}")
            s.low_made = sem(f"low_made_{tag}")
            s.low_rest = sem(f"low_rest_{tag}")
            s.half_used = sem(f"half_used_{tag}")
            s.gathered = sem(f"gathered_{tag}")
            s.x_high = sem(f"x_high_{tag}")
            s.x_made = sem(f"x_made_{tag}")
            s.gu_taken = sem(f"gu_taken_{tag}")
            s.gu_turned = sem(f"gu_turned_{tag}")
            s.silu_done = sem(f"silu_done_{tag}")
            s.h_made = sem(f"h_made_{tag}")
            s.y_high = sem(f"y_high_{tag}")
            s.y_made = sem(f"y_made_{tag}")
            s.oh_turned = sem(f"oh_turned_{tag}")
            s.g_taken = sem(f"g_taken_{tag}")
            s.combined = sem(f"combined_{tag}")
            s.onehot = sem(f"onehot_{tag}")
            s.onehot_g = sem(f"onehot_g_{tag}")
            s.step = sem(f"step_{tag}")
            s.loaded = loaded or [sem(f"ring_loaded{i}_{tag}") for i in range(RING)]
            return s

        M = expert_sems("moe", S.loaded)
        OV = {l: expert_sems(f"more{l}") for l in range(2) if f"moe{l}" in stages}

        def mixer_views():
            c = Carve()
            b = Fields()
            b.q, b.kv = c(TT, 512), c(TT, 256)
            b.v = b.kv[:, :, P:256]
            b.qT, b.kT = c(4, SEQ), c(1, SEQ)
            b.ya, b.yc = c(TT, 512), c(4, SEQ)
            b.tmp = c(256)
            b.stat = c(4, 16)
            b.z = c(4, SEQ + 2)
            b.P = [c(4, SEQ) for _ in range(2)]
            b.Sm = [c(4, SEQ) for _ in range(2)]
            b.PT = [c(2, 4, P) for _ in range(2)]
            b.sq = hp[:, 0, :].rearrange("p (a b) -> p a b", a=4)
            b.gate_c = hp[:, 1, :].rearrange("p (a b) -> p a b", a=4)
            b.cv = b.P[0]
            b.yaT = b.Sm[0]
            b.junk = b.Sm[1]
            return b

        MB = mixer_views()

        def moe_views():
            c = Carve(S_COLS + H_COLS)
            b = Fields()
            top = c.at
            b.gu = c(2, DE)
            b.sE = c(4, CAP)
            b.gs = c(8)
            b.OH = c(TT, P)
            c.at += 2 * SEQ
            c.at += D
            b.OHg = c(TT, 2, P)
            b.pos = c(TT, NE + 2)
            b.gate = c(TT, NE + 2)
            b.posv = c(TT, MORE * NE + 2)
            b.gatev = c(TT, MORE * NE + 2)
            c.at = top
            b.lg = c(TT, NG + NE)
            b.gd, b.ge, b.gh, b.gk = c(TT, NG), c(TT, NG), c(TT, NG), c(TT, NG)
            b.el, b.el3, b.key = c(TT, NE), c(TT, NE), c(TT, NE)
            b.oh1, b.oh2, b.mk = c(TT, NE), c(TT, NE), c(TT, NE)
            b.s = c(12, TT)
            return b

        EB = moe_views()
        marks_at = work_at + 4 * (S_COLS + H_COLS + 2 * DE + 4 * CAP + 8 + TT * P)
        marks = nc.alloc_sbuf_tensor_at("marks", [P, 2, SEQ], F32R, offset=marks_at)
        y_high = [nc.alloc_sbuf_tensor_at(f"y_high{l}", [P, 2, 512], F32R, offset=gB_at + 4 * D * l) for l in range(2)]
        y_low = nc.alloc_sbuf_tensor_at("y_low", [P, 2, 512], F32R, offset=marks_at + 4 * 2 * SEQ)

        def ffn_views():
            c = Carve(S_COLS + KT * SEQ + 2 * 2 * SEQ)
            b = Fields()
            b.sF = c(2, SEQ)
            return b

        FB = ffn_views()
        pool_means = work[:, 0:2048].rearrange("p (a b c) -> p a b c", a=TT, b=4)
        pool_f = work[:, 2048:4096].rearrange("p (a b) -> p a b", a=TT)
        pbias = work[0:1, 4096:4096 + D]

        def nsa_views():
            c = Carve()
            b = Fields()
            b.qnT, b.qrT = c(8, SEQ), c(8, SEQ)
            b.kT = [c(2, SEQ) for _ in range(2)]
            b.kv = [c(TT, 512) for _ in range(2)]
            b.v = [kv[:, :, 256:512] for kv in b.kv]
            b.gts = c(TT, 48)
            b.tmp = c(256)
            b.stat = c(4, 16)
            b.KC = c(60)
            b.Vbd = c(4, 256)
            b.hc = c(2, 120)
            b.Sc = [c(16, NCMP) for _ in range(2)]
            b.cs = c(6, 16)
            top = c.at
            b.qn, b.qr = c(TT, D), c(TT, D)
            b.kvc = c(TT, 512)
            c.at = top
            b.P = [c(4, SEQ) for _ in range(2)]
            b.Sm = [c(4, SEQ) for _ in range(2)]
            b.PT = [c(2, 4, P) for _ in range(2)]
            b.PcT = b.PT[0]
            b.P32 = b.PT[1].rearrange("p a b c -> p (a b c)").rearrange("p (t h n) -> p t h n", t=TT, h=16)
            b.Z = [hp[:, s, 0:960].rearrange("p (a b) -> p a b", a=16) for s in range(2)]
            return b

        NB = nsa_views()

        def z_view(s, g, r, h):
            src = PS[DH * (g % 2):DH * (g % 2 + 1), s, (g // 2) * SEQ:(g // 2 + 1) * SEQ]
            src = src.rearrange("p (n j r) -> p r j n", j=8, r=2)[:, r, :, h:h + NCMP]
            return NB.Z[s][DH * r:DH * (r + 1), 8 * h:8 * h + 8, g * NCMP:(g + 1) * NCMP], src

        def mixer_units():
            return [Unit(t=t, g=g, half=g, gp=0, tile=0, br=0, nk=2, qT=MB.qT, kT=MB.kT, v=MB.v,
                                    mask=const("band")[:, t * SEQ:(t + 1) * SEQ])
                    for t in range(TT) for g in range(2)]

        def nsa_units():
            return [Unit(t=t, g=g, half=g % 2, gp=g // 2, tile=4 * (g // 2), br=br, nk=t + 1,
                                    qT=NB.qrT, kT=NB.kT[br], v=NB.v[br],
                                    mask=const("causal")[:, P * (1 - t):SEQ])
                    for br in range(2) for t in range(TT) for g in range(4)]

        def buffer_of(b, kind):
            if kind == "down":
                return 1 if b < BLOCKS - 1 else 2
            if kind == "gate":
                return 2 if b else 0
            return 0 if b else 1

        def half_of(first, b, kind):
            r = (first + 3 * (b // 2) + ("gate", "up", "down").index(kind)) % RING
            if kind == "down":
                return ring[:, r, (b % 2) * HALF:(b % 2 + 1) * HALF].rearrange("p (k n) -> p k n", k=KT), r
            width = min(512, FF - (b // 2) * 512)
            src = ring[:, r, 0:KT * width].rearrange("p (k n) -> p k n", k=KT)
            return src[:, :, (b % 2) * BLOCK:(b % 2 + 1) * BLOCK], r

        FFN_GAIN = {"ffn00": 2, "ffn01": 3, "ffn10": 4, "ffn11": 6}

        def first_slot(stage):
            return sum(LOADS[name[:3]] for name in stages[:stages.index(stage)])

        MIX_PARAMS, PARAMS = 16 * 7, 16 * (8 + 6 + 6 + 1 + 2 + 1 + 4)

        block = ctx.enter_context(nc.Block())

        @block.sync
        def _(sp):
            w = Follow()
            free = []
            n = [0]

            def load(dst, src, used, k, passed=None, rest=None):
                r = n[0] % RING
                if n[0] >= RING:
                    s, m, over, also = free[n[0] - RING]
                    if also:
                        sp.wait_ge(also, w.to(also, m))
                    if over:
                        w.past(over)
                    sp.wait_ge(s, w.to(s, m))
                sp.dma_start(dst(r), src).then_inc(S.loaded[r], 16)
                free.append((used, k, passed, rest))
                n[0] += 1

            def cols(r_, k, width):
                return lambda r: ring[:, r, 0:k * width].rearrange("p (k n) -> p k n", k=k)

            def wide(src, lo, hi, used, k):
                load(cols(0, KT, hi - lo), src[:, lo:hi].rearrange("(p k) n -> p k n", k=KT), used, k)

            def rows(src, lo, hi, used, k, passed=None):
                m = (hi - lo) // P
                load(cols(0, m, D), src[lo:hi, :].rearrange("(k p) n -> p k n", p=P), used, k, passed)

            def expert_src(l, e, which):
                if which == "down":
                    return a["w_expert_down"][l, e].rearrange("(f p) n -> p f n", p=P)
                return a["w_expert_" + which][l, e].rearrange("(p k) n -> p k n", k=KT)

            PAIR = (("gate", 0), ("up", 0), ("gate", 1), ("down", 0), ("up", 1), ("down", 1))

            def pair_loads(l, s, e0, wait, ff):
                for j, (which, e) in enumerate(PAIR):
                    r = (n[0] + j) % RING
                    if wait:
                        sp.wait_ge(s.low_made, ff.to(s.low_made, 2))
                        sp.wait_ge(s.low_rest, ff.to(s.low_rest, 2))
                    k = 4 if which == "down" else KT
                    dst = ring[:, r, :].rearrange("p (k n) -> p k n", k=k)
                    sp.dma_start(dst, expert_src(l, e0 + e, which)).then_inc(s.loaded[r], 16)

            def moe_loads(l):
                for which, e in PAIR:
                    load(cols(0, 4 if which == "down" else KT, D if which == "down" else DE),
                         expert_src(l, e, which), M.low_made, 2, rest=M.low_rest)
                per = {M.low_made: UNITS, M.low_rest: UNITS}
                with sp.Fori(1, PAIRS) as p:
                    w.enter(p, per, first=1)
                    pair_loads(l, M, 2 * p, True, w)
                    w.leave(PAIRS - 1)
                for which, e in PAIR:
                    free.append((M.low_made, 2, None, M.low_rest))
                n[0] += RING

            def more_loads(l):
                s = OV[l]
                sp.wait_ge(S.flag_ready, w.to(S.flag_ready))
                most = sp.value_load(flag[0:1, l:l + 1], min_val=0, max_val=SEQ)
                with sp.If(most > CAP):
                    sp.wait_ge(M.low_made, w.after(M.low_made, UNITS))
                    sp.wait_ge(M.low_rest, w.after(M.low_rest, UNITS))
                    v = Follow()
                    pair_loads(l, s, 0, False, v)
                    with sp.Fori(1, MORE * PAIRS) as q:
                        v.enter(q, {s.low_made: UNITS, s.low_rest: UNITS}, first=1)
                        pair_loads(l, s, (q % PAIRS) * 2, True, v)
                        v.leave(MORE * PAIRS - 1)
                    sp.wait_ge(s.low_made, v.to(s.low_made, UNITS))
                    sp.wait_ge(s.low_rest, v.to(s.low_rest, UNITS))

            def mixer_loads(l):
                wi = a["w_in"][l]
                for lo, hi, k in ((0, 512, 2), (512, 768, 1), (1280, 1792, 2), (1792, 2304, 2), (768, 1280, 2)):
                    if n[0] == 2:
                        sp.wait_ge(S.mix_param_loaded, MIX_PARAMS)
                    wide(wi, lo, hi, S.projected, k)
                rows(a["w_out"][l], 512, 1024, S.acc_done, 1)
                rows(a["w_out"][l], 0, 512, S.acc_done, 1)

            def ffn_loads(i, j):
                wg, wu, wd = a["ffn_w_gate_2"][i, j], a["ffn_w_up_2"][i, j], a["ffn_w_down_2"][i, j]
                for lo in range(0, FF, 512):
                    hi = min(lo + 512, FF)
                    last = hi == FF
                    wide(wg, lo, hi, S.ffn_low, 0 if last else 1 if lo else 3)
                    wide(wu, lo, hi, S.ffn_low, 0 if last else 1)
                    rows(wd, lo, hi, S.ffn_low, 1 if last else 4, S.acc_done if last else None)

            def nsa_loads():
                wi = a["nsa_w_in_2"][0]
                for lo in range(0, 2560, 512):
                    wide(wi, lo, lo + 512, S.projected, 2)
                wide(wi, 2560, 2608, S.projected, 1)
                for name in ("nsa_cmp_wk1_2", "nsa_cmp_wv1_2"):
                    load(lambda r: ring[:, r, :].rearrange("p (k n) -> p k n", k=16),
                         a[name][0].rearrange("(j p) n -> p j n", p=P), S.hidden, 1)
                rows(a["nsa_w_o_2"][0], 0, 512, S.half_done, 1)
                rows(a["nsa_w_o_2"][0], 512, 1024, S.acc_done, 1)

            sp.dma_start(x[:, :, :], a["x"][0].rearrange("(t p) d -> p t d", p=P)).then_inc(S.x_loaded, 16)
            sp.dma_start(cst[:, :], a["consts"]).then_inc(S.const_loaded, 16)
            for name in stages:
                if name[:3] == "mix":
                    mixer_loads(int(name[3]))
                elif name[:3] == "moe":
                    moe_loads(int(name[3]))
                    more_loads(int(name[3]))
                elif name[:3] == "ffn":
                    ffn_loads(int(name[3]), int(name[4]))
                elif name == "pool":
                    load(lambda r: ring[:, r, 0:2048].rearrange("p (k n) -> p k n", k=8),
                         a["pool_w_2"][0].rearrange("g (c p) e -> p (g c) e", p=P), S.acc_done, 1)
                elif name == "nsa":
                    nsa_loads()
            sp.wait_ge(S.x_ready, TT * len(stages))
            sp.dma_start(out[0].rearrange("(t p) d -> p t d", p=P), x[:, :, :]).then_inc(S.x_stored, 16)
            sp.wait_ge(S.x_stored, 16)

        gains = []

        def gain_list():
            g2 = a["norm_gains_2"]
            src = {"moe0": [a["norm_ffn"][0]], "moe1": [a["norm_ffn"][1]], "final": [a["norm_final"]],
                   "ffn00": [g2[0, 1]], "pool": [a["pool_scale_2"][0], g2[0, 3]], "ffn01": [g2[0, 5]],
                   "ffn10": [g2[1, 1]], "nsa": [g2[1, 3]], "ffn11": [g2[1, 5]]}
            return [(i, s) for i, name in enumerate(stages) for s in src.get(name, [])]

        gains = gain_list()
        N_PARAMS = [0, 0]

        @block.gpsimd
        def _(pool):
            w = Follow()

            def par(dst, src, first=False):
                pool.dma_start(dst, src).then_inc(S.mix_param_loaded if first else S.param_loaded, 16)
                N_PARAMS[0 if first else 1] += 16

            with nc.allow_non_contiguous_dma(reason="small parameters, transposed"):
                g2 = a["norm_gains_2"]
                def mixer_params(l):
                    for t in range(3):
                        par(cw[:, l, t, :], a["conv_w"][l, t].rearrange("(c p) -> p c", p=P), l == 0)
                    par(sink[:, l, :], a["attn_sink"][l].partition_broadcast(P), l == 0)
                    par(gcT[:, l, :], a["norm_conv_out"][l].rearrange("(c p) -> p c", p=P), l == 0)
                    par(gaT[:, l, :], a["norm_attn_out"][l].rearrange("(c p) -> p c", p=P), l == 0)

                par(gT[:, 0, :], a["norm_mix"][0].rearrange("(p k) -> p k", k=KT), True)
                mixer_params(0)
                for l in range(2):
                    par(wr[:, l, :, 0:NG], a["w_router_group"][l].rearrange("(p k) n -> p k n", k=KT))
                    par(wr[:, l, :, NG:], a["w_router_expert"][l].rearrange("(p k) n -> p k n", k=KT))
                    par(rbias[:, l, 0:NG], a["b_router_group"][l].partition_broadcast(P))
                    par(rbias[:, l, NG:], a["b_router_expert"][l].partition_broadcast(P))
                mixer_params(1)
                for n, src in enumerate((a["norm_mix"][1], g2[0, 0], g2[0, 4], g2[1, 0], g2[1, 2], g2[1, 4])):
                    par(gT[:, n + 1, :], src.rearrange("(p k) -> p k", k=KT))
                par(gT[:, 7, :], g2[0, 2].rearrange("(k p) -> p k", p=P))
                for h in range(2):
                    par(w2k[:, :, h * DH:(h + 1) * DH], a["nsa_cmp_wk2_2"][0].rearrange("(c p) d -> p c d", p=P))
                par(w2v[:, :, :], a["nsa_cmp_wv2_2"][0].rearrange("(c p) d -> p c d", p=P))
                for s, name in enumerate(("nsa_cmp_pos_k_2", "nsa_cmp_pos_v_2")):
                    for r in range(2):
                        par(cpos[r * DH:(r + 1) * DH, s, :],
                            a[name][0].rearrange("(j r) d -> r d j", r=2)[r])
            def experts(s, f, first, passes):
                with pool.Fori(0, passes) as p:
                    f.enter(p, {s.high_made: UNITS})
                    for u in range(UNITS):
                        lo = (u % 2) * HALF
                        pool.wait_ge(s.high_made, f.to(s.high_made))
                        pool.tensor_tensor(split[:, u % SPLIT, 1, LOW_V:],
                                           ring[:, (first + u // 2) % RING, lo + LOW_V:lo + HALF],
                                           split[:, u % SPLIT, 0, LOW_V:], ALU.subtract).then_inc(s.low_rest, 1)
                    f.leave(passes)

            def moe(l):
                first = first_slot(f"moe{l}")
                experts(M, w, first, PAIRS)
                pool.wait_ge(S.flag_ready, w.to(S.flag_ready))
                most = pool.value_load(flag[0:1, l:l + 1], min_val=0, max_val=SEQ)
                with pool.If(most > CAP):
                    experts(OV[l], Follow(), first, MORE * PAIRS)

            layers = [l for l in range(2) if f"moe{l}" in stages]
            for i, (st, src) in enumerate(gains):
                while layers and i >= 2 and gains[i - 2][0] >= stages.index(f"moe{layers[0]}"):
                    moe(layers.pop(0))
                if i >= 2:
                    pool.wait_ge(S.x_ready, TT * (gains[i - 2][0] + 1))
                pool.dma_start(gB[:, i % 2, :], src.partition_broadcast(P)).then_inc(S.gB_loaded[i % 2], 16)
                if i + 1 < len(gains) and st < stages.index("pool") <= gains[i + 1][0] if "pool" in stages else False:
                    pool.wait_ge(S.x_ready, TT * stages.index("pool"))
                    pool.dma_start(pool_means, a["means"].rearrange("(t p) w q -> p t w q", p=P)) \
                        .then_inc(S.means_loaded, 16)
                    pool.dma_start(pbias, a["pool_b_2"].rearrange("o g e -> o (g e)")).then_inc(S.means_loaded, 16)
            while layers:
                moe(layers.pop(0))

        assert N_PARAMS == [MIX_PARAMS, PARAMS], N_PARAMS

        @block.tensor
        def _(pe):
            w = Follow()
            n = [0]

            def slot():
                r = n[0] % RING
                n[0] += 1
                pe.wait_ge(S.loaded[r], w.to(S.loaded[r], 16))
                return r

            def view(r, k, width):
                return ring[:, r, 0:k * width].rearrange("p (k n) -> p k n", k=k)

            def transpose_h():
                for b in range(4):
                    for k in (2 * b, 2 * b + 1):
                        for t in range(TT):
                            if k == 0:
                                pe.wait_ge(S.h_ready, w.to(S.h_ready))
                            last = pe.transpose(PS[:, b, (k % 2) * SEQ + t * P:(k % 2) * SEQ + (t + 1) * P],
                                                hp[:, t, k * P:(k + 1) * P], ident)
                    last.then_inc(S.hT_psum, 1)
                pe.wait_ge(S.hT_even, w.to(S.hT_even, 2))
                pe.wait_ge(S.hT_odd, w.to(S.hT_odd, 2))

            def tokens_out(r, width, banks, offs=(0, 0), each=True):
                wv = view(r, KT, width)
                for t in range(TT):
                    for k in range(KT):
                        last = pe.matmul(PS[:, banks[t], offs[t]:offs[t] + width], hT[:, k, t * P:(t + 1) * P],
                                         wv[:, k, :], start=(k == 0), stop=(k == KT - 1))
                    if each:
                        last.then_inc(S.projected, 1)
                if not each:
                    last.then_inc(S.projected, 1)

            def channels_out(r, banks):
                wv = view(r, KT, 512)
                for c in range(4):
                    if c == 2 and banks[1] == 4:
                        pe.wait_ge(S.act_took, w.to(S.act_took))
                    for k in range(KT):
                        last = pe.matmul(PS[:, banks[c // 2], (c % 2) * SEQ:(c % 2 + 1) * SEQ],
                                         wv[:, k, c * P:(c + 1) * P], hT[:, k, :],
                                         start=(k == 0), stop=(k == KT - 1))
                    if c % 2:
                        last.then_inc(S.projected, 1)

            def attend(units, b):
                def scores(i):
                    u = units[i]
                    if i >= 2:
                        pe.wait_ge(S.masked, w.to(S.masked))
                    lo = DH * u.half
                    for r in range(4):
                        last = pe.matmul(PS[:, 2 * (i % 2) + r // 2, (r % 2) * SEQ:(r % 2) * SEQ + u.nk * P],
                                         u.qT[lo:lo + DH, u.tile + r, u.t * P:(u.t + 1) * P],
                                         u.kT[lo:lo + DH, u.gp, 0:u.nk * P], start=True, stop=True)
                    last.then_inc(S.scored, 1)

                def turn(i):
                    u = units[i]
                    pe.wait_ge(S.exped, w.to(S.exped))
                    if i:
                        pe.wait_ge(S.turned_taken, w.to(S.turned_taken))
                    for kt in range(u.nk):
                        for r in range(4):
                            last = pe.transpose(PS[:, 4 + kt, r * P:(r + 1) * P],
                                                b.P[i % 2][:, r, kt * P:(kt + 1) * P], ident)
                    last.then_inc(S.turned, 1)

                def values(i):
                    u = units[i]
                    if i >= 2:
                        pe.wait_ge(S.o_taken, w.to(S.o_taken))
                    for r in range(4):
                        lo = r * DH
                        for kt in range(u.nk):
                            last = pe.matmul(PS[:, 6 + i % 2, lo:lo + DH], b.PT[i % 2][:, kt, r, :],
                                             u.v[:, kt, u.g * DH:(u.g + 1) * DH],
                                             start=(kt == 0), stop=(kt == u.nk - 1))
                    last.then_inc(S.valued, 1)

                scores(0)
                for i in range(len(units)):
                    if i + 1 < len(units):
                        scores(i + 1)
                    turn(i)
                    if i:
                        values(i - 1)
                pe.wait_ge(S.turned_taken, w.to(S.turned_taken))
                values(len(units) - 1)
                pe.wait_ge(S.masked, w.to(S.masked, 2))
                pe.wait_ge(S.o_taken, w.to(S.o_taken, 2))

            def mixer(l):
                transpose_h()
                tokens_out(slot(), 512, (4, 5))
                tokens_out(slot(), 256, (6, 6), (0, 256), each=False)
                channels_out(slot(), (7, 0))
                channels_out(slot(), (1, 2))
                channels_out(slot(), (3, 4))
                pe.wait_ge(S.dve_took, w.to(S.dve_took, 3))
                pe.wait_ge(S.act_took, w.to(S.act_took, 4))
                for t in range(TT):
                    for m in range(4):
                        last = pe.transpose(PS[:, 5 + t, m * P:(m + 1) * P], MB.q[:, t, m * P:(m + 1) * P], ident)
                    last.then_inc(S.turned_q, 1)
                for t in range(TT):
                    last = pe.transpose(PS[:, 7, t * P:(t + 1) * P], MB.kv[:, t, 0:P], ident)
                last.then_inc(S.turned_q, 1)
                pe.wait_ge(S.q_turned_act, w.to(S.q_turned_act, 3))
                pe.wait_ge(S.dve_took, w.to(S.dve_took, 4))
                attend(mixer_units(), MB)
                pe.wait_ge(S.conv_gain, w.to(S.conv_gain, 5))
                for t in range(TT):
                    for c in range(4):
                        last = pe.matmul(PS[:, 7, t:t + 1], MB.sq[:, c, t * P:(t + 1) * P], ones[:, 0:1],
                                         start=(c == 0), stop=(c == 3))
                last.then_inc(S.conv_ss, 1)
                for part in range(2):
                    if part:
                        for c in range(4):
                            for t in range(TT):
                                last = pe.transpose(PS[:, 4 + c // 2, (c % 2) * SEQ + t * P:(c % 2) * SEQ + (t + 1) * P],
                                                    MB.ya[:, t, c * P:(c + 1) * P], ident)
                            if c % 2:
                                last.then_inc(S.ya_psum, 1)
                        pe.wait_ge(S.yaT_ready, w.to(S.yaT_ready, 4))
                        pe.wait_ge(S.conv_root, w.to(S.conv_root))
                    src = MB.yaT if part else MB.yc
                    wv = view(slot(), 4, D)
                    for t in range(TT):
                        for h in range(2):
                            for c in range(4):
                                last = pe.matmul(PS[:, 4 * part + 2 * t + h, :], src[:, c, t * P:(t + 1) * P],
                                                 wv[:, c, h * 512:(h + 1) * 512], start=(c == 0), stop=(c == 3))
                    last.then_inc(S.acc_done, 1)

            def clear_acc():
                for b in range(4):
                    pe.matmul(PS[:, b, :], zeros, cst[0:1, 0:512], start=True, stop=False,
                              skip_group_check=True)

            def experts(s, f, passes, y_high):
                def gather(b):
                    for k in range(4 * b, 4 * b + 4):
                        for t in range(TT):
                            last = pe.matmul(PS[:, 4 + b, (k % 4) * P:(k % 4 + 1) * P],
                                             hp[:, t, k * P:(k + 1) * P], EB.OH[:, t, :],
                                             start=(t == 0), stop=(t == 1))
                    last.then_inc(s.gathered, 1)

                def wide_sums(e, m, u):
                    for h in range(2):
                        pe.wait_ge(s.low_made, f.to(s.low_made))
                        pe.wait_ge(s.low_rest, f.to(s.low_rest))
                        for k in range(4):
                            for part in range(2):
                                wv = split[:, (u + h) % SPLIT, part, :].rearrange("p (k n) -> p k n", k=4)
                                last = pe.matmul(PS[:, 4 + m, :], xs[:, e, 4 * h + k, :], wv[:, k, :],
                                                 start=(h == 0 and k == 0 and part == 0),
                                                 stop=(h == 1 and k == 3 and part == 1))
                        last.then_inc(s.half_used, 1)

                def turn_sums():
                    for m in range(2):
                        for ft in range(4):
                            lo = (4 * m + ft) * CAP
                            last = pe.matmul(PS[:, 6, lo:lo + CAP], EB.gu[:, m, ft * P:(ft + 1) * P], const("fold"),
                                             start=True, stop=True)
                    last.then_inc(s.gu_turned, 1)

                def down(u):
                    for h in range(2):
                        pe.wait_ge(s.low_made, f.to(s.low_made))
                        pe.wait_ge(s.low_rest, f.to(s.low_rest))
                        for k in range(2):
                            for part in range(2):
                                wv = split[:, (u + h) % SPLIT, part, :].rearrange("p (k n) -> p k n", k=2)
                                for c in range(2):
                                    last = pe.matmul(PS[:, 6 + c, :], hid[:, 2 * h + k, :],
                                                     wv[:, k, c * 512:(c + 1) * 512],
                                                     start=(h == 0 and k == 0 and part == 0),
                                                     stop=(h == 1 and k == 1 and part == 1))
                        last.then_inc(s.half_used, 1)

                def combine(e):
                    pe.wait_ge(s.y_made, f.to(s.y_made))
                    for t in range(TT):
                        for c in range(2):
                            for y in (y_high, y_low):
                                last = pe.matmul(PS[:, 2 * t + c, :], marks[:, e, t * P:(t + 1) * P], y[:, c, :],
                                                 start=False, stop=False, skip_group_check=True)
                    return last

                clear_acc()
                pe.wait_ge(s.onehot, f.to(s.onehot))
                gather(0)
                gather(1)
                per = {s.onehot: 1, s.x_made: 2, s.low_made: UNITS, s.low_rest: UNITS, s.onehot_g: 1, s.g_taken: 1, s.gu_taken: 4,
                       s.h_made: 2, s.y_made: 2}
                def one_pair(behind):
                    pe.wait_ge(s.x_made, f.to(s.x_made, 2))
                    wide_sums(0, 0, 0)
                    if behind:
                        combine(1).then_inc(s.combined, 1)
                    wide_sums(0, 1, 2)
                    pe.wait_ge(s.onehot_g, f.to(s.onehot_g))
                    for e in range(2):
                        for t in range(TT):
                            last = pe.transpose(PS[:, 7, e * SEQ + t * P:e * SEQ + (t + 1) * P],
                                                EB.OHg[:, t, e, :], ident)
                    last.then_inc(s.oh_turned, 1)
                    pe.wait_ge(s.gu_taken, f.to(s.gu_taken, 2))
                    turn_sums()
                    wide_sums(1, 0, 4)
                    pe.wait_ge(s.g_taken, f.to(s.g_taken))
                    pe.wait_ge(s.h_made, f.to(s.h_made))
                    down(6)
                    wide_sums(1, 1, 8)
                    combine(0)
                    pe.wait_ge(s.gu_taken, f.to(s.gu_taken, 2))
                    turn_sums()
                    pe.wait_ge(s.onehot, f.to(s.onehot))
                    gather(0)
                    gather(1)
                    pe.wait_ge(s.h_made, f.to(s.h_made))
                    down(10)

                one_pair(False)
                with pe.Fori(1, passes) as p:
                    f.enter(p, per, first=1)
                    one_pair(True)
                    f.leave(passes - 1)
                combine(1).then_inc(s.combined, 1)
                f.past(s.x_made, 2)

            def moe(l):
                transpose_h()
                for t in range(TT):
                    for k in range(KT):
                        last = pe.matmul(PS[:, 4, t * 64:t * 64 + NG + NE], hT[:, k, t * P:(t + 1) * P],
                                         wr[:, l, k, :], start=(k == 0), stop=(k == KT - 1))
                last.then_inc(S.routed, 1)
                pe.wait_ge(S.marked, w.to(S.marked))
                pe.matmul(PS[:, 5, 0:NE], upper, EB.mk[:, 0, :], start=True, stop=True)
                pe.matmul(PS[:, 5, NE:2 * NE], ones, EB.mk[:, 0, :], start=True, stop=False)
                pe.matmul(PS[:, 5, NE:2 * NE], upper, EB.mk[:, 1, :], start=False, stop=True)
                pe.matmul(PS[:, 5, 2 * NE:3 * NE], ones, EB.mk[:, 0, :], start=True, stop=False)
                pe.matmul(PS[:, 5, 2 * NE:3 * NE], ones, EB.mk[:, 1, :], start=False, stop=True) \
                    .then_inc(S.ranked, 1)
                experts(M, w, PAIRS, y_high[l])
                n[0] += RING * PAIRS
                for r in range(RING):
                    w.past(S.loaded[r], 16 * PAIRS)
                pe.wait_ge(S.flag_ready, w.to(S.flag_ready))
                pe.wait_ge(S.moe_added, w.to(S.moe_added))
                most = pe.value_load(flag[0:1, l:l + 1], min_val=0, max_val=SEQ)
                with pe.If(most > CAP):
                    experts(OV[l], Follow(), MORE * PAIRS, y_high[l])

            def ffn():
                transpose_h()

                def wide_sums(b, kind):
                    bank = 4 + 2 * (b % 2) + (kind == "up")
                    pe.wait_ge(S.ffn_low, w.to(S.ffn_low))
                    for ft in range(2):
                        n_ = 0
                        for k in range(KT):
                            for part, hx in ((0, hT_high), (0, hT_low), (1, hT_high)):
                                wv = split[:, buffer_of(b, kind), part, :].rearrange("p (k n) -> p k n", k=KT)
                                last = pe.matmul(PS[:, bank, ft * SEQ:(ft + 1) * SEQ], wv[:, k, ft * P:(ft + 1) * P],
                                                 hx[:, k, :], start=(n_ == 0), stop=(n_ == 3 * KT - 1))
                                n_ += 1
                    last.then_inc(S.ffn_used, 1)

                def down(b):
                    pe.wait_ge(S.ffn_low, w.to(S.ffn_low))
                    pe.wait_ge(S.ffn_h, w.to(S.ffn_h))
                    for ft in range(2):
                        for t in range(TT):
                            for hpart, part in ((0, 0), (0, 1), (1, 0)):
                                wv = split[:, buffer_of(b, "down"), part, :].rearrange("p (k n) -> p k n", k=2)
                                for c in range(2):
                                    last = pe.matmul(PS[:, 2 * t + c, :], ffn_hid[:, hpart, ft, t * P:(t + 1) * P],
                                                     wv[:, ft, c * 512:(c + 1) * 512], start=False, stop=False,
                                                     skip_group_check=True)
                    last.then_inc(S.ffn_used if b < BLOCKS - 1 else S.acc_done, 1)

                pe.wait_ge(S.hT_low, w.to(S.hT_low))
                clear_acc()
                wide_sums(0, "gate")
                wide_sums(0, "up")
                with pe.Fori(0, 2) as p:
                    w.enter(p, {S.ffn_low: 12, S.ffn_h: 4})
                    for b in range(4):
                        wide_sums(b + 1, "gate")
                        wide_sums(b + 1, "up")
                        down(b)
                    w.leave(2)
                for b in range(8, BLOCKS):
                    if b + 1 < BLOCKS:
                        wide_sums(b + 1, "gate")
                        wide_sums(b + 1, "up")
                    down(b)
                for k in range(LOADS["ffn"]):
                    w.past(S.loaded[n[0] % RING], 16)
                    n[0] += 1

            def pool_mix():
                pe.wait_ge(S.means_loaded, w.to(S.means_loaded, 32))
                for c in range(KT):
                    for t in range(TT):
                        if c == 0:
                            pe.wait_ge(S.h_ready, w.to(S.h_ready))
                        last = pe.matmul(PS[:, c // 2, (c % 2) * SEQ:(c % 2 + 1) * SEQ], hp[:, t, c * P:(c + 1) * P],
                                         pool_means[:, t, c // 2, :], start=(t == 0), stop=(t == 1))
                    if c % 2:
                        last.then_inc(S.hT_psum, 1)
                pe.wait_ge(S.hT_even, w.to(S.hT_even, 2))
                pe.wait_ge(S.hT_odd, w.to(S.hT_odd, 2))
                wv = view(slot(), 8, 256)
                for t in range(TT):
                    for g in range(4):
                        o = PS[:, 2 * t + g // 2, (g % 2) * 256:(g % 2 + 1) * 256]
                        for c in range(2):
                            pe.matmul(o, hT[:, 2 * g + c, t * P:(t + 1) * P], wv[:, 2 * g + c, :],
                                      start=(c == 0), stop=False)
                        last = pe.matmul(o, ones[0:1, 0:P], pbias[0:1, g * 256:(g + 1) * 256],
                                         start=False, stop=True)
                last.then_inc(S.acc_done, 1)

            def nsa():
                transpose_h()
                tokens_out(slot(), 512, (4, 5))
                tokens_out(slot(), 512, (6, 7))
                tokens_out(slot(), 512, (0, 1))
                tokens_out(slot(), 512, (2, 3))
                pe.wait_ge(S.act_took, w.to(S.act_took, 2))
                tokens_out(slot(), 512, (4, 5))
                pe.wait_ge(S.act_took, w.to(S.act_took, 1))
                tokens_out(slot(), 48, (6, 6), (0, 48), each=False)
                pe.wait_ge(S.act_took, w.to(S.act_took, 8))
                pe.wait_ge(S.dve_took, w.to(S.dve_took, 8))
                for src, b0 in ((NB.qn, 0), (NB.qr, 4)):
                    for t in range(TT):
                        for gp in range(2):
                            for r in range(4):
                                m = gp * 4 + r
                                last = pe.transpose(PS[:, b0 + 2 * t + gp, r * P:(r + 1) * P],
                                                    src[:, t, m * P:(m + 1) * P], ident)
                            last.then_inc(S.turned_q, 1)
                pe.wait_ge(S.q_turned_act, w.to(S.q_turned_act, 4))
                for b, (src, off) in enumerate(((NB.kvc, 0), (NB.kvc, 256), (NB.kv[0], 0), (NB.kv[1], 0))):
                    for gp in range(2):
                        for t in range(TT):
                            last = pe.transpose(PS[:, b, gp * SEQ + t * P:gp * SEQ + (t + 1) * P],
                                                src[:, t, off + gp * P:off + (gp + 1) * P], ident)
                    last.then_inc(S.turned_q, 1)
                pe.wait_ge(S.q_turned_dve, w.to(S.q_turned_dve, 4))
                for s in range(2):
                    wv = view(slot(), 16, 256)
                    pe.wait_ge(S.z_pos, w.to(S.z_pos))
                    for c in range(2):
                        for j in range(16):
                            last = pe.matmul(PS[:, 4 + s, c * 60:(c + 1) * 60], wv[:, j, c * P:(c + 1) * P],
                                             NB.Z[s][:, j, :], start=(j == 0), stop=(j == 15))
                    last.then_inc(S.hidden, 1)
                pe.wait_ge(S.hc_ready, w.to(S.hc_ready, 2))
                for c in range(2):
                    pe.matmul(PS[:, 6, 0:60], w2k[:, c, :], NB.hc[:, 0, c * 60:(c + 1) * 60],
                              start=(c == 0), stop=(c == 1))
                for g in range(4):
                    for c in range(2):
                        last = pe.matmul(PS[0:NCMP, 7, g * DH:(g + 1) * DH],
                                         NB.hc[:, 1, c * 60 + g * NCMP:c * 60 + (g + 1) * NCMP], w2v[:, c, :],
                                         start=(c == 0), stop=(c == 1))
                last.then_inc(S.compressed, 1)
                pe.wait_ge(S.kc_ready, w.to(S.kc_ready))
                pe.wait_ge(S.q_turned_act, w.to(S.q_turned_act, 2))
                for t in range(TT):
                    for h in range(16):
                        g, r = h // 4, h % 4
                        lo = DH * (g % 2)
                        last = pe.matmul(PS[:, 2 * t + g % 2, h * 16:h * 16 + NCMP],
                                         NB.qnT[lo:lo + DH, 4 * (g // 2) + r, t * P:(t + 1) * P],
                                         NB.KC[lo:lo + DH, g * NCMP:(g + 1) * NCMP], start=True, stop=True)
                    last.then_inc(S.cscored, 1)
                for t in range(TT):
                    pe.wait_ge(S.p_ready, w.to(S.p_ready))
                    for g in range(4):
                        last = pe.transpose(PS[:, 2 + t, g * P:(g + 1) * P], NB.P32[:, t, 4 * g:4 * g + 4, :], ident)
                    last.then_inc(S.p_turned, 1)
                for t in range(TT):
                    pe.wait_ge(S.pT_ready, w.to(S.pT_ready))
                    for g in range(4):
                        last = pe.matmul(PS[:, 4 + 2 * t + g // 2, (g % 2) * 256:(g % 2 + 1) * 256],
                                         NB.PcT[:, t, g, :], NB.Vbd[:, g, :], start=True, stop=True)
                    last.then_inc(S.cvalued, 1)
                pe.wait_ge(S.o_first, w.to(S.o_first, 2))
                attend(nsa_units(), NB)
                transpose_h()
                for m in range(2):
                    wv = view(slot(), 4, D)
                    for t in range(TT):
                        for h in range(2):
                            for k in range(4):
                                last = pe.matmul(PS[:, 2 * t + h + 4, :], hT[:, 4 * m + k, t * P:(t + 1) * P],
                                                 wv[:, k, h * 512:(h + 1) * 512],
                                                 start=(m == 0 and k == 0), stop=(m == 1 and k == 3))
                    last.then_inc(S.acc_done if m else S.half_done, 1)

            pe.wait_ge(S.const_loaded, w.to(S.const_loaded, 16))
            pe.wait_ge(S.set_up, w.to(S.set_up, 2))
            for name in stages:
                if name == "moe0":
                    pe.wait_ge(S.param_loaded, PARAMS)
                if name[:3] == "mix":
                    mixer(int(name[3]))
                elif name[:3] == "moe":
                    moe(int(name[3]))
                elif name[:3] == "ffn":
                    ffn()
                elif name == "pool":
                    pool_mix()
                elif name == "nsa":
                    nsa()

        @block.scalar
        def _(act):
            w = Follow(S.act_step)
            seen_x = [0]
            counted = [0]

            def copy(o, i):
                return act.activation(o, i, ACT.Copy)

            def squares(src, junk, sums):
                for t in range(TT):
                    last = act.activation(junk(t), src(t), ACT.Square, accum_out=sums[:, t:t + 1])
                last.then_inc(S.act_step, 1)
                act.wait_ge(S.act_step, w.to(S.act_step))

            def roots(o, i, width, s):
                act.activation(o, i, ACT.Sqrt, bias=epsb[:, 0:1], scale=1.0 / width).then_inc(s, 1)

            def rms(t, src, junk):
                act.activation(junk, src, ACT.Square, accum_out=ss[:, t:t + 1]).then_inc(S.act_step, 1)
                act.wait_ge(S.act_step, w.to(S.act_step))
                roots(root[:, t:t + 1], ss[:, t:t + 1], D, S.root_ready)

            def x_now():
                seen_x[0] += 1
                if seen_x[0] > TT:
                    act.wait_ge(S.x_ready, w.to(S.x_ready))
                else:
                    act.wait_ge(S.x_loaded, 16)
                    act.wait_ge(S.set_up, 2)

            def norm():
                for t in range(TT):
                    x_now()
                    rms(t, x[:, t, :], hp[:, t, :])

            def take_hT(gain, dst=hT):
                for b in (0, 2):
                    act.wait_ge(S.hT_psum, w.to(S.hT_psum))
                    if gain is None:
                        i = copy(hT[:, 2 * b:2 * b + 2, :].rearrange("p a b -> p (a b)"), PS[:, b, :])
                    else:
                        for k in range(2):
                            i = act.activation(dst[:, 2 * b + k, :], PS[:, b, k * SEQ:(k + 1) * SEQ], ACT.Copy,
                                               scale=gT[:, gain, 2 * b + k:2 * b + k + 1])
                    i.then_inc(S.hT_even, 1)
                    w.past(S.hT_psum)

            def post(bank):
                for t in range(TT):
                    rms(t, PS[:, bank + 2 * t:bank + 2 * t + 2, :], hp[:, t, :].rearrange("p (a b) -> p a b", a=2))

            def attend(units, b, sinks):
                def take(i):
                    act.wait_ge(S.turned, w.to(S.turned))
                    nk = units[i].nk
                    copy(b.PT[i % 2][:, 0:nk, :, :].rearrange("p k r q -> p k (r q)"), PS[:, 4:4 + nk, :]) \
                        .then_inc(S.turned_taken, 1)

                for i, u in enumerate(units):
                    act.wait_ge(S.maxed, w.to(S.maxed))
                    st = b.stat[:, i % 4, :]
                    if sinks:
                        act.activation(st[:, 8:12], st[:, 8:12], ACT.Exp)
                    for r in range(4):
                        last = act.activation(b.P[i % 2][:, r, 0:u.nk * P], b.Sm[i % 2][:, r, 0:u.nk * P], ACT.Exp,
                                              bias=st[:, r:r + 1], scale=SCALE, accum_out=st[:, 4 + r:5 + r])
                    last.then_inc(S.exped, 1)
                    if i:
                        take(i - 1)
                take(len(units) - 1)

            def mixer(l):
                norm()
                if l == 0:
                    act.wait_ge(S.mix_param_loaded, MIX_PARAMS)
                take_hT(l)
                for t in range(TT):
                    act.wait_ge(S.projected, w.to(S.projected))
                    copy(MB.q[:, t, :].rearrange("p (r h d) -> p h r d", h=2, r=4),
                         PS[:, 4 + t, :].rearrange("p (h r d) -> p h r d", h=2, r=4)).then_inc(S.act_took, 1)
                act.wait_ge(S.projected, w.to(S.projected))
                copy(MB.kv.rearrange("p a b -> p (a b)"), PS[:, 6, :]).then_inc(S.act_took, 1)
                for h in range(2):
                    act.wait_ge(S.projected, w.to(S.projected))
                    copy(MB.gate_c[:, 2 * h:2 * h + 2, :].rearrange("p a b -> p (a b)"), PS[:, (7, 0)[h], :]) \
                        .then_inc(S.act_took, 1)
                w.past(S.projected, 4)
                for t in range(TT):
                    act.wait_ge(S.turned_q, w.to(S.turned_q))
                    copy(MB.qT[:, :, t * P:(t + 1) * P], PS[:, 5 + t, :].rearrange("p (m q) -> p m q", m=4)) \
                        .then_inc(S.q_turned_act, 1)
                act.wait_ge(S.turned_q, w.to(S.turned_q))
                copy(MB.kT[:, 0, :], PS[:, 7, 0:SEQ]).then_inc(S.q_turned_act, 1)
                act.wait_ge(S.dve_took, w.to(S.dve_took, 7))
                attend(mixer_units(), MB, True)
                act.activation(MB.sq, MB.yc, ACT.Square).then_inc(S.conv_gain, 1)
                act.wait_ge(S.conv_gain, w.to(S.conv_gain))
                for c in range(4):
                    act.activation(MB.yc[:, c, :], MB.yc[:, c, :], ACT.Copy, scale=gcT[:, l, c:c + 1]) \
                        .then_inc(S.conv_gain, 1)
                w.past(S.conv_gain, 4)
                act.wait_ge(S.o_taken, w.to(S.o_taken, 4))
                squares(lambda t: MB.ya[:, t, :], lambda t: MB.junk[:, 2 * t:2 * t + 2, :].rearrange(
                    "p a b -> p (a b)"), ss)
                roots(root, ss, 512, S.ya_root)
                act.wait_ge(S.conv_ss, w.to(S.conv_ss))
                roots(rootc, PS[:, 7, 0:2], 512, S.conv_root)
                for c in range(4):
                    if c % 2 == 0:
                        act.wait_ge(S.ya_psum, w.to(S.ya_psum))
                    act.activation(MB.yaT[:, c, :], PS[:, 4 + c // 2, (c % 2) * SEQ:(c % 2 + 1) * SEQ], ACT.Copy,
                                   scale=gaT[:, l, c:c + 1]).then_inc(S.yaT_ready, 1)
                w.past(S.acc_done, 2)

            def experts(s, f, first, passes, y_high):
                def high(u):
                    r = (first + u // 2) % RING
                    if u % 2 == 0:
                        act.wait_ge(s.loaded[r], f.to(s.loaded[r], 16))
                    copy(split[:, u % SPLIT, 0, :], ring[:, r, (u % 2) * HALF:(u % 2 + 1) * HALF]) \
                        .then_inc(s.high_made, 1)

                def high_x(b):
                    act.wait_ge(s.gathered, f.to(s.gathered))
                    copy(xs[:, :, 4 * b:4 * b + 4, 0:CAP].rearrange("p e k s -> p k e s"),
                         PS[:, 4 + b, :].rearrange("p (k e s) -> p k e s", k=4, e=2)).then_inc(s.x_high, 1)

                def silu():
                    act.wait_ge(s.gu_turned, f.to(s.gu_turned))
                    act.activation(EB.sE.rearrange("p a b -> p (a b)"), PS[:, 6, 0:4 * CAP], ACT.Silu) \
                        .then_inc(s.silu_done, 1)

                def take_gate():
                    copy(EB.gu[:, 0, :], PS[:, 4, :]).then_inc(s.gu_taken, 1)

                def take_gate_scaled():
                    act.activation(EB.gu[:, 0, :], PS[:, 4, :], ACT.Copy, scale=ones[:, 0:1]).then_inc(s.gu_taken, 1)

                def take_up():
                    copy(EB.gu[:, 1, :], PS[:, 5, :]).then_inc(s.gu_taken, 1)

                def high_y(e):
                    act.activation(y_high[:, :, :], PS[:, 6:8, :], ACT.Copy, scale=EB.gs[:, e:e + 1]) \
                        .then_inc(s.y_high, 1)

                def one_pair(more):
                    act.wait_ge(s.half_used, f.to(s.half_used))
                    high(3)
                    act.wait_ge(s.half_used, f.to(s.half_used))
                    high(4)
                    take_gate_scaled()
                    act.wait_ge(s.half_used, f.to(s.half_used))
                    high(5)
                    act.wait_ge(s.half_used, f.to(s.half_used))
                    take_up()
                    high(6)
                    silu()
                    act.wait_ge(s.half_used, f.to(s.half_used))
                    high(7)
                    act.wait_ge(s.half_used, f.to(s.half_used))
                    high(8)
                    take_gate()
                    act.wait_ge(s.half_used, f.to(s.half_used))
                    high(9)
                    act.wait_ge(s.half_used, f.to(s.half_used))
                    high_y(0)
                    high(10)
                    act.wait_ge(s.half_used, f.to(s.half_used))
                    high(11)
                    act.wait_ge(s.half_used, f.to(s.half_used))
                    take_up()
                    if more:
                        high(12)
                    silu()
                    high_x(0)
                    high_x(1)
                    act.wait_ge(s.half_used, f.to(s.half_used))
                    if more:
                        high(13)
                    act.wait_ge(s.half_used, f.to(s.half_used))
                    high_y(1)
                    if more:
                        high(14)

                for u in range(SPLIT):
                    high(u)
                high_x(0)
                high_x(1)
                per = {s.half_used: UNITS, s.gathered: 2, s.gu_turned: 2}
                per.update({s.loaded[r]: 16 for r in range(RING)})
                with act.Fori(0, passes - 1) as p:
                    f.enter(p, per)
                    one_pair(True)
                    f.leave(passes - 1)
                one_pair(False)

            def moe(l):
                norm()
                take_hT(None)
                act.wait_ge(S.gate_e, w.to(S.gate_e))
                act.activation(EB.ge, EB.gd, ACT.Exp).then_inc(S.gate_exp, 1)
                act.wait_ge(S.gate_e, w.to(S.gate_e))
                act.activation(EB.s[:, 5, :], EB.s[:, 4, :], ACT.Exp).then_inc(S.gate_exp, 1)
                experts(M, w, first_slot(f"moe{l}"), PAIRS, y_high[l])
                act.wait_ge(S.flag_ready, w.to(S.flag_ready))
                most = act.value_load(flag[0:1, l:l + 1], min_val=0, max_val=SEQ)
                with act.If(most > CAP):
                    experts(OV[l], Follow(), first_slot(f"moe{l}"), MORE * PAIRS, y_high[l])

            def count_loads(name):
                for k in range(counted[0], first_slot(name)):
                    w.past(S.loaded[k % RING], 16)
                counted[0] = first_slot(name)

            def ffn(name):
                norm()
                take_hT(FFN_GAIN[name], hT_high)

                def high(b, kind):
                    src, r = half_of(first_slot(name), b, kind)
                    if b % 2 == 0:
                        act.wait_ge(S.loaded[r], w.to(S.loaded[r], 16))
                    copy(split[:, buffer_of(b, kind), 0, :].rearrange("p (k n) -> p k n", k=KT), src) \
                        .then_inc(S.ffn_high, 1)

                def silu(b):
                    act.activation(FB.sF.rearrange("p a b -> p (a b)"), PS[:, 4 + 2 * (b % 2), :], ACT.Silu) \
                        .then_inc(S.ffn_silu, 1)

                def follow(b):
                    if b + 1 < BLOCKS:
                        act.wait_ge(S.ffn_used, w.to(S.ffn_used))
                        high(b + 1, "up")
                    act.wait_ge(S.ffn_used, w.to(S.ffn_used))
                    high(b, "down")
                    if b + 1 < BLOCKS:
                        act.wait_ge(S.ffn_used, w.to(S.ffn_used))
                        act.wait_ge(S.ffn_h, w.to(S.ffn_h))
                        silu(b + 1)
                    if b + 2 < BLOCKS:
                        high(b + 2, "gate")

                high(0, "gate")
                high(0, "up")
                high(1, "gate")
                act.wait_ge(S.ffn_used, w.after(S.ffn_used, 1))
                silu(0)
                per = {S.ffn_used: 12, S.ffn_h: 4}
                per.update({S.loaded[r]: 16 for r in range(RING)})
                with act.Fori(0, 2) as p:
                    w.enter(p, per)
                    for b in range(4):
                        follow(b)
                    w.leave(2)
                for b in range(8, BLOCKS):
                    follow(b)
                w.past(S.ffn_used, 1)
                w.past(S.ffn_h)
                act.wait_ge(S.acc_done, w.to(S.acc_done))
                post(0)

            def pool_mix():
                norm()
                take_hT(7)
                w.past(S.acc_done)
                for t in range(TT):
                    act.wait_ge(S.scaled, w.to(S.scaled))
                    rms(t, pool_f[:, t, :], hp[:, t, :])

            def nsa():
                norm()
                take_hT(5)
                for gp in range(2):
                    for t in range(TT):
                        act.wait_ge(S.projected, w.to(S.projected))
                        copy(NB.qn[:, t, gp * 512:(gp + 1) * 512].rearrange("p (r h d) -> p h r d", r=4, h=2),
                             PS[:, 4 + 2 * gp + t, :].rearrange("p (h r d) -> p h r d", r=4, h=2)) \
                            .then_inc(S.act_took, 1)
                for t in range(TT):
                    act.wait_ge(S.projected, w.to(S.projected))
                    copy(NB.kvc[:, t, :], PS[:, t, :]).then_inc(S.act_took, 1)
                for br in range(2):
                    for t in range(TT):
                        act.wait_ge(S.projected, w.to(S.projected))
                        copy(NB.kv[br][:, t, :], PS[:, 2 + 2 * br + t, :]).then_inc(S.act_took, 1)
                act.wait_ge(S.projected, w.to(S.projected))
                act.activation(NB.gts.rearrange("p a b -> p (a b)"), PS[:, 6, 0:96], ACT.Sigmoid) \
                    .then_inc(S.act_took, 1)
                for t in range(TT):
                    for gp in range(2):
                        act.wait_ge(S.turned_q, w.to(S.turned_q))
                        copy(NB.qnT[:, 4 * gp:4 * gp + 4, t * P:(t + 1) * P],
                             PS[:, 2 * t + gp, :].rearrange("p (m q) -> p m q", m=4)).then_inc(S.q_turned_act, 1)
                w.past(S.turned_q, 5)
                act.wait_ge(S.turned_q, w.to(S.turned_q))
                for g in range(4):
                    for r in range(2):
                        for h in range(2):
                            last = copy(*z_view(1, g, r, h))
                last.then_inc(S.z_built, 1)
                for br in range(2):
                    act.wait_ge(S.turned_q, w.to(S.turned_q))
                    copy(NB.kT[br].rearrange("p a b -> p (a b)"), PS[:, 2 + br, :]).then_inc(S.q_turned_act, 1)
                for s in range(2):
                    act.wait_ge(S.hidden, w.to(S.hidden))
                    act.activation(NB.hc[:, s, :], PS[:, 4 + s, 0:120], ACT.Silu).then_inc(S.hc_ready, 1)
                for t in range(TT):
                    act.wait_ge(S.csub, w.to(S.csub))
                    act.activation(NB.Sc[t], NB.Sc[t], ACT.Exp, scale=SCALE).then_inc(S.cexp, 1)
                for t in range(TT):
                    act.wait_ge(S.p_turned, w.to(S.p_turned))
                    copy(NB.PcT[:, t, :, :].rearrange("p a b -> p (a b)"), PS[:, 2 + t, :]).then_inc(S.pT_ready, 1)
                for t in range(TT):
                    act.wait_ge(S.cvalued, w.to(S.cvalued))
                    copy(hp[:, t, :].rearrange("p (a b) -> p a b", a=2), PS[:, 4 + 2 * t:6 + 2 * t, :]) \
                        .then_inc(S.o_first, 1)
                attend(nsa_units(), NB, False)
                take_hT(None)
                act.wait_ge(S.acc_done, w.to(S.acc_done))
                post(4)

            for name in stages:
                if name == "moe0":
                    act.wait_ge(S.param_loaded, PARAMS)
                if name[:3] == "mix":
                    mixer(int(name[3]))
                elif name[:3] == "moe":
                    count_loads(name)
                    moe(int(name[3]))
                    counted[0] += RING * PAIRS
                elif name == "final":
                    norm()
                elif name[:3] == "ffn":
                    count_loads(name)
                    ffn(name)
                    counted[0] += LOADS["ffn"]
                elif name == "pool":
                    pool_mix()
                elif name == "nsa":
                    nsa()

        @block.vector
        def _(v):
            w = Follow(S.dve_step)
            gi = [0]

            def gain_rows():
                i = gi[0]
                gi[0] += 1
                v.wait_ge(S.gB_loaded[i % 2], w.to(S.gB_loaded[i % 2], 16))
                return gB[:, i % 2, :]

            def reciprocal(o, i):
                v.reciprocal(o, i).then_inc(S.dve_step, 1)
                v.wait_ge(S.dve_step, w.to(S.dve_step))

            def bc(ap, shape):
                return ap.to_broadcast(shape)

            def norm(permute=True, gain=None):
                for t in range(TT):
                    v.wait_ge(S.root_ready, w.to(S.root_ready))
                    reciprocal(rstd[:, t:t + 1], root[:, t:t + 1])
                    xi, o = x[:, t, :], hp[:, t, :]
                    if permute:
                        xi = xi.rearrange("p (q k) -> p k q", k=KT)
                        o = o.rearrange("p (k q) -> p k q", k=KT)
                    if gain is None:
                        i = v.tensor_scalar(o, xi, rstd[:, t:t + 1], None, ALU.mult)
                    else:
                        i = v.scalar_tensor_tensor(o, xi, rstd[:, t:t + 1],
                                                   gain.rearrange("p (q k) -> p k q", k=KT), ALU.mult, ALU.mult)
                    i.then_inc(S.h_ready, 1)

            def take_hT(gain, dst=hT):
                for b in (1, 3):
                    v.wait_ge(S.hT_psum, w.to(S.hT_psum, 2))
                    if gain is None:
                        i = v.tensor_copy(hT[:, 2 * b:2 * b + 2, :].rearrange("p a b -> p (a b)"), PS[:, b, :])
                    else:
                        for k in range(2):
                            i = v.tensor_scalar(dst[:, 2 * b + k, :], PS[:, b, k * SEQ:(k + 1) * SEQ],
                                                gT[:, gain, 2 * b + k:2 * b + k + 1], None, ALU.mult)
                    i.then_inc(S.hT_odd, 1)
                w.past(S.hT_odd, 2)

            def post(src, factor):
                gain = gain_rows()
                for t in range(TT):
                    v.wait_ge(S.root_ready, w.to(S.root_ready))
                    reciprocal(rstd[:, t:t + 1], root[:, t:t + 1])
                    v.scalar_tensor_tensor(hp[:, t, :], src(t), rstd[:, t:t + 1], gain, ALU.mult, ALU.mult).then_inc(S.dve_step, 1)
                    v.wait_ge(S.dve_step, w.to(S.dve_step))
                    v.scalar_tensor_tensor(x[:, t, :], hp[:, t, :], factor, x[:, t, :], ALU.mult, ALU.add).then_inc(S.x_ready, 1)
                    v.wait_ge(S.x_ready, w.to(S.x_ready))

            def psum_rows(bank):
                return lambda t: PS[:, bank + 2 * t:bank + 2 * t + 2, :].rearrange("p a b -> p (a b)")

            def rotate(src, dst, t, tmp):
                n = src.shape[1]
                A = tmp[:, 0:n * ROPE].rearrange("p (h c) -> p h c", c=ROPE)
                B = tmp[:, 128:128 + n * ROPE].rearrange("p (h c) -> p h c", c=ROPE)
                H2 = ROPE // 2

                def table(name, lo, hi):
                    c0 = CONSTS[name][0] + t * ROPE
                    return cst[:, c0 + lo:c0 + hi].unsqueeze(1).to_broadcast([P, n, hi - lo])

                v.tensor_tensor(A, src[:, :, 0:ROPE], table("rope_c", 0, ROPE), ALU.mult)
                v.tensor_tensor(B[:, :, 0:H2], src[:, :, H2:ROPE], table("rope_s", 0, H2), ALU.mult)
                v.tensor_tensor(B[:, :, H2:ROPE], src[:, :, 0:H2], table("rope_s", H2, ROPE), ALU.mult).then_inc(S.dve_step, 1)
                v.wait_ge(S.dve_step, w.to(S.dve_step))
                return v.tensor_tensor(dst[:, :, 0:ROPE], A, B, ALU.add)

            def attend(units, b, sinks, finish):
                def stats(i):
                    u = units[i]
                    st = b.stat[:, i % 4, :]
                    n = u.nk * P
                    v.wait_ge(S.scored, w.to(S.scored))
                    if i >= 2:
                        v.wait_ge(S.exped, w.to(S.exped))
                    s4 = PS[:, 2 * (i % 2):2 * (i % 2) + 2, :].rearrange("p a (r k) -> p (a r) k", r=2)[:, :, 0:n]
                    sm = b.Sm[i % 2][:, :, 0:n]
                    v.tensor_tensor(sm, s4, u.mask.unsqueeze(1).to_broadcast([P, 4, n]), ALU.add).then_inc(S.masked, 1)
                    v.wait_ge(S.masked, w.to(S.masked))
                    v.tensor_reduce(st[:, 0:4], sm, AX_X, ALU.max).then_inc(S.dve_step, 1)
                    v.wait_ge(S.dve_step, w.to(S.dve_step))
                    if sinks is None:
                        v.tensor_scalar(st[:, 0:4], st[:, 0:4], -SCALE, None, ALU.mult).then_inc(S.maxed, 1)
                    else:
                        sk = sinks[:, 4 * u.g:4 * u.g + 4]
                        v.scalar_tensor_tensor(st[:, 0:4], st[:, 0:4], SCALE, sk, ALU.mult, ALU.max).then_inc(S.dve_step, 1)
                        v.wait_ge(S.dve_step, w.to(S.dve_step))
                        v.tensor_scalar(st[:, 0:4], st[:, 0:4], -1.0, None, ALU.mult).then_inc(S.dve_step, 1)
                        v.wait_ge(S.dve_step, w.to(S.dve_step))
                        v.tensor_tensor(st[:, 8:12], st[:, 0:4], sk, ALU.add).then_inc(S.maxed, 1)

                def output(i):
                    u = units[i]
                    st = b.stat[:, i % 4, :]
                    v.wait_ge(S.valued, w.to(S.valued))
                    if sinks is not None:
                        v.tensor_tensor(st[:, 4:8], st[:, 4:8], st[:, 8:12], ALU.add).then_inc(S.dve_step, 1)
                        v.wait_ge(S.dve_step, w.to(S.dve_step))
                    reciprocal(st[:, 12:16], st[:, 4:8])
                    finish(i, u, PS[:, 6 + i % 2, 0:SEQ].rearrange("p (r d) -> p r d", r=4),
                           st[:, 12:16])

                for i in range(len(units)):
                    stats(i)
                    if i >= 2:
                        output(i - 2)
                output(len(units) - 2)
                output(len(units) - 1)
                w.past(S.exped, 2)

            def mixer(l):
                norm()
                if l == 0:
                    v.wait_ge(S.mix_param_loaded, MIX_PARAMS)
                take_hT(l)
                v.memset(MB.z[:, :, 0:1], 0.0)
                v.memset(MB.z[:, :, SEQ + 1:SEQ + 2], 0.0)
                for t in range(TT):
                    v.wait_ge(S.act_took, w.to(S.act_took))
                    q = MB.q[:, t, :].rearrange("p (h d) -> p h d", d=DH)
                    rotate(q, q, t, MB.tmp).then_inc(S.dve_took, 1)
                    v.wait_ge(S.dve_took, w.to(S.dve_took))
                v.wait_ge(S.act_took, w.to(S.act_took))
                for t in range(TT):
                    k = MB.kv[:, t, 0:P].rearrange("p (h d) -> p h d", d=DH)
                    rotate(k, k, t, MB.tmp).then_inc(S.dve_took if t else S.dve_step, 1)
                    v.wait_ge(S.dve_took if t else S.dve_step, w.to(S.dve_took if t else S.dve_step))
                w.past(S.projected, 5)
                v.wait_ge(S.act_took, w.to(S.act_took, 2))
                for h in range(2):
                    v.wait_ge(S.projected, w.to(S.projected))
                    i = v.tensor_tensor(MB.z[:, 2 * h:2 * h + 2, 1:SEQ + 1],
                                        PS[:, 1 + h, :].rearrange("p (a b) -> p a b", a=2),
                                        MB.gate_c[:, 2 * h:2 * h + 2, :], ALU.mult)
                    i.then_inc(S.dve_took, 1)
                    v.wait_ge(S.dve_took, w.to(S.dve_took))
                for c in range(4):
                    v.tensor_scalar(MB.cv[:, c, :], MB.z[:, c, 0:SEQ], cw[:, l, 0, c:c + 1], None, ALU.mult).then_inc(S.dve_step, 1)
                    v.wait_ge(S.dve_step, w.to(S.dve_step))
                    for tap in (1, 2):
                        v.scalar_tensor_tensor(MB.cv[:, c, :], MB.z[:, c, tap:tap + SEQ],
                                               cw[:, l, tap, c:c + 1], MB.cv[:, c, :], ALU.mult, ALU.add).then_inc(S.dve_step, 1)
                        v.wait_ge(S.dve_step, w.to(S.dve_step))
                for h in range(2):
                    v.wait_ge(S.projected, w.to(S.projected))
                    i = v.tensor_tensor(MB.yc[:, 2 * h:2 * h + 2, :],
                                        PS[:, 3 + h, :].rearrange("p (a b) -> p a b", a=2),
                                        MB.cv[:, 2 * h:2 * h + 2, :], ALU.mult)
                    i.then_inc(S.dve_took, 1)
                    v.wait_ge(S.dve_took, w.to(S.dve_took))

                def finish(i, u, o, fac):
                    v.tensor_tensor(MB.ya[:, u.t, u.g * 256:(u.g + 1) * 256].rearrange("p (r d) -> p r d", r=4),
                                    o, fac.unsqueeze(2).to_broadcast([P, 4, DH]), ALU.mult).then_inc(S.o_taken, 1)
                    w.past(S.o_taken)

                w.past(S.turned_q, 3)
                attend(mixer_units(), MB, sink[:, l, :], finish)
                for root_sem, o, i, bank in ((S.conv_root, rstdc, rootc, 0), (S.ya_root, rstd, root, 4)):
                    v.wait_ge(root_sem, w.to(root_sem))
                    reciprocal(o, i)
                    v.wait_ge(S.acc_done, w.to(S.acc_done))
                    for t in range(TT):
                        v.scalar_tensor_tensor(x[:, t, :], psum_rows(bank)(t), o[:, t:t + 1], x[:, t, :],
                                               ALU.mult, ALU.add).then_inc(S.x_ready if bank else S.dve_step, 1)
                        v.wait_ge(S.x_ready if bank else S.dve_step, w.to(S.x_ready if bank else S.dve_step))

            def experts(s, f, first, passes, pos, gate, y_high):
                f.step = s.step
                iota = const("iota").unsqueeze(1).to_broadcast([P, 2, CAP])

                def tokens_of(e):
                    for t in range(TT):
                        last = v.tensor_tensor(EB.OH[:, t, :].rearrange("p (e s) -> p e s", e=2), iota,
                                               pos[:, t, bass.ds(e, 2)].unsqueeze(2).to_broadcast([P, 2, CAP]),
                                               ALU.is_equal)
                    last.then_inc(s.onehot, 1)
                    v.wait_ge(s.onehot, f.to(s.onehot))

                def low(u):
                    r = (first + u // 2) % RING
                    v.wait_ge(s.high_made, f.to(s.high_made))
                    v.tensor_tensor(split[:, u % SPLIT, 1, 0:LOW_V], ring[:, r, (u % 2) * HALF:(u % 2) * HALF + LOW_V],
                                    split[:, u % SPLIT, 0, 0:LOW_V], ALU.subtract).then_inc(s.low_made, 1)

                def low_y(e):
                    v.wait_ge(s.y_high, f.to(s.y_high))
                    v.scalar_tensor_tensor(y_low[:, :, :], PS[:, 6:8, :], EB.gs[:, e:e + 1], y_high[:, :, :],
                                           ALU.mult, ALU.subtract).then_inc(s.y_made, 1)

                def low_x(b):
                    v.wait_ge(s.x_high, f.to(s.x_high))
                    at = xs[:, :, 4 * b:4 * b + 4, :].rearrange("p e k s -> p k e s")
                    v.tensor_tensor(at[:, :, :, CAP:], PS[:, 4 + b, :].rearrange("p (k e s) -> p k e s", k=4, e=2),
                                    at[:, :, :, 0:CAP], ALU.subtract).then_inc(s.x_made, 1)

                def hidden():
                    v.wait_ge(s.silu_done, f.to(s.silu_done))
                    v.tensor_tensor(EB.sE, PS[:, 6, 4 * CAP:].rearrange("p (k s) -> p k s", k=4), EB.sE, ALU.mult) \
                        .then_inc(s.step, 1)
                    v.wait_ge(s.step, f.to(s.step))
                    v.tensor_copy(hid[:, :, 0:CAP], EB.sE).then_inc(s.step, 1)
                    v.wait_ge(s.step, f.to(s.step))
                    v.tensor_tensor(hid[:, :, CAP:], EB.sE, hid[:, :, 0:CAP], ALU.subtract).then_inc(s.h_made, 1)

                def one_pair(e, more):
                    low(3)
                    for t in range(TT):
                        for part in range(2):
                            last = v.tensor_tensor(EB.OHg[:, t, :, part * CAP:(part + 1) * CAP],
                                                   EB.OH[:, t, :].rearrange("p (e s) -> p e s", e=2),
                                                   gate[:, t, bass.ds(e, 2)].unsqueeze(2).to_broadcast([P, 2, CAP]),
                                                   ALU.mult)
                    last.then_inc(s.onehot_g, 1)
                    low(4)
                    low(5)
                    v.wait_ge(s.oh_turned, f.to(s.oh_turned))
                    v.tensor_reduce(EB.gs[:, 0:2], PS[:, 7, :].rearrange("p (e q) -> p e q", e=2), AX_X, ALU.max)
                    v.tensor_scalar(marks.rearrange("p a b -> p (a b)"), PS[:, 7, :], 0.0, None, ALU.is_gt) \
                        .then_inc(s.g_taken, 1)
                    low(6)
                    hidden()
                    low(7)
                    tokens_of(e + 2)
                    low(8)
                    low(9)
                    low_y(0)
                    low(10)
                    low(11)
                    if more:
                        low(12)
                    hidden()
                    low_x(0)
                    low_x(1)
                    if more:
                        low(13)
                    low_y(1)
                    if more:
                        low(14)

                tokens_of(0)
                low(0)
                low(1)
                low(2)
                low_x(0)
                low_x(1)
                with v.Fori(0, passes - 1) as p:
                    f.enter(p, {s.high_made: UNITS, s.onehot: 1, s.x_high: 2, s.oh_turned: 1, s.silu_done: 2,
                                s.step: 4, s.y_high: 2})
                    one_pair(2 * p, True)
                    f.leave(passes - 1)
                one_pair(2 * (passes - 1), False)
                v.wait_ge(s.combined, f.to(s.combined, passes))
                for t in range(TT):
                    last = v.tensor_tensor(x[:, t, :], psum_rows(0)(t), x[:, t, :], ALU.add)
                return last

            def first_best(vals, n, key, best, hot, tie, top):
                v.tensor_reduce(top, vals, AX_X, ALU.max).then_inc(S.dve_step, 1)
                v.wait_ge(S.dve_step, w.to(S.dve_step))
                v.tensor_tensor(key, vals, top.unsqueeze(2).to_broadcast([P, TT, n]), ALU.is_equal).then_inc(S.dve_step, 1)
                v.wait_ge(S.dve_step, w.to(S.dve_step))
                v.tensor_tensor(key, key, tie.unsqueeze(1).to_broadcast([P, TT, n]), ALU.mult).then_inc(S.dve_step, 1)
                v.wait_ge(S.dve_step, w.to(S.dve_step))
                v.tensor_reduce(best, key, AX_X, ALU.max).then_inc(S.dve_step, 1)
                v.wait_ge(S.dve_step, w.to(S.dve_step))
                v.tensor_tensor(hot, key, best.unsqueeze(2).to_broadcast([P, TT, n]), ALU.is_equal).then_inc(S.dve_step, 1)
                v.wait_ge(S.dve_step, w.to(S.dve_step))

            def moe(l):
                norm(gain=gain_rows())
                take_hT(None)
                B = EB
                tie = const("tie")
                gm, gs, pg, m1, d, e2, m2, g1, g2, best = (B.s[:, i, :] for i in (0, 1, 2, 3, 4, 5, 6, 7, 8, 9))

                def over(ap, n):
                    return ap.unsqueeze(2).to_broadcast([P, TT, n])

                v.wait_ge(S.routed, w.to(S.routed))
                v.tensor_tensor(B.lg, PS[:, 4, 0:P].rearrange("p (t n) -> p t n", t=TT)[:, :, 0:NG + NE],
                                rbias[:, l, :].unsqueeze(1).to_broadcast([P, TT, NG + NE]), ALU.add).then_inc(S.dve_step, 1)
                v.wait_ge(S.dve_step, w.to(S.dve_step))
                gl, el = B.lg[:, :, 0:NG], B.lg[:, :, NG:]
                first_best(gl, NG, B.gk, best, B.gh, tie[:, 0:NG], gm)
                v.tensor_tensor(B.gd, gl, over(gm, NG), ALU.subtract).then_inc(S.gate_e, 1)
                v.tensor_scalar(B.gk, B.gh, 1.0, BIG, ALU.subtract, ALU.mult).then_inc(S.dve_step, 1)
                v.wait_ge(S.dve_step, w.to(S.dve_step))
                for t in range(TT):
                    last = v.tensor_tensor(B.el[:, t, :].rearrange("p (g e) -> p g e", g=NG),
                                           el[:, t, :].rearrange("p (g e) -> p g e", g=NG),
                                           B.gk[:, t, :].unsqueeze(2).to_broadcast([P, NG, NE // NG]), ALU.add)
                last.then_inc(S.dve_step, 1)
                v.wait_ge(S.dve_step, w.to(S.dve_step))
                first_best(B.el, NE, B.key, best, B.oh1, tie[:, NG:], m1)
                v.scalar_tensor_tensor(B.el3, B.oh1, -2 * BIG, B.el, ALU.mult, ALU.add).then_inc(S.dve_step, 1)
                v.wait_ge(S.dve_step, w.to(S.dve_step))
                first_best(B.el3, NE, B.key, best, B.oh2, tie[:, NG:], m2)
                v.tensor_tensor(B.mk, B.oh1, B.oh2, ALU.add).then_inc(S.marked, 1)
                v.wait_ge(S.marked, w.to(S.marked))
                v.tensor_tensor(d, m2, m1, ALU.subtract).then_inc(S.gate_e, 1)
                v.wait_ge(S.gate_exp, w.to(S.gate_exp))
                v.tensor_reduce(gs, B.ge, AX_X, ALU.add).then_inc(S.dve_step, 1)
                v.wait_ge(S.dve_step, w.to(S.dve_step))
                reciprocal(pg, gs)
                v.wait_ge(S.gate_exp, w.to(S.gate_exp))
                v.tensor_scalar(g1, e2, 1.0, None, ALU.add).then_inc(S.dve_step, 1)
                v.wait_ge(S.dve_step, w.to(S.dve_step))
                reciprocal(g2, g1)
                v.tensor_tensor(g1, g2, pg, ALU.mult).then_inc(S.dve_step, 1)
                v.wait_ge(S.dve_step, w.to(S.dve_step))
                v.tensor_tensor(g2, g1, e2, ALU.mult).then_inc(S.dve_step, 1)
                v.wait_ge(S.dve_step, w.to(S.dve_step))
                v.memset(B.gate[:, :, NE:NE + 2], 0.0).then_inc(S.dve_step, 1)
                v.wait_ge(S.dve_step, w.to(S.dve_step))
                v.memset(B.pos[:, :, NE:NE + 2], FAR).then_inc(S.dve_step, 1)
                v.wait_ge(S.dve_step, w.to(S.dve_step))
                v.tensor_tensor(B.oh1, B.oh1, over(g1, NE), ALU.mult).then_inc(S.dve_step, 1)
                v.wait_ge(S.dve_step, w.to(S.dve_step))
                v.tensor_tensor(B.oh2, B.oh2, over(g2, NE), ALU.mult).then_inc(S.dve_step, 1)
                v.wait_ge(S.dve_step, w.to(S.dve_step))
                v.tensor_tensor(B.gate[:, :, 0:NE], B.oh1, B.oh2, ALU.add).then_inc(S.dve_step, 1)
                v.wait_ge(S.dve_step, w.to(S.dve_step))
                v.tensor_scalar(B.key, B.mk, -FAR, FAR, ALU.mult, ALU.add).then_inc(S.dve_step, 1)
                v.wait_ge(S.dve_step, w.to(S.dve_step))
                v.wait_ge(S.ranked, w.to(S.ranked))
                v.tensor_tensor(B.pos[:, :, 0:NE], PS[:, 5, 0:2 * NE].rearrange("p (t n) -> p t n", t=TT),
                                B.key, ALU.add).then_inc(S.dve_step, 1)
                v.wait_ge(S.dve_step, w.to(S.dve_step))
                v.tensor_reduce(flag_f[:, :], PS[:, 5, 2 * NE:3 * NE], AX_X, ALU.max).then_inc(S.dve_step, 1)
                v.wait_ge(S.dve_step, w.to(S.dve_step))
                v.tensor_copy(flag[:, l:l + 1], flag_f[:, :]).then_inc(S.flag_ready, 1)
                v.wait_ge(S.flag_ready, w.to(S.flag_ready))
                experts(M, w, first_slot(f"moe{l}"), PAIRS, B.pos, B.gate, y_high[l]).then_inc(S.moe_added, 1)
                v.wait_ge(S.moe_added, w.to(S.moe_added))
                w.step = S.dve_step
                most = v.value_load(flag[0:1, l:l + 1], min_val=0, max_val=SEQ)
                with v.If(most > CAP):
                    f = Follow(OV[l].step)
                    v.memset(B.gatev[:, :, MORE * NE:], 0.0).then_inc(f.step, 1)
                    v.wait_ge(f.step, f.to(f.step))
                    v.memset(B.posv[:, :, MORE * NE:], FAR).then_inc(f.step, 1)
                    v.wait_ge(f.step, f.to(f.step))
                    for r in range(MORE):
                        v.tensor_copy(B.gatev[:, :, r * NE:(r + 1) * NE], B.gate[:, :, 0:NE]).then_inc(f.step, 1)
                        v.wait_ge(f.step, f.to(f.step))
                        v.tensor_scalar(B.posv[:, :, r * NE:(r + 1) * NE], B.pos[:, :, 0:NE],
                                        float(CAP * (r + 1)), None, ALU.subtract).then_inc(f.step, 1)
                        v.wait_ge(f.step, f.to(f.step))
                    experts(OV[l], f, first_slot(f"moe{l}"), MORE * PAIRS, B.posv, B.gatev, y_high[l]).then_inc(f.step, 1)
                    v.wait_ge(f.step, f.to(f.step))
                for t in range(TT):
                    v.tensor_copy(flag_f[:, :], rstd[:, 0:1]).then_inc(S.x_ready, 1)
                    v.wait_ge(S.x_ready, w.to(S.x_ready))

            def ffn(name):
                norm()
                gain = FFN_GAIN[name]
                take_hT(gain, hT_high)
                v.wait_ge(S.hT_odd, w.after(S.hT_odd, 0))
                v.wait_ge(S.hT_even, w.after(S.hT_odd, 0))
                for k in range(KT):
                    last = v.scalar_tensor_tensor(hT_low[:, k, :], PS[:, k // 2, (k % 2) * SEQ:(k % 2 + 1) * SEQ],
                                                  gT[:, gain, k:k + 1], hT_high[:, k, :], ALU.mult, ALU.subtract)
                last.then_inc(S.hT_low, 1)

                def low(b, kind):
                    src, _ = half_of(first_slot(name), b, kind)
                    v.wait_ge(S.ffn_high, w.to(S.ffn_high))
                    at = split[:, buffer_of(b, kind), :, :].rearrange("p a (k n) -> p a k n", k=KT)
                    v.tensor_tensor(at[:, 1], src, at[:, 0], ALU.subtract).then_inc(S.ffn_low, 1)

                def follow(b):
                    if b + 1 < BLOCKS:
                        low(b + 1, "up")
                    v.wait_ge(S.ffn_used, w.to(S.ffn_used, 0))
                    w.past(S.ffn_used, 3)
                    v.wait_ge(S.ffn_silu, w.to(S.ffn_silu))
                    sF = FB.sF
                    v.tensor_tensor(sF, PS[:, 5 + 2 * (b % 2), :].rearrange("p (k s) -> p k s", k=2), sF, ALU.mult) \
                        .then_inc(S.ffn_step, 1)
                    v.wait_ge(S.ffn_step, w.to(S.ffn_step))
                    v.tensor_copy(ffn_hid[:, 0], sF).then_inc(S.ffn_step, 1)
                    v.wait_ge(S.ffn_step, w.to(S.ffn_step))
                    v.tensor_tensor(ffn_hid[:, 1], sF, ffn_hid[:, 0], ALU.subtract).then_inc(S.ffn_h, 1)
                    low(b, "down")
                    if b + 2 < BLOCKS:
                        low(b + 2, "gate")

                low(0, "gate")
                low(0, "up")
                low(1, "gate")
                w.past(S.ffn_used, 2)
                with v.Fori(0, 2) as p:
                    w.enter(p, {S.ffn_high: 12, S.ffn_used: 12, S.ffn_silu: 4, S.ffn_step: 8})
                    for b in range(4):
                        follow(b)
                    w.leave(2)
                for b in range(8, BLOCKS):
                    follow(b)
                w.past(S.ffn_used, -3)
                w.past(S.acc_done)
                post(psum_rows(0), 0.5)

            def pool_mix():
                norm(permute=False)
                take_hT(7)
                scale = gain_rows()
                v.wait_ge(S.acc_done, w.to(S.acc_done))
                for t in range(TT):
                    v.tensor_tensor(pool_f[:, t, :], psum_rows(0)(t), scale, ALU.mult).then_inc(S.scaled, 1)
                    v.wait_ge(S.scaled, w.to(S.scaled))
                post(lambda t: pool_f[:, t, :], 1.0)

            def nsa():
                norm()
                take_hT(5)
                w.past(S.projected, 11)
                for gp in range(2):
                    for t in range(TT):
                        v.wait_ge(S.act_took, w.to(S.act_took))
                        q = NB.qn[:, t, gp * 512:(gp + 1) * 512].rearrange("p (h d) -> p h d", d=DH)
                        r = NB.qr[:, t, gp * 512:(gp + 1) * 512].rearrange("p (h d) -> p h d", d=DH)
                        v.tensor_copy(r[:, :, ROPE:DH], q[:, :, ROPE:DH])
                        rotate(q, r, t, NB.tmp).then_inc(S.dve_took, 1)
                        v.wait_ge(S.dve_took, w.to(S.dve_took))
                w.past(S.act_took, 2)
                for br in range(2):
                    for t in range(TT):
                        v.wait_ge(S.act_took, w.to(S.act_took))
                        k = NB.kv[br][:, t, 0:256].rearrange("p (h d) -> p h d", d=DH)
                        rotate(k, k, t, NB.tmp).then_inc(S.dve_took, 1)
                        v.wait_ge(S.dve_took, w.to(S.dve_took))
                v.memset(NB.Vbd, 0.0)
                v.memset(NB.P32, 0.0).then_inc(S.dve_step, 1)
                v.wait_ge(S.dve_step, w.to(S.dve_step))
                w.past(S.turned_q, 4)
                for t in range(TT):
                    for gp in range(2):
                        v.wait_ge(S.turned_q, w.to(S.turned_q))
                        v.tensor_copy(NB.qrT[:, 4 * gp:4 * gp + 4, t * P:(t + 1) * P],
                                      PS[:, 4 + 2 * t + gp, :].rearrange("p (m q) -> p m q", m=4)) \
                            .then_inc(S.q_turned_dve, 1)
                v.wait_ge(S.turned_q, w.to(S.turned_q))
                for g in range(4):
                    for r in range(2):
                        for h in range(2):
                            last = v.tensor_copy(*z_view(0, g, r, h))
                last.then_inc(S.dve_step, 1)
                v.wait_ge(S.dve_step, w.to(S.dve_step))
                for s in range(2):
                    if s:
                        v.wait_ge(S.z_built, w.to(S.z_built))
                    v.tensor_tensor(NB.Z[s], NB.Z[s], cpos[:, s, :].unsqueeze(2).to_broadcast([P, 16, 60]),
                                    ALU.add).then_inc(S.z_pos, 1)
                w.past(S.turned_q, 3)
                v.wait_ge(S.compressed, w.to(S.compressed))
                v.tensor_copy(NB.KC, PS[:, 6, 0:60])
                for r in range(4):
                    last = v.tensor_copy(NB.Vbd[32 * r:32 * r + NCMP, :, r * DH:(r + 1) * DH],
                                         PS[0:NCMP, 7, 0:256].rearrange("p (g d) -> p g d", g=4))
                last.then_inc(S.kc_ready, 1)
                mask, some = const("cmp_mask"), const("cmp_any")
                for t in range(TT):
                    v.wait_ge(S.cscored, w.to(S.cscored))
                    for g in range(4):
                        last = v.tensor_tensor(NB.Sc[t][:, 4 * g:4 * g + 4, :],
                                               PS[:, 2 * t + g % 2, 64 * g:64 * g + 64]
                                               .rearrange("p (h n) -> p h n", h=4)[:, :, 0:NCMP],
                                               mask[:, t * NCMP:(t + 1) * NCMP].unsqueeze(1)
                                               .to_broadcast([P, 4, NCMP]), ALU.add)
                    last.then_inc(S.dve_step, 1)
                    v.wait_ge(S.dve_step, w.to(S.dve_step))
                    v.tensor_reduce(NB.cs[:, t, :], NB.Sc[t], AX_X, ALU.max).then_inc(S.dve_step, 1)
                    v.wait_ge(S.dve_step, w.to(S.dve_step))
                    v.tensor_tensor(NB.Sc[t], NB.Sc[t], NB.cs[:, t, :].unsqueeze(2)
                                    .to_broadcast([P, 16, NCMP]), ALU.subtract).then_inc(S.csub, 1)
                    v.wait_ge(S.csub, w.to(S.csub))
                v.wait_ge(S.act_took, w.to(S.act_took))
                for t in range(TT):
                    v.wait_ge(S.cexp, w.to(S.cexp))
                    cs = NB.cs[:, 2 + 2 * t, :]
                    fac = NB.cs[:, 3 + 2 * t, :]
                    v.tensor_reduce(cs, NB.Sc[t], AX_X, ALU.add).then_inc(S.dve_step, 1)
                    v.wait_ge(S.dve_step, w.to(S.dve_step))
                    reciprocal(fac, cs)
                    v.scalar_tensor_tensor(fac, fac, some[:, t:t + 1], NB.gts[:, t, 0:16], ALU.mult, ALU.mult).then_inc(S.dve_step, 1)
                    v.wait_ge(S.dve_step, w.to(S.dve_step))
                    v.tensor_tensor(NB.P32[:, t, :, 0:NCMP], NB.Sc[t], fac.unsqueeze(2)
                                    .to_broadcast([P, 16, NCMP]), ALU.mult).then_inc(S.p_ready, 1)
                v.wait_ge(S.o_first, w.to(S.o_first, 2))
                units = nsa_units()

                def finish(i, u, o, fac):
                    lo = (1 + u.br) * 16 + 4 * u.g
                    v.tensor_tensor(fac, fac, NB.gts[:, u.t, lo:lo + 4], ALU.mult).then_inc(S.dve_step, 1)
                    v.wait_ge(S.dve_step, w.to(S.dve_step))
                    tmp = NB.tmp.rearrange("p (r d) -> p r d", r=4)
                    v.tensor_tensor(tmp, o, fac.unsqueeze(2).to_broadcast([P, 4, DH]), ALU.mult).then_inc(S.o_taken, 1)
                    v.wait_ge(S.o_taken, w.to(S.o_taken))
                    dst = hp[:, u.t, u.g * 256:(u.g + 1) * 256]
                    add = v.tensor_tensor(dst, dst, NB.tmp, ALU.add)
                    if i >= len(units) - 2:
                        add.then_inc(S.h_ready, 1)
                    else:
                        add.then_inc(S.dve_step, 1)
                        v.wait_ge(S.dve_step, w.to(S.dve_step))

                attend(units, NB, None, finish)
                take_hT(None)
                w.past(S.acc_done)
                post(psum_rows(4), 1.0)

            v.memset(epsb[:, :], EPS).then_inc(S.set_up, 1)
            v.memset(zeros, 0.0).then_inc(S.set_up, 1)
            v.wait_ge(S.x_loaded, w.to(S.x_loaded, 16))
            v.wait_ge(S.const_loaded, w.to(S.const_loaded, 16))
            for name in stages:
                if name == "moe0":
                    v.wait_ge(S.param_loaded, PARAMS)
                if name[:3] == "mix":
                    mixer(int(name[3]))
                elif name[:3] == "moe":
                    moe(int(name[3]))
                elif name == "final":
                    gain = gain_rows()
                    for t in range(TT):
                        v.wait_ge(S.root_ready, w.to(S.root_ready))
                        reciprocal(rstd[:, t:t + 1], root[:, t:t + 1])
                        v.scalar_tensor_tensor(x[:, t, :], x[:, t, :], rstd[:, t:t + 1], gain,
                                               ALU.mult, ALU.mult).then_inc(S.x_ready, 1)
                        v.wait_ge(S.x_ready, w.to(S.x_ready))
                elif name[:3] == "ffn":
                    ffn(name)
                elif name == "pool":
                    pool_mix()
                elif name == "nsa":
                    nsa()


NAMES = ["x", "norm_mix", "w_in", "attn_sink", "conv_w", "norm_attn_out", "norm_conv_out", "w_out", "norm_ffn",
         "w_router_group", "b_router_group", "w_router_expert", "b_router_expert", "w_expert_gate", "w_expert_up",
         "w_expert_down", "norm_final", "norm_gains_2", "ffn_w_gate_2", "ffn_w_up_2", "ffn_w_down_2", "pool_w_2",
         "pool_b_2", "pool_scale_2", "nsa_w_in_2", "nsa_cmp_pos_k_2", "nsa_cmp_pos_v_2", "nsa_cmp_wk1_2",
         "nsa_cmp_wk2_2", "nsa_cmp_wv1_2", "nsa_cmp_wv2_2", "nsa_w_o_2"]


def kernel(**inputs):
    import concourse.bacc as bacc
    from concourse.bass_utils import run_bass_kernel_spmd

    nc = bacc.Bacc("TRN2", target_bir_lowering=False, num_devices=1)
    table, means = constants()
    arrays = {name: np.ascontiguousarray(inputs[name]) for name in NAMES}
    arrays["consts"], arrays["means"] = table, means
    aps = {}
    feed = {}
    for name, v in arrays.items():
        feed[f"in_{name}"] = v
        aps[name] = nc.dram_tensor(f"in_{name}", v.shape, mybir.dt.from_np(v.dtype), kind="ExternalInput").ap()
    out = nc.dram_tensor("out_x", (1, SEQ, D), F32, kind="ExternalOutput").ap()
    build(nc, aps, out, STAGES)
    r = run_bass_kernel_spmd(nc, [feed], core_ids=[0])
    return r.results[0]["out_x"]
```
